# Optimizing a Trainium2 kernel written in Bass

```python
import jax, jax.numpy as jnp
from jax import lax
import numpy as np

D_MODEL = 1024
BATCH = 1
SEQ = 1024
DEPTH = 1

FOX_HEAD_DIM = 64
FOX_WIDTH = D_MODEL // 2
FOX_HEADS = FOX_WIDTH // FOX_HEAD_DIM
Q_BLOCK = 128
MLSTM_HEADS = 4
MLSTM_WIDTH = D_MODEL // 2
MLSTM_HEAD_DIM = MLSTM_WIDTH // MLSTM_HEADS
CONV_WIDTH = 4
CHUNK = 128
D_FF = -(-8 * D_MODEL // (3 * 256)) * 256
EPS = 1e-6

IN_SPLIT_SIZES = (
    FOX_WIDTH, FOX_WIDTH, FOX_WIDTH, FOX_HEADS,
    MLSTM_WIDTH, MLSTM_WIDTH, MLSTM_WIDTH, MLSTM_HEADS, MLSTM_HEADS,
    MLSTM_WIDTH,
    D_MODEL, D_MODEL,
)
IN_WIDTH = sum(IN_SPLIT_SIZES)

kernel_name = 'fox_mlstm_gated_hybrid_block'

def rms_norm(x, g):
    xf = x.astype(jnp.float32)
    y = xf * lax.rsqrt(jnp.mean(xf * xf, axis=-1, keepdims=True) + EPS)
    return (y * g.astype(jnp.float32)).astype(x.dtype)

def head_layer_norm(x, g):
    B, S, H, d = x.shape
    xf = x.astype(jnp.float32)
    mu = jnp.mean(xf, axis=-1, keepdims=True)
    xc = xf - mu
    y = xc * lax.rsqrt(jnp.mean(xc * xc, axis=-1, keepdims=True) + EPS)
    return y.reshape(B, S, H * d) * g.astype(jnp.float32)

def causal_conv_silu(u, w, b):
    S = u.shape[1]
    up = jnp.pad(u, ((0, 0), (CONV_WIDTH - 1, 0), (0, 0)))
    y = b + sum(w[j] * up[:, j:j + S] for j in range(CONV_WIDTH))
    return jax.nn.silu(y)

def fox_attention(q, k, v, logf):
    B, S, H, d = q.shape
    nb = S // Q_BLOCK
    scale = d ** -0.5
    c = jnp.cumsum(logf, axis=1).transpose(0, 2, 1)
    q_blocks = q.reshape(B, nb, Q_BLOCK, H, d).transpose(1, 0, 2, 3, 4)
    c_blocks = c.reshape(B, H, nb, Q_BLOCK).transpose(2, 0, 1, 3)
    k_pos = jnp.arange(S)

    def block(args):
        qi, ci, bi = args
        s = jnp.einsum('bqhd,bkhd->bhqk', qi, k).astype(jnp.float32) * scale
        s = s + ci[..., :, None] - c[:, :, None, :]
        q_pos = bi * Q_BLOCK + jnp.arange(Q_BLOCK)
        s = jnp.where(k_pos[None, :] <= q_pos[:, None], s, -jnp.inf)
        p = jax.nn.softmax(s, axis=-1).astype(v.dtype)
        return jnp.einsum('bhqk,bkhd->bqhd', p, v)

    out = lax.map(block, (q_blocks, c_blocks, jnp.arange(nb)))
    return out.transpose(1, 0, 2, 3, 4).reshape(B, S, H, d)

def mlstm_chunkwise(q, k, v, logi, logf):
    B, S, H, d = q.shape
    nc = S // CHUNK
    f32 = jnp.float32

    def to_chunks(t):
        return t.astype(f32).reshape(B, nc, CHUNK, H, -1).transpose(1, 0, 3, 2, 4)

    qc = to_chunks(q)
    kc = to_chunks(k) * (d ** -0.5)
    vc = to_chunks(v)
    ic = to_chunks(logi[..., None])[..., 0]
    fc = to_chunks(logf[..., None])[..., 0]
    causal = jnp.tril(jnp.ones((CHUNK, CHUNK), dtype=bool))

    def step(carry, inp):
        C, n, m = carry
        qi, ki, vi, li, lf = inp
        b = jnp.cumsum(lf, axis=-1)
        a = b + m[..., None]
        D = jnp.where(causal, b[..., :, None] - b[..., None, :] + li[..., None, :], -jnp.inf)
        m_t = jnp.maximum(a, jnp.max(D, axis=-1))
        w_inter = jnp.exp(a - m_t)
        w_intra = jnp.exp(D - m_t[..., None])
        s = jnp.einsum('bhtd,bhsd->bhts', qi, ki) * w_intra
        num = w_inter[..., None] * jnp.einsum('bhvk,bhtk->bhtv', C, qi) + jnp.einsum('bhts,bhsv->bhtv', s, vi)
        den = w_inter * jnp.einsum('bhk,bhtk->bht', n, qi) + jnp.sum(s, axis=-1)
        h = num / jnp.maximum(jnp.abs(den), jnp.exp(-m_t))[..., None]
        m_new = m_t[..., -1]
        w_state = jnp.exp(b[..., -1:] - b + li - m_new[..., None])
        decay = jnp.exp(b[..., -1] + m - m_new)
        C_new = decay[..., None, None] * C + jnp.einsum('bhs,bhsv,bhsk->bhvk', w_state, vi, ki)
        n_new = decay[..., None] * n + jnp.einsum('bhs,bhsk->bhk', w_state, ki)
        return (C_new, n_new, m_new), h

    init = (jnp.zeros((B, H, d, d), f32), jnp.zeros((B, H, d), f32), jnp.zeros((B, H), f32))
    _, h = lax.scan(step, init, (qc, kc, vc, ic, fc))
    return h.transpose(1, 0, 3, 2, 4).reshape(B, S, H, d)

def hybrid_mixer(x, g_mix, w_in, b_fox_f, g_q_fox, g_k_fox, conv_w, conv_b,
                 b_mlstm_i, b_mlstm_f, g_mlstm_h, w_fox_out, w_mlstm_out, w_o):
    B, S, _ = x.shape
    h = rms_norm(x, g_mix)
    proj = h @ w_in
    split_points = [int(p) for p in np.cumsum(IN_SPLIT_SIZES)[:-1]]
    (qa, ka, va, fa, qb, kb, vb, ib, fb, ob, ga, gb) = jnp.split(proj, split_points, axis=-1)

    qa = rms_norm(qa.reshape(B, S, FOX_HEADS, FOX_HEAD_DIM), g_q_fox)
    ka = rms_norm(ka.reshape(B, S, FOX_HEADS, FOX_HEAD_DIM), g_k_fox)
    va = va.reshape(B, S, FOX_HEADS, FOX_HEAD_DIM)
    logf_a = jax.nn.log_sigmoid((fa + b_fox_f).astype(jnp.float32))
    ya = fox_attention(qa, ka, va, logf_a).reshape(B, S, FOX_WIDTH)

    qkb = causal_conv_silu(jnp.concatenate([qb, kb], axis=-1), conv_w, conv_b)
    qb, kb = jnp.split(qkb, 2, axis=-1)
    qb = qb.reshape(B, S, MLSTM_HEADS, MLSTM_HEAD_DIM)
    kb = kb.reshape(B, S, MLSTM_HEADS, MLSTM_HEAD_DIM)
    vb = vb.reshape(B, S, MLSTM_HEADS, MLSTM_HEAD_DIM)
    logi_b = (ib + b_mlstm_i).astype(jnp.float32)
    logf_b = jax.nn.log_sigmoid((fb + b_mlstm_f).astype(jnp.float32))
    hb = mlstm_chunkwise(qb, kb, vb, logi_b, logf_b)
    yb = (head_layer_norm(hb, g_mlstm_h) * jax.nn.sigmoid(ob.astype(jnp.float32))).astype(x.dtype)

    merged = jax.nn.sigmoid(ga) * (ya @ w_fox_out) + jax.nn.sigmoid(gb) * (yb @ w_mlstm_out)
    return merged @ w_o

def swiglu_ffn(x, g_ffn, w_gate, w_up, w_down):
    h = rms_norm(x, g_ffn)
    return (jax.nn.silu(h @ w_gate) * (h @ w_up)) @ w_down

def setup_inputs(seed: int = 0) -> dict:
    key = jax.random.key(seed)
    ks = jax.random.split(key, 20)

    def nrm(k, shape, scale):
        return jax.random.normal(k, shape, jnp.float32) * scale

    return {
        'x': nrm(ks[0], (BATCH, SEQ, D_MODEL), 1.0),
        'g_mix': 1.0 + nrm(ks[1], (DEPTH, D_MODEL), 0.02),
        'w_in': nrm(ks[2], (DEPTH, D_MODEL, IN_WIDTH), D_MODEL ** -0.5),
        'b_fox_f': jnp.linspace(1.0, 4.0, FOX_HEADS)[None, :] + nrm(ks[3], (DEPTH, FOX_HEADS), 0.01),
        'g_q_fox': 1.0 + nrm(ks[4], (DEPTH, FOX_HEAD_DIM), 0.02),
        'g_k_fox': 1.0 + nrm(ks[5], (DEPTH, FOX_HEAD_DIM), 0.02),
        'conv_w': nrm(ks[6], (DEPTH, CONV_WIDTH, 2 * MLSTM_WIDTH), CONV_WIDTH ** -0.5),
        'conv_b': nrm(ks[7], (DEPTH, 2 * MLSTM_WIDTH), 0.01),
        'b_mlstm_i': nrm(ks[8], (DEPTH, MLSTM_HEADS), 0.1),
        'b_mlstm_f': jnp.linspace(3.0, 6.0, MLSTM_HEADS)[None, :] + nrm(ks[9], (DEPTH, MLSTM_HEADS), 0.01),
        'g_mlstm_h': 1.0 + nrm(ks[10], (DEPTH, MLSTM_WIDTH), 0.02),
        'w_fox_out': nrm(ks[11], (DEPTH, FOX_WIDTH, D_MODEL), FOX_WIDTH ** -0.5),
        'w_mlstm_out': nrm(ks[12], (DEPTH, MLSTM_WIDTH, D_MODEL), MLSTM_WIDTH ** -0.5),
        'w_o': nrm(ks[13], (DEPTH, D_MODEL, D_MODEL), D_MODEL ** -0.5),
        'g_ffn': 1.0 + nrm(ks[14], (DEPTH, D_MODEL), 0.02),
        'w_gate': nrm(ks[15], (DEPTH, D_MODEL, D_FF), D_MODEL ** -0.5),
        'w_up': nrm(ks[16], (DEPTH, D_MODEL, D_FF), D_MODEL ** -0.5),
        'w_down': nrm(ks[17], (DEPTH, D_FF, D_MODEL), D_FF ** -0.5),
    }

def reference(x, g_mix, w_in, b_fox_f, g_q_fox, g_k_fox, conv_w, conv_b, b_mlstm_i, b_mlstm_f,
              g_mlstm_h, w_fox_out, w_mlstm_out, w_o, g_ffn, w_gate, w_up, w_down):
    for l in range(DEPTH):
        x = x + hybrid_mixer(x, g_mix[l], w_in[l], b_fox_f[l], g_q_fox[l], g_k_fox[l], conv_w[l], conv_b[l],
                             b_mlstm_i[l], b_mlstm_f[l], g_mlstm_h[l], w_fox_out[l], w_mlstm_out[l], w_o[l])
        x = x + swiglu_ffn(x, g_ffn[l], w_gate[l], w_up[l], w_down[l])
    return x


_drawn_inputs = setup_inputs


def setup_inputs(seed=0):
    import zlib

    import numpy as np

    out = dict(_drawn_inputs(seed))
    spreads = {}
    factors = {'g_mix': 3.843,
     'g_q_fox': 8.0,
     'g_k_fox': 8.0,
     'conv_b': 64.0,
     'b_mlstm_i': 64.0,
     'g_mlstm_h': 8.0,
     'g_ffn': 4.064}
    for name, (base, spread) in spreads.items():
        noise = np.random.default_rng([zlib.crc32(name.encode()), seed]).standard_normal(out[name].shape)
        drawn = base * np.exp(spread * noise) if base else spread * noise
        out[name] = __import__('jax').numpy.asarray(drawn.astype(out[name].dtype))
    for name, factor in factors.items():
        out[name] = (out[name] * factor).astype(out[name].dtype)
    return out
```

```python
from contextlib import ExitStack

import numpy as np

import concourse.bass as bass
from concourse import mybir

F32 = mybir.dt.float32
F32R = mybir.dt.float32r
BF16 = mybir.dt.bfloat16
ACT = mybir.ActivationFunctionType
ALU = mybir.AluOpType
AX_X = mybir.AxisListType.X

P = 128
SEQ = 1024
D_MODEL = 1024
KT = D_MODEL // P
TT = SEQ // P
HALF = SEQ // 2
FOX_HEADS, FOX_DIM = 8, 64
FOX_WIDTH = FOX_HEADS * FOX_DIM
PAIRS = FOX_HEADS // 2
ML_HEADS, ML_DIM = 4, 128
ML_WIDTH = ML_HEADS * ML_DIM
CHUNK = 128
CHUNKS = SEQ // CHUNK
TAPS = 4
D_FF = 2816
FT = D_FF // P
EPS = 1e-6
MASKED = -1e30
LOWEST = -3e38

COL = {}
_at = 0
for _name, _width in (("qa", FOX_WIDTH), ("ka", FOX_WIDTH), ("va", FOX_WIDTH), ("fa", FOX_HEADS),
                      ("qb", ML_WIDTH), ("kb", ML_WIDTH), ("vb", ML_WIDTH), ("ib", ML_HEADS), ("fb", ML_HEADS),
                      ("ob", ML_WIDTH), ("ga", D_MODEL), ("gb", D_MODEL)):
    COL[_name] = _at
    _at += _width
IN_WIDTH = _at

ROW_FA, ROW_IB, ROW_FB = 0, 32, 64
GATE_ROWS = ROW_FB + ML_HEADS

RING = 3
U_GATES = 0
U_VALUES = 1
U_FOX = U_VALUES + 8
FOX_UNITS = 6
U_ML = U_FOX + PAIRS * FOX_UNITS
ML_UNITS = 3
ML_STEPS = CHUNKS // 2
U_MERGE = U_ML + ML_STEPS * ML_UNITS
U_FFN = U_MERGE + 2 * KT
U_END = U_FFN + 3 * FT
assert U_FOX % RING == 0 and FOX_UNITS % RING == 0 and ML_UNITS % RING == 0 and U_MERGE % RING == 0
G_IN_FOX = PAIRS
N_TAPS_COLS = TAPS + 1


N_CONST = 15


def raw_count(n, rounds):
    return n // RING + (1 if n % RING else 0) + rounds


def ml_stores(q, j):
    before = 4 + 2 * PAIRS
    return before + 2 * q + (j == 2) if j % 2 == 0 else before + q


def fox_schedule():
    def half(j, h):
        return ([("unit", j)] if h == 0 else []) + [("dense", j, h, a, a + 1) for a in range(24)] + [("half", j, h)]
    def then(j, h, x, xh):
        steps = half(j, h)
        return steps[:7] + [("norm", x, xh)] + steps[7:]
    head = half(0, 0) + then(0, 1, 0, 0) + then(1, 0, 0, 1) + then(1, 1, 1, 0) + then(2, 0, 1, 1)
    rest = half(2, 1) + [e for j in (3, 4, 5) for h in (0, 1) for e in half(j, h)]
    attend = []
    steps = 2 * TT
    for k in range(steps + 1):
        if k < steps:
            attend.append([("scores", k)])
        if k > 0:
            attend.append([("turn", k - 1, 0)])
            if (k - 1) // 2 >= 4:
                attend.append([("turn", k - 1, 1)])
            attend.append([("values", k - 1)])
    n_mm = sum(e[0] == "dense" for e in rest)
    out, seen, used, silu = [], 0, 0, []
    for e in rest:
        if e[0] == "dense":
            while used < len(attend) and used * n_mm <= seen * len(attend):
                out += attend[used]
                used += 1
                if silu and seen >= silu[0][1]:
                    out.append(silu.pop(0)[0])
            seen += 1
        out.append(e)
        if e[0] == "half" and e[1] in (2, 3) and e[2] == 1:
            silu.append((("silu", e[1]), seen + 10))
    out += [x for a in attend[used:] for x in a] + [s for s, _ in silu]
    return head + out


def ml_schedule():
    steps = [("kq", 0), ("num", 0), ("state", 0), ("kq", 1), ("out", 0), ("num", 1), ("state", 1), ("out", 1)]
    at = [0, 18, 36, 62, 66, 86, 106, 143]
    out, seen = [], 0
    for j in range(ML_UNITS):
        for h in (0, 1):
            if h == 0:
                out.append(("unit", j))
            for a in range(24):
                while at and at[0] <= seen:
                    out.append(steps.pop(0))
                    at.pop(0)
                out.append(("dense", j, h, a, a + 1))
                seen += 1
            out.append(("half", j, h))
    return out + steps


def turn_fill(s, part):
    i = s // 2
    return (s if i < 4 else 8 + 2 * (s - 8)) + part


FILLS = turn_fill(2 * TT - 1, 1) + 1


ML_STEP_COUNT = {"kq": 5, "num": 7, "state": 4, "out": 7}
ML_SETUP = 2
ML_OFFSET = {}
ML_V_STEPS = 0
for _step in ml_schedule():
    if _step[0] in ML_STEP_COUNT:
        ML_OFFSET[_step] = ML_V_STEPS
        ML_V_STEPS += ML_STEP_COUNT[_step[0]]

X_START = 16
DOWN_START = 16


def ml_at(q, kind, c, steps):
    return ML_SETUP + ML_V_STEPS * q + ML_OFFSET[kind, c] + steps


def hybrid_block(nc, x, g_mix, w_in, b_fox_f, g_q_fox, g_k_fox, conv_w, conv_b, b_mlstm_i, b_mlstm_f,
                 g_mlstm_h, w_fox_out, w_mlstm_out, w_o, g_ffn, w_gate, w_up, w_down, out):
    fox_steps, ml_steps = fox_schedule(), ml_schedule()
    w_in, conv_w, w_fox_out, w_mlstm_out, w_o = w_in[0], conv_w[0], w_fox_out[0], w_mlstm_out[0], w_o[0]
    w_gate, w_up, w_down = w_gate[0], w_up[0], w_down[0]

    d_qk = nc.dram_tensor("d_qk", (2 * ML_HEADS, P, SEQ), F32, kind="Internal").ap()
    d_v = nc.dram_tensor("d_v", (TT, P, ML_WIDTH), F32, kind="Internal").ap()
    d_ob = nc.dram_tensor("d_ob", (ML_HEADS, P, SEQ), F32, kind="Internal").ap()
    d_g = nc.dram_tensor("d_g", (2 * KT, P, SEQ), F32, kind="Internal").ap()
    d_c = nc.dram_tensor("d_c", (2, FOX_HEADS, SEQ), F32, kind="Internal").ap()
    d_m = nc.dram_tensor("d_m", (2, ML_HEADS, SEQ), F32, kind="Internal").ap()

    x_tiles = x[0].rearrange("(t p) d -> t p d", p=P)
    out_tiles = out[0].rearrange("(t p) d -> t p d", p=P)

    def w_cols(w, col, n=P):
        return w.rearrange("(k p) n -> p k n", p=P)[:, :, bass.ds(col, n)]

    with ExitStack() as ctx:
        def sb(name, shape, dt=F32, where=ctx):
            return where.enter_context(nc.sbuf_tensor(name, shape, dt))

        def sem(name):
            return ctx.enter_context(nc.semaphore(name))

        actT_hi = sb("actT_hi", [P, KT, SEQ], F32R)
        actT_lo = sb("actT_lo", [P, KT, SEQ], F32R)
        W_hi = sb("W_hi", [P, RING, 1024], F32R)
        W_lo = sb("W_lo", [P, RING, 1024], F32R)
        W_raw = sb("W_raw", [P, RING, 1024])
        ident = sb("ident", [P, P])
        ident_bf = sb("ident_bf", [P, P], BF16)
        mask_bf = sb("mask_bf", [P, P], BF16)
        mask_ml = sb("mask_ml", [P, P])
        head_mean = sb("head_mean", [P, P])
        g_cols = sb("g_cols", [P, 2, KT])
        g_qk = sb("g_qk", [P, 2])
        g_ml = sb("g_ml", [P, ML_HEADS])
        gate_bias = sb("gate_bias", [GATE_ROWS, 1])
        taps = sb("taps", [P, 2 * ML_HEADS, N_TAPS_COLS])
        eps_col = sb("eps_col", [P, 1])
        stat = sb("stat", [P, 3, TT])
        uT = sb("uT", [P, CHUNKS, ML_HEADS])
        emT = sb("emT", [P, CHUNKS, ML_HEADS])
        nmax = sb("nmax", [P, 2])
        psumrow = sb("psumrow", [P, 2])
        rinv = sb("rinv", [P, 2])
        hstat = sb("hstat", [P, 6, ML_HEADS])

        with ExitStack() as early:
            X0 = sb("X0", [P, TT, D_MODEL], where=early)
            XN0 = sb("XN0", [P, TT, D_MODEL], where=early)
        with ExitStack() as gates:
            V = sb("V", [P, TT, FOX_WIDTH], where=gates)
            z = sb("z", [GATE_ROWS, SEQ], where=gates)
            soft = sb("soft", [GATE_ROWS, SEQ], where=gates)
            logs = sb("logs", [GATE_ROWS, SEQ], where=gates)
            keep = sb("keep", [GATE_ROWS, SEQ], where=gates)
            csum = sb("csum", [GATE_ROWS, SEQ], where=gates)
            negs = sb("negs", [GATE_ROWS, SEQ], where=gates)
            u_m = sb("u_m", [GATE_ROWS, 2, SEQ], where=gates)
            shift = sb("shift", [GATE_ROWS, SEQ], where=gates)
            wi_em = sb("wi_em", [GATE_ROWS, 2, SEQ], where=gates)
            m_prev = sb("m_prev", [GATE_ROWS, CHUNKS], where=gates)
        with ExitStack() as mid:
            V_ = sb("V_", [P, TT, FOX_WIDTH], where=mid)
            QA = sb("QA", [FOX_DIM + 2, 2, SEQ], where=mid)
            KA = sb("KA", [FOX_DIM + 2, 2, SEQ], where=mid)
            Y = sb("Y", [P, TT, FOX_WIDTH], where=mid)
            HN = sb("HN", [P, CHUNKS, ML_WIDTH], where=mid)
        with ExitStack() as mlp:
            qc = sb("qc", [P, 2, ML_HEADS, CHUNK], where=mlp)
            kc = sb("kc", [P, 2, ML_HEADS, CHUNK], where=mlp)
            vc = sb("vc", [P, 2, ML_HEADS, ML_DIM + 1], where=mlp)
            m_rows = sb("m_rows", [P, 2, 2, ML_HEADS, CHUNK], where=mlp)
            state = sb("state", [P, ML_HEADS, ML_DIM + 1], where=mlp)
        with ExitStack() as late:
            X = sb("X", [P, TT, D_MODEL], where=late)
            XN = sb("XN", [P, TT, D_MODEL], where=late)

        big = ctx.enter_context(nc.sbuf_tensor("big_region", [P, 2 * TT * D_MODEL], F32))
        with ExitStack() as fox:
            stage = sb("stage", [P, 2, SEQ], where=fox)
            sq = sb("sq", [P, HALF], where=fox)
            root = sb("root", [P, HALF], where=fox)
            qk_raw = sb("qk_raw", [P, 2, SEQ], where=fox)
            prob = sb("prob", [P, 2, SEQ], where=fox)
            probT = sb("probT", [P, TT, P], where=fox)
            conv_in = sb("conv_in", [P, TAPS - 1 + SEQ], where=fox)
            conv_acc = sb("conv_acc", [P, SEQ], where=fox)
        with ExitStack() as mlt:
            stage_ = sb("stage_", [P, 2, SEQ], where=mlt)
            decay = sb("decay", [P, ML_HEADS, CHUNK], where=mlt)
            qs = sb("qs", [P, ML_HEADS, CHUNK], where=mlt)
            sw = sb("sw", [P, ML_HEADS, CHUNK], where=mlt)
            kw = sb("kw", [P, ML_HEADS, ML_DIM], where=mlt)
            hb = sb("hb", [P, ML_HEADS, ML_DIM], where=mlt)
            hsq = sb("hsq", [P, ML_HEADS, ML_DIM], where=mlt)
        with ExitStack() as turn:
            sob = sb("sob", [P, ML_HEADS, SEQ], where=turn)
            yb = sb("yb", [P, 2, HALF], where=turn)
        with ExitStack() as fin:
            A_hi = sb("A_hi", [P, 3, SEQ], F32R, where=fin)
            A_lo = sb("A_lo", [P, 3, SEQ], F32R, where=fin)
            sg = sb("sg", [P, 2, SEQ], where=fin)

        PS = ctx.enter_context(nc.psum_tensor("PS", [P, 8, HALF], F32))

        def score_row(s):
            bank = 2 + 2 * (s % 2)
            return PS[:, bank:bank + 2, :].rearrange("p b n -> p (b n)")[:, 0:(s // 2 + 1) * P]

        x_in = [sem(f"x_in{t}") for t in range(TT)]
        const_in = sem("const_in")
        const_set = sem("const_set")
        cols_set = sem("cols_set")
        gate_zero = sem("gate_zero")
        gate_raw = sem("gate_raw")
        w_raw = [sem(f"w_raw{s}") for s in range(RING)]
        w_first = sem("w_first")
        w_hi = sem("w_hi")
        w_lo = sem("w_lo")
        w_used = sem("w_used")
        sumsq = sem("sumsq")
        rooted = sem("rooted")
        scaled = sem("scaled")
        turned = sem("turned")
        act_hi = sem("act_hi")
        act_lo = sem("act_lo")
        gate_mm = sem("gate_mm")
        gate_v = sem("gate_v")
        gate_a = sem("gate_a")
        gate_turn = sem("gate_turn")
        gate_out = sem("gate_out")
        rows_out = sem("rows_out")
        val_mm = sem("val_mm")
        val_out = sem("val_out")
        tile_mm = sem("tile_mm")
        tile_out = sem("tile_out")
        sq_set = sem("sq_set")
        mean_mm = sem("mean_mm")
        root_set = sem("root_set")
        inv_set = sem("inv_set")
        qk_set = sem("qk_set")
        ones_set = sem("ones_set")
        c_in = [sem("cq_in"), sem("ck_in")]
        score_mm = sem("score_mm")
        nmax_set = sem("nmax_set")
        prob_set = sem("prob_set")
        prob_turn = sem("prob_turn")
        probT_set = sem("probT_set")
        y_mm = sem("y_mm")
        rinv_set = sem("rinv_set")
        y_set = sem("y_set")
        conv_step = sem("conv_step")
        tanh_set = sem("tanh_set")
        conv_mul = sem("conv_mul")
        tile_set = sem("tile_set")
        stored = [sem("stored0"), sem("stored1")]
        chunk_in = [[sem(f"{n}_in{b}") for b in range(2)] for n in ("qc", "kc", "vc", "mc", "wc")]
        kq_mm = sem("kq_mm")
        num_mm = sem("num_mm")
        state_mm = sem("state_mm")
        ml_v = sem("ml_v")
        decay_set = sem("decay_set")
        ml_root = sem("ml_root")
        sob_in = sem("sob_in")
        yb_set = sem("yb_set")
        g_in = [sem("ga_in"), sem("gb_in")]
        sg_set = sem("sg_set")
        br_mm = sem("br_mm")
        mix_v = sem("mix_v")
        a_hi = sem("a_hi")
        a_lo = sem("a_lo")
        down_mm = sem("down_mm")
        x_add = sem("x_add")
        gu_mm = sem("gu_mm")
        tanh_g = sem("tanh_g")
        glu_a = sem("glu_a")
        glu_b = sem("glu_b")
        out_in = sem("out_in")
        transfer_due = sem("transfer_due")

        def w_tile(parts, slot):
            return parts[:, slot, :].rearrange("p (k n) -> p k n", k=KT)

        def hi_lo(product, hi_a, lo_a, hi_b, lo_b, first, last):
            product(hi_a, hi_b, first, False)
            product(hi_a, lo_b, False, False)
            return product(lo_a, hi_b, False, last)

        block = ctx.enter_context(nc.Block())

        @block.tensor
        def _(pe):
            def product(dst):
                return lambda a, b, start, stop: pe.matmul(dst, a, b, start=start, stop=stop)

            def dense(bank, slot, half, a, b):
                tokens = slice(half * HALF, (half + 1) * HALF)
                hi, lo = w_tile(W_hi, slot), w_tile(W_lo, slot)
                for n in range(a, b):
                    k, part = divmod(n, 3)
                    w = (hi, hi, lo)[part][:, k, :]
                    act = (actT_hi, actT_lo, actT_hi)[part][:, k, tokens]
                    last = pe.matmul(PS[:, bank, :], w, act, start=n == 0, stop=n == 23)
                return last

            def norm_turn(round_, ready):
                for h in range(2):
                    pe.wait_ge(scaled, round_ * (2 + TT) + (h + 1) * 5)
                    for k in range(KT):
                        if h or round_:
                            pe.wait_ge(act_lo, ready + h * KT + k - 7)
                        for j in range(4):
                            last = pe.transpose(PS[:, k, j * P:(j + 1) * P],
                                                XN[:, 4 * h + j, k * P:(k + 1) * P], ident[:])
                        last.then_inc(turned, 1)

            pe.wait_ge(const_set, 8)
            pe.wait_ge(cols_set, 5)
            norm_turn(0, 0)

            pe.wait_ge(act_lo, 2 * KT)
            pe.wait_ge(w_lo, 1)
            for h in range(2):
                last = dense(h, 0, h, 0, 24)
                last.then_inc(gate_mm, 1)

            for b in range(2):
                for u in range(4):
                    n = U_VALUES + 4 * b + u
                    slot = n % RING
                    pe.wait_ge(w_lo, n + 1)
                    for t in range(TT):
                        if u == 0 and b == 0 and t < 2:
                            pe.wait_ge(gate_v, 2)
                        if u == 0 and b == 1:
                            pe.wait_ge(val_out, t + 1)
                        for i in range(2):
                            k = 2 * u + i
                            tok = slice(t * P, (t + 1) * P)
                            cols = slice(i * 512, (i + 1) * 512)
                            last = hi_lo(product(PS[:, t, :]), actT_hi[:, k, tok], actT_lo[:, k, tok],
                                         W_hi[:, slot, cols], W_lo[:, slot, cols], k == 0, k == KT - 1)
                        if u == 3:
                            last.then_inc(val_mm, 1)
                    if u < 3:
                        last.then_inc(w_used, 1)

            pe.wait_ge(val_mm, 2 * TT)
            pe.sem_inc(tile_mm, 2)

            pe.wait_ge(gate_a, 6)
            pe.wait_ge(val_out, 2 * TT)
            rows = slice(ROW_FB, ROW_FB + ML_HEADS)
            for kind, src in enumerate((u_m[rows, 0, :], wi_em[rows, 1, :])):
                for c in range(CHUNKS):
                    at = (kind * CHUNKS + c) * ML_HEADS
                    last = pe.transpose(PS[:, 2, at:at + ML_HEADS], src[:, c * CHUNK:(c + 1) * CHUNK],
                                        ident[rows, rows])
            last.then_inc(gate_turn, 1)

            pe.wait_ge(gate_out, 2)
            with pe.Fori(0, PAIRS) as p:
                for step in fox_steps:
                    kind, *at = step
                    if kind == "unit":
                        j, = at
                        pe.wait_ge(w_lo, U_FOX + FOX_UNITS * p + j + 1)
                    elif kind == "dense":
                        j, h, a, b = at
                        if a == 0:
                            pe.wait_ge(tile_out, 2 * FOX_UNITS * p + 2 * j + h + 1)
                        last = dense(h, j % RING, h, a, b)
                        if b == 24:
                            last.then_inc(tile_mm, 1)
                    elif kind == "norm":
                        q_or_k, h = at
                        pe.wait_ge(sq_set, 4 * p + 2 * q_or_k + h + 1)
                        pe.matmul(PS[:, 2 + 2 * q_or_k + h, :], head_mean[:], sq[:], start=True,
                                  stop=True).then_inc(mean_mm, 1)
                    elif kind == "scores":
                        s, = at
                        i, hd = divmod(s, 2)
                        length = (i + 1) * P
                        if s == 0:
                            pe.wait_ge(qk_set, 8 * p + 8)
                            pe.wait_ge(c_in[0], 16 * (p + 1))
                            pe.wait_ge(c_in[1], 16 * (p + 1))
                        if s >= 2:
                            pe.wait_ge(prob_set, 2 * TT * p + s - 1)
                        query = QA[:, hd, i * P:(i + 1) * P]
                        bank = 2 + 2 * (s % 2)
                        for part in range(0, length, HALF):
                            n = min(HALF, length - part)
                            diagonal = part + n == length
                            last = pe.matmul(PS[:, bank + part // HALF, 0:n], query, KA[:, hd, part:part + n],
                                             start=True, stop=not diagonal)
                            if diagonal:
                                last = pe.matmul(PS[:, bank + part // HALF, n - P:n], ident_bf[:], mask_bf[:],
                                                 start=False, stop=True)
                        last.then_inc(score_mm, 1)
                    elif kind == "turn":
                        s, part = at
                        f = turn_fill(s, part)
                        if part == 0:
                            pe.wait_ge(prob_set, 2 * TT * p + s + 1)
                        if f:
                            pe.wait_ge(probT_set, FILLS * p + f)
                        for b in range(4 * part, min(4 * part + 4, s // 2 + 1)):
                            last = pe.transpose(PS[:, 6, (b % 4) * P:(b % 4 + 1) * P],
                                                prob[:, s % 2, b * P:(b + 1) * P], ident[:])
                        last.then_inc(prob_turn, 1)
                    elif kind == "values":
                        s, = at
                        i, hd = divmod(s, 2)
                        pe.wait_ge(probT_set, FILLS * p + turn_fill(s, int(i >= 4)) + 1)
                        if s:
                            pe.wait_ge(y_set, 2 * TT * p + s)
                        for b in range(i + 1):
                            head = bass.ds(p * P + hd * FOX_DIM, FOX_DIM)
                            last = pe.matmul(PS[:, 7, 0:FOX_DIM], probT[:, b, :], V[:, b, head],
                                             start=b == 0, stop=b == i)
                        last.then_inc(y_mm, 1)

            pe.wait_ge(ml_v, ML_SETUP)
            with pe.Fori(0, ML_STEPS) as q:
                for step in ml_steps:
                    kind, *at = step
                    if kind == "unit":
                        j, = at
                        pe.wait_ge(w_lo, U_ML + ML_UNITS * q + j + 1)
                    elif kind == "dense":
                        j, h, a, b = at
                        done = 2 * FOX_UNITS * PAIRS + 2 * ML_UNITS * q + 2 * j + h
                        if a == 0:
                            pe.wait_ge(tile_out, done + 1)
                        last = dense(h, j % RING, h, a, b)
                        if b == 24:
                            last.then_inc(tile_mm, 1)
                    elif kind == "kq":
                        c, = at
                        for which in (0, 1):
                            pe.wait_ge(chunk_in[which][c], 16 * (q + 1))
                        for h in range(ML_HEADS):
                            pe.transpose(PS[:, 6, h * P:(h + 1) * P], kc[:, c, h, :], ident[:])
                        for h in range(ML_HEADS):
                            last = pe.matmul(PS[:, 2, h * P:(h + 1) * P], kc[:, c, h, :], qc[:, c, h, :],
                                             start=True, stop=True)
                        last.then_inc(kq_mm, 1)
                    elif kind == "num":
                        c, = at
                        pe.wait_ge(chunk_in[2][c], 16 * (q + 1))
                        pe.wait_ge(ml_v, ml_at(q, "kq", c, 4))
                        for h in range(ML_HEADS):
                            dst = PS[:, 3 + h // 2, (h % 2) * 129:(h % 2 + 1) * 129]
                            pe.matmul(dst, sw[:, h, :], vc[:, c, h, :], start=True, stop=False)
                            last = pe.matmul(dst, qs[:, h, :], state[:, h, :], start=False, stop=True)
                        last.then_inc(num_mm, 1)
                    elif kind == "state":
                        c, = at
                        pe.wait_ge(ml_v, ml_at(q, "kq", c, 5))
                        for h in range(ML_HEADS):
                            dst = PS[:, (5, 7)[h // 2], (h % 2) * 129:(h % 2 + 1) * 129]
                            last = pe.matmul(dst, kw[:, h, :], vc[:, c, h, :], start=True, stop=True)
                        last.then_inc(state_mm, 1)

            pe.wait_ge(ml_v, ML_SETUP + ML_STEPS * ML_V_STEPS)
            pe.wait_ge(tile_out, 2 + 2 * FOX_UNITS * PAIRS + 2 * ML_UNITS * ML_STEPS)
            for k in range(KT):
                src = Y if k < PAIRS else HN
                for h in range(2):
                    n = 2 * k + h
                    if n >= 8:
                        pe.wait_ge(act_lo, 2 * KT + n - 7)
                    for j in range(4):
                        t = 4 * h + j
                        last = pe.transpose(PS[:, n % 8, j * P:(j + 1) * P],
                                            src[:, t, (k % 4) * P:(k % 4 + 1) * P], ident[:])
                    last.then_inc(turned, 1)

            def down(n, slot, a_slot, tile):
                pe.wait_ge(w_lo, n + 1)
                pe.wait_ge(a_lo, 2 * (tile + 1))
                for t in range(TT):
                    for c in range(2):
                        g = 2 * t + c
                        pe.wait_ge(x_add, X_START + 16 * tile + g - 3)
                        tok, cols = slice(t * P, (t + 1) * P), slice(c * 512, (c + 1) * 512)
                        last = hi_lo(product(PS[:, 4 + g % 4, :]), A_hi[:, a_slot, tok], A_lo[:, a_slot, tok],
                                     W_hi[:, slot, cols], W_lo[:, slot, cols], True, True)
                        last.then_inc(down_mm, 1)

            def branches(m, n, slot):
                pe.wait_ge(w_lo, n + 1)
                hi, lo = w_tile(W_hi, slot), w_tile(W_lo, slot)
                for b in range(2):
                    for h in range(2):
                        tokens = slice(h * HALF, (h + 1) * HALF)
                        if not (isinstance(m, int) and m == 0):
                            pe.wait_ge(mix_v, 6 * m)
                        for i in range(4):
                            k = 4 * b + i
                            last = hi_lo(product(PS[:, 2 * b + h, :]), hi[:, k, :], lo[:, k, :],
                                         actT_hi[:, k, tokens], actT_lo[:, k, tokens], i == 0, i == 3)
                        last.then_inc(br_mm, 1)

            pe.wait_ge(act_lo, 4 * KT)
            branches(0, U_MERGE, 0)
            pe.wait_ge(br_mm, 4)
            pe.sem_inc(down_mm, DOWN_START)
            with pe.Fori(0, 2) as r:
                for i in range(3):
                    m = 3 * r + i + 1
                    branches(m, U_MERGE + 6 * r + 2 * i + 1, (2 * i + 1) % RING)
                    down(U_MERGE + 6 * r + 2 * i + 2, (2 * i + 2) % RING, i, 3 * r + i)
            branches(KT - 1, U_MERGE + 13, 13 % RING)
            down(U_MERGE + 14, 14 % RING, 0, KT - 2)
            down(U_MERGE + 15, 15 % RING, 1, KT - 1)

            pe.wait_ge(x_add, X_START + 16 * KT)
            norm_turn(1, 4 * KT)

            def gate_up(m, n, slot):
                for b in range(2):
                    pe.wait_ge(w_lo, n + b + 1)
                    for h in range(2):
                        if not (isinstance(m, int) and m == 0):
                            pe.wait_ge((glu_a, glu_b)[b], 2 * m + h - 1)
                        last = dense(2 * b + h, (slot + b) % RING, h, 0, 24)
                        last.then_inc(gu_mm, 1)

            pe.wait_ge(act_lo, 6 * KT)
            gate_up(0, U_FFN, U_FFN % RING)
            with pe.Fori(0, FT // 2 - 1) as r:
                for i in range(2):
                    at = 3 * i + 2
                    gate_up(2 * r + i + 1, U_FFN + 6 * r + at, (U_FFN + at) % RING)
                    down(U_FFN + 6 * r + at + 2, (U_FFN + at + 2) % RING, i, KT + 2 * r + i)
            at = U_FFN + 3 * (FT - 2) + 2
            gate_up(FT - 1, at, at % RING)
            down(at + 2, (at + 2) % RING, 0, KT + FT - 2)
            down(at + 3, (at + 3) % RING, 1, KT + FT - 1)

        @block.scalar
        def _(act):
            def split(n, rounds=0):
                slot = n % RING
                act.wait_ge(w_raw[slot], 16 * raw_count(n, rounds))
                act.activation(W_hi[:, slot, :], W_raw[:, slot, :], ACT.Copy).then_inc(w_hi, 1)

            def norm_rows(round_, arrived, src, dst):
                for t in range(TT):
                    arrived(t)
                    act.activation(dst[:, t, :], src[:, t, :], ACT.Square,
                                   accum_out=stat[:, 0, t:t + 1]).then_inc(sumsq, 1)
                    if t % 4 == 3:
                        act.wait_ge(sumsq, TT * round_ + t + 1)
                        act.activation(stat[:, 1, t - 3:t + 1], stat[:, 0, t - 3:t + 1], ACT.Sqrt,
                                       bias=eps_col[:], scale=1.0 / D_MODEL).then_inc(rooted, 1)

            def norm_hi(round_, base):
                for h in range(2):
                    for k in range(KT):
                        act.wait_ge(turned, base + h * KT + k + 1)
                        act.activation(actT_hi[:, k, h * HALF:(h + 1) * HALF], PS[:, k, :], ACT.Copy,
                                       scale=g_cols[:, round_, k:k + 1]).then_inc(act_hi, 1)

            act.wait_ge(cols_set, 1)
            act.wait_ge(const_in, 16 * N_CONST)
            norm_rows(0, lambda t: act.wait_ge(x_in[t], 16), X0, XN0)
            act.wait_ge(gate_raw, 48)
            act.activation(W_hi[:, 0, :], W_raw[:, 0, :], ACT.Copy).then_inc(w_hi, 1)
            split(1)
            split(2)
            norm_hi(0, 0)

            rows = slice(ROW_FB, ROW_FB + ML_HEADS)
            act.wait_ge(gate_v, 2)
            act.activation(u_m[rows, 0, :], z[ROW_IB:ROW_IB + ML_HEADS, :], ACT.Copy).then_inc(gate_a, 1)
            act.activation(soft[:], z[:], ACT.Abs).then_inc(gate_a, 1)
            act.wait_ge(gate_a, 2)
            act.activation(soft[:], soft[:], ACT.Exp, scale=-1.0).then_inc(gate_a, 1)
            act.wait_ge(gate_a, 3)
            act.activation(soft[:], soft[:], ACT.Ln, bias=1.0).then_inc(gate_a, 1)
            act.wait_ge(gate_mm, 2)
            split(3)
            act.wait_ge(gate_v, 17)
            act.activation(wi_em[rows, 0, :], wi_em[rows, 0, :], ACT.Exp).then_inc(gate_a, 1)
            act.activation(wi_em[rows, 1, :], wi_em[rows, 1, :], ACT.Exp, scale=-1.0).then_inc(gate_a, 1)

            for n in (4, 5, 6):
                act.wait_ge(w_used, n - 3)
                split(n)
            for t in range(TT):
                act.wait_ge(val_mm, t + 1)
                act.activation(V[:, t, :], PS[:, t, :], ACT.Copy).then_inc(val_out, 1)
            split(7)
            for n in (8, 9, 10):
                act.wait_ge(w_used, n - 4)
                split(n)
            for t in range(TT):
                act.wait_ge(val_mm, TT + t + 1)
                if t >= 2:
                    act.wait_ge(stored[t % 2], 16 * (t // 2))
                act.activation(stage[:, t % 2, 0:ML_WIDTH], PS[:, t, :], ACT.Copy).then_inc(val_out, 1)
            act.sem_inc(tile_out, 2)

            with act.Fori(0, PAIRS) as p:
                for step in fox_steps:
                    kind, *at = step
                    if kind == "unit":
                        j, = at
                        act.wait_ge(tile_mm, 2 + 2 * FOX_UNITS * p + 2 * j)
                        split(U_FOX + j + 2, FOX_UNITS // RING * p)
                    elif kind == "half":
                        j, h = at
                        n = 2 * FOX_UNITS * p + 2 * j + h
                        tokens = slice(h * HALF, (h + 1) * HALF)
                        if j < 2:
                            if j or h:
                                act.wait_ge(mean_mm, 4 * p + 2 * j + h)
                            act.wait_ge(tile_mm, n + 3)
                            act.activation(sq[:], PS[:, h, :], ACT.Square).then_inc(sq_set, 1)
                            act.activation(qk_raw[:, j, tokens], PS[:, h, :], ACT.Copy).then_inc(tile_out, 1)
                        elif j < 4:
                            if j == 3 and h == 0:
                                act.wait_ge(conv_step, 8 * p + 4)
                            act.wait_ge(tile_mm, n + 3)
                            act.activation(conv_in[:, TAPS - 1 + h * HALF:TAPS - 1 + (h + 1) * HALF],
                                           PS[:, h, :], ACT.Copy).then_inc(tile_out, 1)
                        else:
                            if h == 0:
                                act.wait_ge(stored[j % 2], 16 * (4 + 2 * p + 1))
                            act.wait_ge(tile_mm, n + 3)
                            act.activation(stage[:, j % 2, tokens], PS[:, h, :], ACT.Tanh,
                                           scale=0.5).then_inc(tile_out, 1)
                    elif kind == "norm":
                        x_, h = at
                        if x_ or h:
                            act.wait_ge(qk_set, 8 * p + 2 * (2 * x_ + h))
                        act.wait_ge(mean_mm, 4 * p + 2 * x_ + h + 1)
                        act.activation(root[:], PS[:, 2 + 2 * x_ + h, :], ACT.Sqrt,
                                       bias=eps_col[:]).then_inc(root_set, 1)
                    elif kind == "silu":
                        j, = at
                        act.wait_ge(stored[j % 2], 16 * (4 + 2 * p))
                        act.wait_ge(conv_step, 4 * (2 * p + j - 2) + 4)
                        act.activation(stage[:, j % 2, :], conv_acc[:], ACT.Tanh, scale=0.5).then_inc(tanh_set, 1)
                    elif kind == "scores":
                        s, = at
                        length = (s // 2 + 1) * P
                        if s >= 2:
                            act.wait_ge(prob_turn, FILLS * p + turn_fill(s - 2, int((s - 2) // 2 >= 4)) + 1)
                        act.wait_ge(nmax_set, 2 * TT * p + s + 1)
                        act.activation(prob[:, s % 2, 0:length], score_row(s), ACT.Exp, bias=nmax[:, s % 2:s % 2 + 1],
                                       accum_out=psumrow[:, s % 2:s % 2 + 1]).then_inc(prob_set, 1)

            with act.Fori(0, ML_STEPS) as q:
                for step in ml_steps:
                    kind, *at = step
                    if kind == "unit":
                        j, = at
                        act.wait_ge(tile_mm, 2 + 2 * FOX_UNITS * PAIRS + 2 * ML_UNITS * q + 2 * j)
                        split(U_ML + j + 2, ML_UNITS // RING * q)
                    elif kind == "half":
                        j, h = at
                        n = 2 * FOX_UNITS * PAIRS + 2 * ML_UNITS * q + 2 * j + h
                        if h == 0:
                            act.wait_ge(stored[j % 2], 16 * ml_stores(q, j))
                        act.wait_ge(tile_mm, n + 3)
                        act.activation(stage[:, j % 2, h * HALF:(h + 1) * HALF], PS[:, h, :], ACT.Tanh,
                                       scale=0.5).then_inc(tile_out, 1)
                    elif kind == "kq":
                        c, = at
                        act.wait_ge(ml_v, ml_at(q, "kq", c, 2))
                        act.activation(decay[:], decay[:], ACT.Exp).then_inc(decay_set, 1)
                    elif kind == "out":
                        c, = at
                        act.wait_ge(ml_v, ml_at(q, "out", c, 5))
                        act.activation(hstat[:, 4, :], hstat[:, 3, :], ACT.Sqrt, bias=eps_col[:],
                                       scale=1.0 / ML_DIM).then_inc(ml_root, 1)

            for k in range(KT):
                for h in range(2):
                    n = 2 * k + h
                    if k < PAIRS:
                        act.wait_ge(turned, 2 * KT + n + 1)
                        src = PS[:, n % 8, :]
                    else:
                        act.wait_ge(yb_set, n - 7)
                        src = yb[:, h, :]
                    act.activation(actT_hi[:, k, h * HALF:(h + 1) * HALF], src, ACT.Copy).then_inc(act_hi, 1)

            def merge_hi(m, a_slot):
                for h in range(2):
                    act.wait_ge(mix_v, 6 * m + 4 + 2 * h)
                    act.activation(A_hi[:, a_slot, h * HALF:(h + 1) * HALF], sg[:, 0, h * HALF:(h + 1) * HALF],
                                   ACT.Copy).then_inc(a_hi, 1)

            act.wait_ge(tile_mm, 2 + 2 * (U_MERGE - U_FOX))
            split(U_MERGE + 2)
            merge_hi(0, 0)
            with act.Fori(0, 2) as r:
                for i in range(3):
                    m = 3 * r + i + 1
                    act.wait_ge(down_mm, DOWN_START + 16 * (m - 1))
                    split(U_MERGE + 2 * i + 3, 2 * r)
                    merge_hi(m, (i + 1) % 3)
                    act.wait_ge(br_mm, 4 * (m + 1))
                    split(U_MERGE + 2 * i + 4, 2 * r)
            act.wait_ge(down_mm, DOWN_START + 16 * (KT - 2))
            split(U_MERGE + 15)
            merge_hi(KT - 1, 1)
            act.wait_ge(br_mm, 4 * KT)
            split(U_FFN)
            act.wait_ge(down_mm, DOWN_START + 16 * (KT - 1))
            split(U_FFN + 1)

            norm_rows(1, lambda t: act.wait_ge(x_add, X_START + 16 * (KT - 1) + 2 * t + 2), X, XN)
            norm_hi(1, 4 * KT)

            def gate_tanh(m, h):
                act.wait_ge(gu_mm, 4 * m + h + 1)
                act.activation(sg[:, 0, h * HALF:(h + 1) * HALF], PS[:, h, :], ACT.Tanh,
                               scale=0.5).then_inc(tanh_g, 1)

            def glu_hi(m, h, a_slot):
                act.wait_ge(glu_b, 2 * m + h + 1)
                act.activation(A_hi[:, a_slot, h * HALF:(h + 1) * HALF], sg[:, 1, h * HALF:(h + 1) * HALF],
                               ACT.Copy).then_inc(a_hi, 1)

            act.wait_ge(down_mm, DOWN_START + 16 * KT)
            split(U_FFN + 2)
            for h in range(2):
                gate_tanh(0, h)
            act.wait_ge(gu_mm, 2)
            split(U_FFN + 3)
            for h in range(2):
                glu_hi(0, h, 0)

            def ffn_tile(m, n, rounds, a_slot, more):
                act.wait_ge(gu_mm, 4 * m)
                act.wait_ge(down_mm, DOWN_START + 16 * (KT + m - 1))
                split(n + 2, rounds)
                for h in range(2):
                    gate_tanh(m, h)
                act.wait_ge(gu_mm, 4 * m + 2)
                split(n + 3, rounds)
                glu_hi(m, 0, a_slot)
                if more:
                    act.wait_ge(gu_mm, 4 * m + 4)
                    split(n + 4, rounds)
                glu_hi(m, 1, a_slot)

            with act.Fori(0, FT // 2 - 1) as r:
                for i in range(2):
                    at = 3 * i + 2
                    ffn_tile(2 * r + i + 1, U_FFN + at, 2 * r, (i + 1) % 2, True)
            at = U_FFN + 3 * (FT - 2) + 2
            ffn_tile(FT - 1, at, 0, 1, False)

        @block.vector
        def _(dve):
            def split(n, rounds=0):
                slot = n % RING
                dve.wait_ge(w_hi, n + RING * rounds + 1)
                dve.tensor_tensor(W_lo[:, slot, :], W_raw[:, slot, :], W_hi[:, slot, :].bitcast(F32),
                                  ALU.subtract).then_inc(w_lo, 1)

            def scale_rows(round_, src, dst):
                for h in range(2):
                    dve.wait_ge(rooted, 2 * round_ + h + 1)
                    dve.reciprocal(stat[:, 2, 4 * h:4 * h + 4], stat[:, 1, 4 * h:4 * h + 4]).then_inc(scaled, 1)
                    dve.wait_ge(scaled, 10 * round_ + 5 * h + 1)
                    for t in range(4 * h, 4 * h + 4):
                        dve.tensor_scalar(dst[:, t, :], src[:, t, :], stat[:, 2, t:t + 1], None,
                                          ALU.mult).then_inc(scaled, 1)

            def norm_lo(round_, base):
                for h in range(2):
                    for k in range(KT):
                        tokens = slice(h * HALF, (h + 1) * HALF)
                        dve.wait_ge(act_hi, base + h * KT + k + 1)
                        dve.scalar_tensor_tensor(actT_lo[:, k, tokens], PS[:, k, :], g_cols[:, round_, k:k + 1],
                                                 actT_hi[:, k, tokens].bitcast(F32), ALU.mult,
                                                 ALU.subtract).then_inc(act_lo, 1)

            dve.memset(eps_col[:], EPS).then_inc(cols_set, 1)
            dve.memset(conv_in[:, 0:TAPS - 1], 0.0).then_inc(cols_set, 1)
            dve.memset(head_mean[:], 0.0).then_inc(cols_set, 1)
            dve.wait_ge(cols_set, 3)
            for hd in range(2):
                at = slice(hd * FOX_DIM, (hd + 1) * FOX_DIM)
                dve.memset(head_mean[at, at], 1.0 / FOX_DIM).then_inc(cols_set, 1)
            dve.wait_ge(const_in, 16 * N_CONST)
            dve.tensor_scalar(g_qk[:, 0:1], g_qk[:, 0:1], FOX_DIM ** -0.5, None, ALU.mult).then_inc(cols_set, 1)

            scale_rows(0, X0, XN0)
            dve.wait_ge(w_hi, 1)
            dve.tensor_tensor(W_lo[:, 0, :], W_raw[:, 0, :], W_hi[:, 0, :].bitcast(F32),
                              ALU.subtract).then_inc(w_lo, 1)
            split(1)
            split(2)
            norm_lo(0, 0)

            ml = slice(ROW_FB, ROW_FB + ML_HEADS)
            fx = slice(ROW_FA, ROW_FA + FOX_HEADS)
            for h in range(2):
                dve.wait_ge(gate_mm, h + 1)
                dve.tensor_scalar(z[:, h * HALF:(h + 1) * HALF], PS[0:GATE_ROWS, h, :], gate_bias[:], None,
                                  ALU.add).then_inc(gate_v, 1)
            dve.memset(keep[:], 1.0).then_inc(gate_v, 1)
            dve.memset(shift[ml, :], 0.0).then_inc(gate_v, 1)
            dve.memset(m_prev[ml, :], 0.0).then_inc(gate_v, 1)
            dve.wait_ge(gate_v, 3)
            starts = keep[ml, :].rearrange("p (c t) -> p c t", t=CHUNK)[:, :, 0:1]
            dve.memset(starts, 0.0).then_inc(gate_v, 1)
            split(3)
            dve.wait_ge(gate_a, 4)
            dve.scalar_tensor_tensor(logs[:], z[:], 0.0, soft[:], ALU.min, ALU.subtract).then_inc(gate_v, 1)
            dve.wait_ge(gate_v, 7)
            dve.tensor_tensor_scan(csum[fx, :], keep[fx, :], logs[fx, :], 0.0, ALU.mult, ALU.add).then_inc(gate_v, 1)
            dve.tensor_tensor_scan(csum[ml, :], keep[ml, :], logs[ml, :], 0.0, ALU.mult, ALU.add).then_inc(gate_v, 1)
            dve.wait_ge(gate_v, 9)
            dve.tensor_scalar(negs[fx, :], csum[fx, :], -1.0, None, ALU.mult).then_inc(gate_v, 1)
            u_row, m_row = u_m[ml, 0, :], u_m[ml, 1, :]
            dve.tensor_tensor(u_row, u_row, csum[ml, :], ALU.subtract).then_inc(gate_v, 1)

            def ends(row):
                return row.rearrange("p (c t) -> p c t", t=CHUNK)[:, 0:CHUNKS - 1, CHUNK - 1]

            dve.tensor_copy(shift[ml, :].rearrange("p (c t) -> p c t", t=CHUNK)[:, 1:CHUNKS, 0],
                            ends(csum[ml, :])).then_inc(gate_v, 1)
            dve.wait_ge(gate_v, 12)
            dve.tensor_tensor_scan(m_row, shift[ml, :], u_row, 0.0, ALU.add, ALU.max).then_inc(gate_v, 1)
            dve.wait_ge(gate_v, 13)
            dve.tensor_tensor(m_prev[ml, 1:CHUNKS], ends(m_row), ends(csum[ml, :]), ALU.add).then_inc(gate_v, 1)
            dve.tensor_scalar(negs[ml, :], m_row, -1.0, None, ALU.mult).then_inc(gate_v, 1)
            dve.wait_ge(gate_v, 14)
            dve.tensor_tensor(wi_em[ml, 0, :].rearrange("p (c t) -> p c t", t=CHUNK),
                              m_prev[ml, :].unsqueeze(2).to_broadcast([ML_HEADS, CHUNKS, CHUNK]),
                              m_row.rearrange("p (c t) -> p c t", t=CHUNK), ALU.subtract).then_inc(gate_v, 1)
            dve.tensor_tensor(wi_em[ml, 1, :], csum[ml, :], m_row, ALU.add).then_inc(gate_v, 1)

            for n in range(4, 11):
                split(n)
            dve.wait_ge(gate_turn, 1)
            cols = CHUNKS * ML_HEADS
            dve.tensor_copy(uT[:].rearrange("p c h -> p (c h)"), PS[:, 2, 0:cols]).then_inc(gate_out, 1)
            dve.tensor_copy(emT[:].rearrange("p c h -> p (c h)"), PS[:, 2, cols:2 * cols]).then_inc(gate_out, 1)
            dve.wait_ge(rows_out, 64)
            dve.memset(QA[FOX_DIM:FOX_DIM + 2, :, :], 1.0).then_inc(ones_set, 1)
            dve.memset(KA[FOX_DIM:FOX_DIM + 2, :, :], 1.0).then_inc(ones_set, 1)

            with dve.Fori(0, PAIRS) as p:
                for step in fox_steps:
                    kind, *at = step
                    if kind == "unit":
                        j, = at
                        split(U_FOX + j + 2, FOX_UNITS // RING * p)
                    elif kind == "half":
                        j, h = at
                        n = 2 * FOX_UNITS * p + 2 * j + h
                        if h == 0 or j < 2:
                            continue
                        dve.wait_ge(tile_out, n + 3)
                        if j < 4:
                            tile = bass.ds(p + (j - 2) * ML_HEADS, 1)
                            done = 4 * (2 * p + j - 2)
                            dve.tensor_scalar(conv_acc[:], conv_in[:, TAPS - 1:TAPS - 1 + SEQ],
                                              taps[:, tile, TAPS - 1].opt(), taps[:, tile, TAPS].opt(),
                                              ALU.mult, ALU.add).then_inc(conv_step, 1)
                            for n_tap, tap in enumerate(range(TAPS - 2, -1, -1)):
                                dve.wait_ge(conv_step, done + n_tap + 1)
                                dve.scalar_tensor_tensor(conv_acc[:], conv_in[:, tap:tap + SEQ],
                                                         taps[:, tile, tap].opt(), conv_acc[:], ALU.mult,
                                                         ALU.add).then_inc(conv_step, 1)
                        else:
                            dve.tensor_scalar(stage[:, j % 2, :], stage[:, j % 2, :], 0.5, 0.5, ALU.mult,
                                              ALU.add).then_inc(tile_set, 1)
                    elif kind == "norm":
                        x_, h = at
                        tokens = slice(h * HALF, (h + 1) * HALF)
                        dst = (QA, KA)[x_]
                        dve.wait_ge(root_set, 4 * p + 2 * x_ + h + 1)
                        dve.reciprocal(root[:], root[:]).then_inc(inv_set, 1)
                        dve.wait_ge(inv_set, 4 * p + 2 * x_ + h + 1)
                        for hd in range(2):
                            rows = slice(hd * FOX_DIM, (hd + 1) * FOX_DIM)
                            dve.scalar_tensor_tensor(dst[0:FOX_DIM, hd, tokens], qk_raw[rows, x_, tokens],
                                                     g_qk[rows, x_:x_ + 1], root[rows, :], ALU.mult,
                                                     ALU.mult).then_inc(qk_set, 1)
                    elif kind == "silu":
                        j, = at
                        n = 2 * p + j - 2
                        dve.wait_ge(tanh_set, n + 1)
                        dve.scalar_tensor_tensor(stage[:, j % 2, :], stage[:, j % 2, :], 1.0, conv_acc[:], ALU.add,
                                                 ALU.mult).then_inc(conv_mul, 1)
                        dve.wait_ge(conv_mul, n + 1)
                        dve.tensor_scalar(stage[:, j % 2, :], stage[:, j % 2, :],
                                          0.5 if j == 2 else 0.5 * ML_DIM ** -0.5, None,
                                          ALU.mult).then_inc(tile_set, 1)
                    elif kind == "scores":
                        s, = at
                        dve.wait_ge(score_mm, 2 * TT * p + s + 1)
                        dve.tensor_reduce(nmax[:, s % 2:s % 2 + 1], score_row(s), AX_X, ALU.max,
                                          negate=True).then_inc(nmax_set, 1)
                    elif kind == "turn":
                        s, part = at
                        n = min(4, s // 2 + 1 - 4 * part)
                        if s and part == 0:
                            dve.wait_ge(y_mm, 2 * TT * p + s)
                        dve.wait_ge(prob_turn, FILLS * p + turn_fill(s, part) + 1)
                        dve.tensor_copy(probT[:, 4 * part:4 * part + n, :].rearrange("p b q -> p (b q)"),
                                        PS[:, 6, 0:n * P]).then_inc(probT_set, 1)
                    elif kind == "values":
                        s, = at
                        i, hd = divmod(s, 2)
                        n = 2 * TT * p + s
                        dve.wait_ge(prob_set, n + 1)
                        dve.reciprocal(rinv[:, hd:hd + 1], psumrow[:, hd:hd + 1]).then_inc(rinv_set, 1)
                        dve.wait_ge(rinv_set, n + 1)
                        dve.wait_ge(y_mm, n + 1)
                        dve.tensor_scalar(Y[:, i, bass.ds(p * P + hd * FOX_DIM, FOX_DIM)], PS[:, 7, 0:FOX_DIM],
                                          rinv[:, hd:hd + 1], None, ALU.mult).then_inc(y_set, 1)

            dve.memset(vc[:, :, :, ML_DIM:ML_DIM + 1].rearrange("p b h n -> p (b h) n"), 1.0).then_inc(ml_v, 1)
            dve.memset(state[:].rearrange("p h n -> p (h n)"), 0.0).then_inc(ml_v, 1)
            with dve.Fori(0, ML_STEPS) as q:
                for step in ml_steps:
                    kind, *at = step
                    if kind == "unit":
                        j, = at
                        split(U_ML + j + 2, ML_UNITS // RING * q)
                        continue
                    if kind == "half":
                        j, h = at
                        if h:
                            dve.wait_ge(tile_out, 2 * FOX_UNITS * PAIRS + 2 * ML_UNITS * q + 2 * j + h + 3)
                            dve.tensor_scalar(stage[:, j % 2, :], stage[:, j % 2, :], 0.5, 0.5, ALU.mult,
                                              ALU.add).then_inc(tile_set, 1)
                        continue
                    if kind == "dense":
                        continue
                    c, = at
                    chunk = bass.ds(2 * q + c, 1)

                    def step_done(n, kind=kind, c=c):
                        dve.wait_ge(ml_v, ml_at(q, kind, c, n))

                    def by_head(cols):
                        return cols.unsqueeze(2).to_broadcast([P, ML_HEADS, CHUNK])

                    if kind == "kq":
                        dve.wait_ge(chunk_in[3][c], 16 * (q + 1))
                        dve.tensor_tensor(decay[:], m_rows[:, c, 0, :, :],
                                          mask_ml[:].unsqueeze(1).to_broadcast([P, ML_HEADS, CHUNK]),
                                          ALU.add).then_inc(ml_v, 1)
                        step_done(1)
                        u_cols = uT[:, chunk, :].rearrange("p a h -> p (a h)")
                        dve.tensor_tensor(decay[:], decay[:], by_head(u_cols), ALU.add).then_inc(ml_v, 1)
                        dve.wait_ge(chunk_in[4][c], 16 * (q + 1))
                        dve.wait_ge(chunk_in[0][c], 16 * (q + 1))
                        dve.tensor_tensor(qs[:], qc[:, c, :, :], m_rows[:, c, 1, :, :], ALU.mult).then_inc(ml_v, 1)
                        dve.wait_ge(decay_set, 2 * q + c + 1)
                        dve.wait_ge(kq_mm, 2 * q + c + 1)
                        dve.tensor_tensor(sw[:], PS[:, 2, :].rearrange("p (h t) -> p h t", h=ML_HEADS), decay[:],
                                          ALU.mult).then_inc(ml_v, 1)
                        dve.tensor_tensor(kw[:], PS[:, 6, :].rearrange("p (h t) -> p h t", h=ML_HEADS),
                                          by_head(decay[:, :, CHUNK - 1]), ALU.mult).then_inc(ml_v, 1)
                    elif kind == "num":
                        dve.wait_ge(num_mm, 2 * q + c + 1)
                        for b in range(2):
                            two = PS[:, 3 + b, 0:258].rearrange("p (h n) -> p h n", h=2)
                            dve.scalar_tensor_tensor(
                                hstat[:, 0, 2 * b:2 * b + 2], two[:, :, ML_DIM], -1.0,
                                emT[:, chunk, 2 * b:2 * b + 2].rearrange("p a h -> p (a h)"), ALU.mult,
                                ALU.max).then_inc(ml_v, 1)
                        step_done(2)
                        for b in range(2):
                            two = PS[:, 3 + b, 0:258].rearrange("p (h n) -> p h n", h=2)
                            den = hstat[:, 0, 2 * b:2 * b + 2]
                            dve.tensor_tensor(den, two[:, :, ML_DIM], den, ALU.max).then_inc(ml_v, 1)
                        step_done(4)
                        dve.reciprocal(hstat[:, 1, :], hstat[:, 0, :]).then_inc(ml_v, 1)
                        step_done(5)
                        for b in range(2):
                            two = PS[:, 3 + b, 0:258].rearrange("p (h n) -> p h n", h=2)
                            dve.tensor_tensor(hb[:, 2 * b:2 * b + 2, :], two[:, :, 0:ML_DIM],
                                              hstat[:, 1, 2 * b:2 * b + 2].unsqueeze(2).to_broadcast([P, 2, ML_DIM]),
                                              ALU.mult).then_inc(ml_v, 1)
                    elif kind == "state":
                        dve.wait_ge(state_mm, 2 * q + c + 1)
                        for h in range(ML_HEADS):
                            dve.scalar_tensor_tensor(
                                state[:, h, :], state[:, h, :], m_rows[:, c, 1, h, CHUNK - 1:CHUNK],
                                PS[:, (5, 7)[h // 2], (h % 2) * 129:(h % 2 + 1) * 129], ALU.mult,
                                ALU.add).then_inc(ml_v, 1)
                    elif kind == "out":
                        step_done(7, "num")
                        dve.tensor_reduce(hstat[:, 2, :], hb[:], AX_X, ALU.add).then_inc(ml_v, 1)
                        step_done(1)
                        dve.tensor_scalar(hstat[:, 2, :], hstat[:, 2, :], -1.0 / ML_DIM, None,
                                          ALU.mult).then_inc(ml_v, 1)
                        step_done(2)
                        dve.tensor_tensor(hb[:], hb[:], by_head(hstat[:, 2, :]), ALU.add).then_inc(ml_v, 1)
                        step_done(3)
                        dve.tensor_tensor(hsq[:], hb[:], hb[:], ALU.mult).then_inc(ml_v, 1)
                        step_done(4)
                        dve.tensor_reduce(hstat[:, 3, :], hsq[:], AX_X, ALU.add).then_inc(ml_v, 1)
                        dve.wait_ge(ml_root, 2 * q + c + 1)
                        dve.reciprocal(hstat[:, 5, :], hstat[:, 4, :]).then_inc(ml_v, 1)
                        step_done(6)
                        dve.tensor_tensor(HN[:, chunk, :].rearrange("p a (h n) -> p (a h) n", h=ML_HEADS), hb[:],
                                          by_head(hstat[:, 5, :]), ALU.mult).then_inc(ml_v, 1)

            dve.wait_ge(sob_in, 16)
            for k in range(KT):
                for h in range(2):
                    n = 2 * k + h
                    tokens = slice(h * HALF, (h + 1) * HALF)
                    src = PS[:, n % 8, :]
                    if k >= PAIRS:
                        dve.wait_ge(turned, 2 * KT + n + 1)
                        dve.scalar_tensor_tensor(yb[:, h, :], src, g_ml[:, k - PAIRS:k - PAIRS + 1],
                                                 sob[:, k - PAIRS, tokens], ALU.mult, ALU.mult).then_inc(yb_set, 1)
                        src = yb[:, h, :]
                    dve.wait_ge(act_hi, 2 * KT + n + 1)
                    dve.tensor_tensor(actT_lo[:, k, tokens], src, actT_hi[:, k, tokens].bitcast(F32),
                                      ALU.subtract).then_inc(act_lo, 1)
            split(U_MERGE + 2)

            def add_down(tile):
                for g in range(16):
                    t, c = divmod(g, 2)
                    cols = slice(c * 512, (c + 1) * 512)
                    dve.wait_ge(x_add, X_START + 16 * (tile - 1) + g + 1)
                    dve.wait_ge(down_mm, DOWN_START + 16 * tile + g + 1)
                    dve.tensor_tensor(X[:, t, cols], X[:, t, cols], PS[:, 4 + g % 4, :],
                                      ALU.add).then_inc(x_add, 1)

            def a_lo_part(tile, h, a_slot, src):
                tokens = slice(h * HALF, (h + 1) * HALF)
                dve.wait_ge(a_hi, 2 * tile + h + 1)
                dve.tensor_tensor(A_lo[:, a_slot, tokens], sg[:, src, tokens],
                                  A_hi[:, a_slot, tokens].bitcast(F32), ALU.subtract).then_inc(a_lo, 1)

            def mix(m, a_slot):
                dve.wait_ge(g_in[0], 16 * (m + 1))
                dve.wait_ge(g_in[1], 16 * (m + 1))
                for h in range(2):
                    tokens = slice(h * HALF, (h + 1) * HALF)
                    dve.wait_ge(br_mm, 4 * m + h + 1)
                    dve.tensor_tensor(sg[:, 0, tokens], PS[:, h, :], sg[:, 0, tokens], ALU.mult).then_inc(mix_v, 1)
                for h in range(2):
                    tokens = slice(h * HALF, (h + 1) * HALF)
                    dve.wait_ge(br_mm, 4 * m + h + 3)
                    dve.tensor_tensor(sg[:, 1, tokens], PS[:, 2 + h, :], sg[:, 1, tokens],
                                      ALU.mult).then_inc(mix_v, 1)
                    dve.wait_ge(mix_v, 6 * m + 3 + 2 * h)
                    dve.tensor_tensor(sg[:, 0, tokens], sg[:, 0, tokens], sg[:, 1, tokens],
                                      ALU.add).then_inc(mix_v, 1)
                for h in range(2):
                    a_lo_part(m, h, a_slot, 0)

            dve.sem_inc(x_add, X_START)
            mix(0, 0)
            for t in range(TT):
                dve.wait_ge(x_in[t], 32)
            with dve.Fori(0, 2) as r:
                for i in range(3):
                    split(U_MERGE + 2 * i + 3, 2 * r)
                    mix(3 * r + i + 1, (i + 1) % 3)
                    split(U_MERGE + 2 * i + 4, 2 * r)
                    add_down(3 * r + i)
            split(U_MERGE + 15)
            mix(KT - 1, 1)
            split(U_FFN)
            add_down(KT - 2)
            split(U_FFN + 1)
            add_down(KT - 1)

            scale_rows(1, X, XN)
            norm_lo(1, 4 * KT)

            def glu_gate(m, h):
                tokens = slice(h * HALF, (h + 1) * HALF)
                dve.wait_ge(tanh_g, 2 * m + h + 1)
                dve.scalar_tensor_tensor(sg[:, 0, tokens], sg[:, 0, tokens], 1.0, PS[:, h, :], ALU.add,
                                         ALU.mult).then_inc(glu_a, 1)

            def glu_up(m, h):
                tokens = slice(h * HALF, (h + 1) * HALF)
                dve.wait_ge(glu_a, 2 * m + h + 1)
                dve.wait_ge(gu_mm, 4 * m + h + 3)
                dve.scalar_tensor_tensor(sg[:, 1, tokens], sg[:, 0, tokens], 0.5, PS[:, 2 + h, :], ALU.mult,
                                         ALU.mult).then_inc(glu_b, 1)

            split(U_FFN + 2)
            for h in range(2):
                glu_gate(0, h)
            split(U_FFN + 3)
            for h in range(2):
                glu_up(0, h)
                a_lo_part(KT, h, 0, 1)

            def ffn_tile(m, n, rounds, a_slot, more):
                split(n + 2, rounds)
                for h in range(2):
                    glu_gate(m, h)
                split(n + 3, rounds)
                glu_up(m, 0)
                a_lo_part(KT + m, 0, a_slot, 1)
                glu_up(m, 1)
                if more:
                    split(n + 4, rounds)
                a_lo_part(KT + m, 1, a_slot, 1)
                add_down(KT + m - 1)

            with dve.Fori(0, FT // 2 - 1) as r:
                for i in range(2):
                    at = 3 * i + 2
                    ffn_tile(2 * r + i + 1, U_FFN + at, 2 * r, (i + 1) % 2, True)
            at = U_FFN + 3 * (FT - 2) + 2
            ffn_tile(FT - 1, at, 0, 1, False)
            add_down(KT + FT - 1)

        @block.sync
        def _(sp):
            for t in range(TT):
                sp.dma_start(X0[:, t, :], x_tiles[t]).then_inc(x_in[t], 16)
            sp.wait_ge(gate_zero, 2)
            w_gates = w_tile(W_raw, 0)
            for row, name, n in ((ROW_FA, "fa", FOX_HEADS), (ROW_IB, "ib", ML_HEADS), (ROW_FB, "fb", ML_HEADS)):
                sp.dma_start(w_gates[:, :, row:row + n], w_cols(w_in, COL[name], n)).then_inc(gate_raw, 16)
            consts = (
                [(g_cols[:, i, :], g[0].rearrange("(k p) -> p k", p=P)) for i, g in enumerate((g_mix, g_ffn))]
                + [(g_qk[hd * FOX_DIM:(hd + 1) * FOX_DIM, i:i + 1], g[0].rearrange("(p a) -> p a", a=1))
                   for i, g in enumerate((g_q_fox, g_k_fox)) for hd in range(2)]
                + [(g_ml[:], g_mlstm_h[0].rearrange("(k p) -> p k", p=P))]
                + [(gate_bias[row:row + n, :], b[0].rearrange("(p a) -> p a", a=1))
                   for row, b, n in ((ROW_FA, b_fox_f, FOX_HEADS), (ROW_IB, b_mlstm_i, ML_HEADS),
                                     (ROW_FB, b_mlstm_f, ML_HEADS))]
                + [(taps[:, :, tap], conv_w[tap].rearrange("(k p) -> p k", p=P)) for tap in range(TAPS)]
                + [(taps[:, :, TAPS], conv_b[0].rearrange("(k p) -> p k", p=P))])
            assert len(consts) == N_CONST
            for dst, src in consts:
                sp.dma_start(dst, src, allow_slow_non_contiguous=True).then_inc(const_in, 16)

            def load(n, slot, src, free=True):
                if free:
                    sp.wait_ge(w_lo, n - 2)
                sp.dma_start(w_tile(W_raw, slot), src).then_inc(w_raw[slot], 16)

            for b, name in enumerate(("va", "vb")):
                for u in range(4):
                    n = U_VALUES + 4 * b + u
                    if n >= RING:
                        sp.wait_ge(w_lo, n - 2)
                    src = w_in[2 * u * P:2 * (u + 1) * P, COL[name]:COL[name] + 512]
                    sp.dma_start(W_raw[:, n % RING, :].rearrange("p (k n) -> p k n", k=2),
                                 src.rearrange("(k p) n -> p k n", p=P)).then_inc(w_raw[n % RING], 16)

            with sp.Fori(0, PAIRS) as p:
                for j, name in enumerate(("qa", "ka", "qb", "kb", "ob", "ga")):
                    load(U_FOX + FOX_UNITS * p + j, j % RING, w_cols(w_in, P * p + COL[name]))

            with sp.Fori(0, ML_STEPS) as q:
                for j in range(ML_UNITS):
                    col = COL["ga"] + P * G_IN_FOX + P * ML_UNITS * q + P * j
                    load(U_ML + ML_UNITS * q + j, j % RING, w_cols(w_in, col))

            def load_branches(n, slot, m):
                sp.wait_ge(w_lo, n - 2)
                raw = w_tile(W_raw, slot)
                sp.dma_start(raw[:, 0:4, :], w_cols(w_fox_out, P * m)).then_inc(w_first, 16)
                sp.wait_ge(w_first, 16 * (m + 1))
                sp.dma_start(raw[:, 4:8, :], w_cols(w_mlstm_out, P * m)).then_inc(w_raw[slot], 16)

            def load_rows(n, slot, w, tile):
                sp.wait_ge(w_lo, n - 2)
                sp.dma_start(W_raw[:, slot, :],
                             w.rearrange("(k p) n -> k p n", p=P)[bass.ds(tile, 1)].rearrange("a p n -> (a p) n"))\
                    .then_inc(w_raw[slot], 16)

            load_branches(U_MERGE, 0, 0)
            load_branches(U_MERGE + 1, 1, 1)
            sp.wait_ge(ml_v, ML_SETUP + ML_STEPS * ML_V_STEPS)
            for t in range(TT):
                sp.dma_start(X[:, t, :], x_tiles[t]).then_inc(x_in[t], 16)
            load_rows(U_MERGE + 2, 2, w_o, 0)
            with sp.Fori(0, 2) as r:
                for i in range(3):
                    n = U_MERGE + 6 * r + 2 * i + 3
                    load_branches(n, (2 * i + 3) % RING, 3 * r + i + 2)
                    load_rows(n + 1, (2 * i + 4) % RING, w_o, 3 * r + i + 1)
            load_rows(U_MERGE + 15, 15 % RING, w_o, KT - 1)

            load(U_FFN, U_FFN % RING, w_cols(w_gate, 0))
            load(U_FFN + 1, (U_FFN + 1) % RING, w_cols(w_up, 0))
            with sp.Fori(0, FT // 2 - 1) as r:
                for i in range(2):
                    n = U_FFN + 6 * r + 3 * i + 2
                    slot = U_FFN + 3 * i + 2
                    m = 2 * r + i + 1
                    load(n, slot % RING, w_cols(w_gate, P * m))
                    load(n + 1, (slot + 1) % RING, w_cols(w_up, P * m))
                    load_rows(n + 2, (slot + 2) % RING, w_down, m - 1)
            n = U_FFN + 3 * (FT - 2) + 2
            load(n, n % RING, w_cols(w_gate, P * (FT - 1)))
            load(n + 1, (n + 1) % RING, w_cols(w_up, P * (FT - 1)))
            load_rows(n + 2, (n + 2) % RING, w_down, FT - 2)
            load_rows(n + 3, (n + 3) % RING, w_down, FT - 1)

            for t in range(TT):
                sp.wait_ge(x_add, X_START + 16 * (KT + FT - 1) + 2 * t + 2)
                sp.dma_start(out_tiles[t], X[:, t, :]).then_inc(out_in, 16)
            sp.wait_ge(out_in, 16 * TT)

        @block.gpsimd
        def _(pool):
            def wait(signal, count):
                pool.wait_ge(signal, count)
                pool.sem_inc(transfer_due, 1)

            pool.memset(W_raw[:, 0, :], 0.0).then_inc(gate_zero, 1)
            pool.memset(gate_bias[:], 0.0).then_inc(gate_zero, 1)
            pool.memset(ident[:], 0.0).then_inc(const_set, 1)
            pool.memset(ident_bf[:], 0.0).then_inc(const_set, 1)
            pool.memset(mask_bf[:], 0.0).then_inc(const_set, 1)
            pool.memset(mask_ml[:], 0.0).then_inc(const_set, 1)
            pool.wait_ge(const_set, 4)
            for m in (ident, ident_bf):
                pool.affine_select(out=m[:], in_=m[:], compare_op=ALU.not_equal, fill=1.0, base=0,
                                   pattern=[[-1, P]], channel_multiplier=1).then_inc(const_set, 1)
            pool.affine_select(out=mask_bf[:], in_=mask_bf[:], compare_op=ALU.is_ge, fill=MASKED, base=0,
                               pattern=[[-1, P]], channel_multiplier=1).then_inc(const_set, 1)
            pool.affine_select(out=mask_ml[:], in_=mask_ml[:], compare_op=ALU.is_ge, fill=MASKED, base=0,
                               pattern=[[1, P]], channel_multiplier=-1).then_inc(const_set, 1)

            rows = slice(ROW_FB, ROW_FB + ML_HEADS)
            pool.wait_ge(gate_a, 6)
            for dst, src in ((d_c[0], csum[0:FOX_HEADS, :]), (d_c[1], negs[0:FOX_HEADS, :]),
                             (d_m[0], negs[rows, :]), (d_m[1], wi_em[rows, 0, :])):
                pool.dma_start(dst, src).then_inc(rows_out, 16)

            for t in range(TT):
                pool.wait_ge(val_out, TT + t + 1)
                pool.dma_start(d_v[t], stage[:, t % 2, 0:ML_WIDTH]).then_inc(stored[t % 2], 16)

            def store(dst, slot):
                pool.dma_start(dst, stage[:, slot, :]).then_inc(stored[slot], 16)

            def one(d, at):
                return d[bass.ds(at, 1)].rearrange("a p n -> (a p) n")

            pool.wait_ge(rows_out, 64)
            pool.wait_ge(ones_set, 2)
            with pool.Fori(0, PAIRS) as p:
                wait(qk_set, 8 * p + 1)
                pair = bass.ds(2 * p, 2)
                pool.dma_start(QA[FOX_DIM:FOX_DIM + 1, :, :], d_c[0:1, pair, :]).then_inc(c_in[0], 16)
                pool.dma_start(KA[FOX_DIM + 1:FOX_DIM + 2, :, :], d_c[1:2, pair, :]).then_inc(c_in[1], 16)
                for n, (d, at) in enumerate(((d_qk, p), (d_qk, p + ML_HEADS), (d_ob, p), (d_g, p))):
                    wait(tile_set, 4 * p + n + 1)
                    store(one(d, at), n % 2)

            pool.wait_ge(stored[0], 16 * (4 + 2 * PAIRS))
            pool.wait_ge(stored[1], 16 * (4 + 2 * PAIRS))
            pool.wait_ge(ml_v, ML_SETUP)

            def load_chunk(n, b):
                tok = bass.ds(CHUNK * n, CHUNK)
                pool.dma_start(m_rows[:, b, 0, :, :], d_m[0, :, tok].partition_broadcast(P))\
                    .then_inc(chunk_in[3][b], 16)
                pool.dma_start(m_rows[:, b, 1, :, :], d_m[1, :, tok].partition_broadcast(P))\
                    .then_inc(chunk_in[4][b], 16)
                pool.dma_start(qc[:, b, :, :], d_qk[0:ML_HEADS, :, tok].rearrange("h p t -> p h t"))\
                    .then_inc(chunk_in[0][b], 16)
                pool.dma_start(kc[:, b, :, :], d_qk[ML_HEADS:2 * ML_HEADS, :, tok].rearrange("h p t -> p h t"))\
                    .then_inc(chunk_in[1][b], 16)
                pool.dma_start(vc[:, b, :, 0:ML_DIM],
                               one(d_v, n).rearrange("p (h n) -> p h n", h=ML_HEADS)).then_inc(chunk_in[2][b], 16)

            def ml_stage(q, more):
                for step in ml_steps:
                    kind, *at = step
                    if kind == "half" and at[1] == 1:
                        j = at[0]
                        wait(tile_set, 4 * PAIRS + ML_UNITS * q + j + 1)
                        store(one(d_g, G_IN_FOX + ML_UNITS * q + j), j % 2)
                    elif kind == "out" and more:
                        c, = at
                        wait(ml_v, ml_at(q, "state", c, 4))
                        load_chunk(2 * q + 2 + c, c)

            load_chunk(0, 0)
            load_chunk(1, 1)
            with pool.Fori(0, ML_STEPS - 1) as q:
                ml_stage(q, True)
            ml_stage(ML_STEPS - 1, False)

            pool.wait_ge(stored[0], 16 * ml_stores(ML_STEPS, 0))
            pool.wait_ge(stored[1], 16 * ml_stores(ML_STEPS, 1))
            pool.wait_ge(ml_v, ML_SETUP + ML_STEPS * ML_V_STEPS)
            pool.dma_start(sob[:], d_ob.rearrange("k p n -> p k n")).then_inc(sob_in, 16)

            def load_g(m):
                for i in range(2):
                    pool.dma_start(sg[:, i, :], one(d_g, m + KT * i)).then_inc(g_in[i], 16)

            pool.wait_ge(act_lo, 4 * KT)
            load_g(0)
            with pool.Fori(1, KT) as m:
                wait(a_lo, 2 * m)
                load_g(m)


_INS = ["x", "g_mix", "w_in", "b_fox_f", "g_q_fox", "g_k_fox", "conv_w", "conv_b", "b_mlstm_i", "b_mlstm_f",
        "g_mlstm_h", "w_fox_out", "w_mlstm_out", "w_o", "g_ffn", "w_gate", "w_up", "w_down"]


def kernel(**inputs):
    import concourse.bacc as bacc
    from concourse.bass_utils import run_bass_kernel_spmd

    nc = bacc.Bacc("TRN2", target_bir_lowering=False, num_devices=1)
    arrays, args = {}, []
    for name in _INS:
        a = np.ascontiguousarray(inputs[name])
        arrays[f"in_{name}"] = a
        args.append(nc.dram_tensor(f"in_{name}", a.shape, F32, kind="ExternalInput").ap())
    out = nc.dram_tensor("out", (1, SEQ, D_MODEL), F32, kind="ExternalOutput").ap()
    hybrid_block(nc, *args, out)
    r = run_bass_kernel_spmd(nc, [arrays], core_ids=[0])
    return r.results[0]["out"]
```

```python
from contextlib import ExitStack

import numpy as np

import concourse.bass as bass
from concourse import mybir

F32 = mybir.dt.float32
F32R = mybir.dt.float32r
BF16 = mybir.dt.bfloat16
ACT = mybir.ActivationFunctionType
ALU = mybir.AluOpType
AX_X = mybir.AxisListType.X

P = 128
SEQ = 1024
D_MODEL = 1024
KT = D_MODEL // P
TT = SEQ // P
HALF = SEQ // 2
FOX_HEADS, FOX_DIM = 8, 64
FOX_WIDTH = FOX_HEADS * FOX_DIM
PAIRS = FOX_HEADS // 2
ML_HEADS, ML_DIM = 4, 128
ML_WIDTH = ML_HEADS * ML_DIM
CHUNK = 128
CHUNKS = SEQ // CHUNK
TAPS = 4
D_FF = 2816
FT = D_FF // P
EPS = 1e-6
MASKED = -1e30
LOWEST = -3e38

COL = {}
_at = 0
for _name, _width in (("qa", FOX_WIDTH), ("ka", FOX_WIDTH), ("va", FOX_WIDTH), ("fa", FOX_HEADS),
                      ("qb", ML_WIDTH), ("kb", ML_WIDTH), ("vb", ML_WIDTH), ("ib", ML_HEADS), ("fb", ML_HEADS),
                      ("ob", ML_WIDTH), ("ga", D_MODEL), ("gb", D_MODEL)):
    COL[_name] = _at
    _at += _width
IN_WIDTH = _at

ROW_FA, ROW_IB, ROW_FB = 0, 32, 64
GATE_ROWS = ROW_FB + ML_HEADS

RING = 3
U_GATES = 0
U_VALUES = 1
U_FOX = U_VALUES + 8
FOX_UNITS = 6
U_ML = U_FOX + PAIRS * FOX_UNITS
ML_UNITS = 3
ML_STEPS = CHUNKS // 2
U_MERGE = U_ML + ML_STEPS * ML_UNITS
U_FFN = U_MERGE + 2 * KT
U_END = U_FFN + 3 * FT
assert U_FOX % RING == 0 and FOX_UNITS % RING == 0 and ML_UNITS % RING == 0 and U_MERGE % RING == 0
G_IN_FOX = PAIRS
N_TAPS_COLS = TAPS + 1


N_CONST = 13


def raw_count(n, rounds):
    return n // RING + (1 if n % RING else 0) + rounds


def ml_stores(q, j):
    before = 4 + 2 * PAIRS
    return before + 2 * q + (j == 2) if j % 2 == 0 else before + q


TURN_GAP, VALUES_GAP = 3, 6
ATTEND_AFTER = 12


def fox_schedule():
    def half(j, h):
        return ([("unit", j)] if h == 0 else []) + [("dense", j, h, a, a + 1) for a in range(24)] + [("half", j, h)]
    def then(j, h, x, xh):
        steps = half(j, h)
        return steps[:7] + [("norm", x, xh)] + steps[7:]
    head = half(0, 0) + then(0, 1, 0, 0) + then(1, 0, 0, 1) + then(1, 1, 1, 0) + then(2, 0, 1, 1)
    rest = half(2, 1) + [e for j in (3, 4, 5) for h in (0, 1) for e in half(j, h)]
    steps = 2 * TT
    attend, gap = [[("scores", 0), ("exp", 0), ("scores", 1), ("exp", 1)]], [0]
    for s in range(steps):
        group = [("turn", s, 0)]
        if s + 2 < steps:
            group.append(("scores", s + 2))
        if s // 2 >= 4:
            if s + 2 >= steps:
                attend.append(group)
                gap.append(TURN_GAP)
                group = []
            group.append(("turn", s, 1))
        if s + 2 < steps:
            group.append(("exp", s + 2))
        attend += [group, [("values", s)]]
        gap += [TURN_GAP, VALUES_GAP if s // 2 >= 4 else TURN_GAP + 1]
    n_mm = sum(e[0] == "dense" for e in rest)
    out, seen, used, later = [], 0, 0, []
    for e in rest:
        if e[0] == "dense":
            while used < len(attend) and sum(gap[:used + 1]) * (n_mm - ATTEND_AFTER) <= (seen - ATTEND_AFTER) * sum(gap):
                out += attend[used]
                used += 1
            while later and seen >= later[0][0]:
                out.append(later.pop(0)[1])
            seen += 1
        out.append(e)
        if e[0] == "half" and e[1] in (2, 3) and e[2] == 1:
            later += [(seen + 5 * n, ("conv", e[1], n)) for n in range(TAPS)] + [(seen + 21, ("silu", e[1]))]
    assert not later
    return head + out + [x for a in attend[used:] for x in a]


def ml_schedule():
    steps = [("kq", 0), ("num", 0), ("state", 0), ("kq", 1), ("out", 0), ("num", 1), ("flip", 0), ("state", 1),
             ("out", 1), ("flip", 1)]
    at = [0, 18, 34, 54, 58, 74, 84, 90, 104, 138]
    out, seen = [], 0
    for j in range(ML_UNITS):
        for h in (0, 1):
            if h == 0:
                out.append(("unit", j))
            for a in range(24):
                while at and at[0] <= seen:
                    out.append(steps.pop(0))
                    at.pop(0)
                out.append(("dense", j, h, a, a + 1))
                seen += 1
            out.append(("half", j, h))
    return out + steps


def turn_fill(s, part):
    i = s // 2
    return (s if i < 4 else 8 + 2 * (s - 8)) + part


FILLS = turn_fill(2 * TT - 1, 1) + 1


ML_STEP_COUNT = {"kq": 5, "num": 7, "state": 4, "out": 7, "flip": 1}
ML_SETUP = 3
ML_OFFSET = {}
ML_V_STEPS = 0
for _step in ml_schedule():
    if _step[0] in ML_STEP_COUNT:
        ML_OFFSET[_step] = ML_V_STEPS
        ML_V_STEPS += ML_STEP_COUNT[_step[0]]

Y_BANKS = (4, 5, 7, 6, 2, 3, 4, 5)
X_START = 16
DOWN_START = 16


def ml_at(q, kind, c, steps):
    return ML_SETUP + ML_V_STEPS * q + ML_OFFSET[kind, c] + steps


def hybrid_block(nc, x, g_mix, w_in, b_fox_f, g_q_fox, g_k_fox, conv_w, conv_b, b_mlstm_i, b_mlstm_f,
                 g_mlstm_h, w_fox_out, w_mlstm_out, w_o, g_ffn, w_gate, w_up, w_down, out):
    fox_steps, ml_steps = fox_schedule(), ml_schedule()
    w_in, conv_w, w_fox_out, w_mlstm_out, w_o = w_in[0], conv_w[0], w_fox_out[0], w_mlstm_out[0], w_o[0]
    w_gate, w_up, w_down = w_gate[0], w_up[0], w_down[0]

    d_qk = nc.dram_tensor("d_qk", (2 * ML_HEADS, P, SEQ), F32, kind="Internal").ap()
    d_v = nc.dram_tensor("d_v", (TT, P, ML_WIDTH), F32, kind="Internal").ap()
    d_ob = nc.dram_tensor("d_ob", (ML_HEADS, P, SEQ), F32, kind="Internal").ap()
    d_g = nc.dram_tensor("d_g", (2 * KT, P, SEQ), F32, kind="Internal").ap()
    d_c = nc.dram_tensor("d_c", (2, FOX_HEADS, SEQ), F32, kind="Internal").ap()
    d_m = nc.dram_tensor("d_m", (2, ML_HEADS, SEQ), F32, kind="Internal").ap()

    x_tiles = x[0].rearrange("(t p) d -> t p d", p=P)
    out_tiles = out[0].rearrange("(t p) d -> t p d", p=P)

    def w_cols(w, col, n=P):
        return w.rearrange("(k p) n -> p k n", p=P)[:, :, bass.ds(col, n)]

    with ExitStack() as ctx:
        def sb(name, shape, dt=F32, where=ctx):
            return where.enter_context(nc.sbuf_tensor(name, shape, dt))

        def sem(name):
            return ctx.enter_context(nc.semaphore(name))

        actT_hi = sb("actT_hi", [P, KT, SEQ], F32R)
        actT_lo = sb("actT_lo", [P, KT, SEQ], F32R)
        W_hi = sb("W_hi", [P, RING, 1024], F32R)
        W_lo = sb("W_lo", [P, RING, 1024], F32R)
        W_raw = sb("W_raw", [P, RING, 1024])
        ident = sb("ident", [P, P])
        ident_bf = sb("ident_bf", [P, P], BF16)
        mask_bf = sb("mask_bf", [P, P], BF16)
        mask_ml = sb("mask_ml", [P, P])
        head_mean = sb("head_mean", [P, P])
        g_cols = sb("g_cols", [P, 2, KT])
        g_qk = sb("g_qk", [P, 2])
        g_ml = sb("g_ml", [P, ML_HEADS])
        gate_bias = sb("gate_bias", [GATE_ROWS, 1])
        taps = sb("taps", [P, 2 * ML_HEADS, N_TAPS_COLS])
        eps_col = sb("eps_col", [P, 1])
        stat = sb("stat", [P, 3, TT])
        uT = sb("uT", [P, CHUNKS, ML_HEADS])
        emT = sb("emT", [P, CHUNKS, ML_HEADS])
        nmax = sb("nmax", [P, 2])
        psumrow = sb("psumrow", [P, 2])
        rinv = sb("rinv", [P, 2])
        hstat = sb("hstat", [P, 6, ML_HEADS])

        def chunk_buffers(n, where):
            return (sb(f"qc{n}", [P, ML_HEADS, CHUNK], where=where), sb(f"kc{n}", [P, ML_HEADS, CHUNK], where=where),
                    sb(f"vc{n}", [P, ML_HEADS, ML_DIM + 1], where=where),
                    sb(f"m_rows{n}", [P, 2, ML_HEADS, CHUNK], where=where),
                    sb(f"oc{n}", [P, ML_HEADS, CHUNK], where=where))

        with ExitStack() as early:
            X0 = sb("X0", [P, TT, D_MODEL], where=early)
            scale0 = sb("scale0", [P, TT, P], where=early)
            dump0 = sb("dump0", [P, 4, D_MODEL], where=early)
        with ExitStack() as gates:
            V = sb("V", [P, TT, FOX_WIDTH], where=gates)
            z = sb("z", [GATE_ROWS, SEQ], where=gates)
            soft = sb("soft", [GATE_ROWS, SEQ], where=gates)
            logs = sb("logs", [GATE_ROWS, SEQ], where=gates)
            keep = sb("keep", [GATE_ROWS, SEQ], where=gates)
            csum = sb("csum", [GATE_ROWS, SEQ], where=gates)
            negs = sb("negs", [GATE_ROWS, SEQ], where=gates)
            u_m = sb("u_m", [GATE_ROWS, 2, SEQ], where=gates)
            shift = sb("shift", [GATE_ROWS, SEQ], where=gates)
            wi_em = sb("wi_em", [GATE_ROWS, 2, SEQ], where=gates)
            m_prev = sb("m_prev", [GATE_ROWS, CHUNKS], where=gates)
        with ExitStack() as mid:
            sb("fox_V", [P, TT, FOX_WIDTH], where=mid)
            QA = sb("QA", [FOX_DIM + 2, 2, SEQ], where=mid)
            KA = sb("KA", [FOX_DIM + 2, 2, SEQ], where=mid)
            Y = sb("Y", [P, TT, FOX_WIDTH], where=mid)
            YB = sb("YB", [P, ML_HEADS, SEQ], where=mid)
        with ExitStack() as mlp:
            chunk1 = chunk_buffers(1, mlp)
            state = sb("state", [P, ML_HEADS, ML_DIM + 1], where=mlp)
            HN = sb("HN", [P, ML_WIDTH], where=mlp)
        with ExitStack() as late:
            X = sb("X", [P, TT, D_MODEL], where=late)
            scale = sb("scale", [P, TT, P], where=late)
            dump = sb("dump", [P, 4, D_MODEL], where=late)

        big = ctx.enter_context(nc.sbuf_tensor("big_region", [P, 2 * TT * D_MODEL], F32))
        with ExitStack() as fox:
            stage = sb("stage", [P, 2, SEQ], where=fox)
            sq = sb("sq", [P, HALF], where=fox)
            root = sb("root", [P, HALF], where=fox)
            prob = sb("prob", [P, 2, SEQ], where=fox)
            probT = sb("probT", [P, TT, P], where=fox)
            qk_raw = sb("qk_raw", [P, 2, SEQ], where=fox)
            conv_in = sb("conv_in", [P, TAPS - 1 + SEQ], where=fox)
            conv_acc = sb("conv_acc", [P, SEQ], where=fox)
        with ExitStack() as mlt:
            sb("ml_stage_", [P, 2, SEQ], where=mlt)
            decay = sb("decay", [P, ML_HEADS, CHUNK], where=mlt)
            qs = sb("qs", [P, ML_HEADS, CHUNK], where=mlt)
            sw = sb("sw", [P, ML_HEADS, CHUNK], where=mlt)
            kw = sb("kw", [P, ML_HEADS, ML_DIM], where=mlt)
            hb = sb("hb", [P, ML_HEADS, ML_DIM], where=mlt)
            hsq = sb("hsq", [P, ML_HEADS, ML_DIM], where=mlt)
            sb("ml_probT_", [P, TT, P], where=mlt)
            chunk0 = chunk_buffers(0, mlt)
        with ExitStack() as fin:
            A_hi = sb("A_hi", [P, 3, SEQ], F32R, where=fin)
            A_lo = sb("A_lo", [P, 3, SEQ], F32R, where=fin)
            sg = sb("sg", [P, 2, SEQ], where=fin)
        qc, kc, vc, m_rows, oc = zip(chunk0, chunk1)

        PS = ctx.enter_context(nc.psum_tensor("PS", [P, 8, HALF], F32))

        def score_row(s):
            bank = 2 + 2 * (s % 2)
            return PS[:, bank:bank + 2, :].rearrange("p b n -> p (b n)")[:, 0:(s // 2 + 1) * P]

        x_in = [sem(f"x_in{t}") for t in range(TT)]
        gains_in = sem("gains_in")
        const_in = sem("const_in")
        table_in = sem("table_in")
        const_set = sem("const_set")
        cols_set = sem("cols_set")
        gate_zero = sem("gate_zero")
        gate_raw = sem("gate_raw")
        w_raw = [sem(f"w_raw{s}") for s in range(RING)]
        w_first = sem("w_first")
        w_hi = sem("w_hi")
        w_lo = sem("w_lo")
        w_used = sem("w_used")
        sumsq = sem("sumsq")
        rooted = sem("rooted")
        scaled = sem("scaled")
        turned = sem("turned")
        act_hi = sem("act_hi")
        act_lo = sem("act_lo")
        gate_mm = sem("gate_mm")
        gate_v = sem("gate_v")
        gate_a = sem("gate_a")
        gate_turn = sem("gate_turn")
        gate_out = sem("gate_out")
        rows_out = sem("rows_out")
        val_mm = sem("val_mm")
        val_out = sem("val_out")
        tile_mm = sem("tile_mm")
        tile_out = sem("tile_out")
        sq_set = sem("sq_set")
        mean_mm = sem("mean_mm")
        root_set = sem("root_set")
        inv_set = sem("inv_set")
        qk_set = sem("qk_set")
        ones_set = sem("ones_set")
        c_in = [sem("cq_in"), sem("ck_in")]
        score_mm = sem("score_mm")
        nmax_set = sem("nmax_set")
        prob_set = sem("prob_set")
        prob_turn = sem("prob_turn")
        probT_set = [sem("probT_set0"), sem("probT_set1")]
        y_mm = sem("y_mm")
        rinv_set = sem("rinv_set")
        y_set = sem("y_set")
        conv_step = sem("conv_step")
        tanh_set = sem("tanh_set")
        conv_mul = sem("conv_mul")
        tile_set = sem("tile_set")
        stored = [sem("stored0"), sem("stored1")]
        chunk_in = [[sem(f"{n}_in{b}") for b in range(2)] for n in ("qc", "kc", "vc", "mc", "wc", "oc")]
        kq_mm = sem("kq_mm")
        num_mm = sem("num_mm")
        state_mm = sem("state_mm")
        ml_v = sem("ml_v")
        decay_set = sem("decay_set")
        ml_root = sem("ml_root")
        flip_mm = sem("flip_mm")
        g_in = [sem("ga_in"), sem("gb_in")]
        sg_set = sem("sg_set")
        br_mm = sem("br_mm")
        mix_v = sem("mix_v")
        a_hi = sem("a_hi")
        a_lo = sem("a_lo")
        down_mm = sem("down_mm")
        x_add = sem("x_add")
        gu_mm = sem("gu_mm")
        tanh_g = sem("tanh_g")
        glu_a = sem("glu_a")
        glu_b = sem("glu_b")
        out_in = sem("out_in")
        transfer_due = sem("transfer_due")

        def w_tile(parts, slot):
            return parts[:, slot, :].rearrange("p (k n) -> p k n", k=KT)

        def hi_lo(product, hi_a, lo_a, hi_b, lo_b, first, last):
            product(hi_a, hi_b, first, False)
            product(hi_a, lo_b, False, False)
            return product(lo_a, hi_b, False, last)

        block = ctx.enter_context(nc.Block())

        @block.tensor
        def _(pe):
            def product(dst):
                return lambda a, b, start, stop: pe.matmul(dst, a, b, start=start, stop=stop)

            def dense(bank, slot, half, a, b):
                tokens = slice(half * HALF, (half + 1) * HALF)
                hi, lo = w_tile(W_hi, slot), w_tile(W_lo, slot)
                for n in range(a, b):
                    k, part = divmod(n, 3)
                    w = (hi, hi, lo)[part][:, k, :]
                    act = (actT_hi, actT_lo, actT_hi)[part][:, k, tokens]
                    last = pe.matmul(PS[:, bank, :], w, act, start=n == 0, stop=n == 23)
                return last

            def norm_turn(round_, h, tiles, src, scales):
                for k in tiles:
                    if k >= 4:
                        pe.wait_ge(act_lo, 4 * KT * round_ + h * KT + k - 3)
                    for j in range(4):
                        t = 4 * h + j
                        last = pe.matmul(PS[:, 4 * h + k % 4, j * P:(j + 1) * P], src[:, t, k * P:(k + 1) * P],
                                         scales[:, t, :], start=True, stop=True)
                    last.then_inc(turned, 1)

            pe.wait_ge(scaled, 5)
            norm_turn(0, 0, range(KT), X0, scale0)
            pe.wait_ge(scaled, 10)
            norm_turn(0, 1, range(4), X0, scale0)
            pe.wait_ge(act_lo, KT)
            pe.wait_ge(w_lo, 1)
            dense(0, 0, 0, 0, 24).then_inc(gate_mm, 1)
            norm_turn(0, 1, range(4, KT), X0, scale0)
            pe.wait_ge(act_lo, 2 * KT)
            dense(1, 0, 1, 0, 24).then_inc(gate_mm, 1)

            def gates_turn():
                pe.wait_ge(gate_a, 6)
                pe.wait_ge(val_out, TT)
                rows = slice(ROW_FB, ROW_FB + ML_HEADS)
                for kind, src in enumerate((u_m[rows, 0, :], wi_em[rows, 1, :])):
                    for c in range(CHUNKS):
                        at = (kind * CHUNKS + c) * ML_HEADS
                        last = pe.transpose(PS[:, 7, at:at + ML_HEADS], src[:, c * CHUNK:(c + 1) * CHUNK],
                                            ident[rows, rows])
                last.then_inc(gate_turn, 1)

            for b in range(2):
                for u in range(4):
                    n = U_VALUES + 4 * b + u
                    slot = n % RING
                    pe.wait_ge(w_lo, n + 1)
                    for t in range(TT):
                        if u == 0 and b == 0 and t < 2:
                            pe.wait_ge(gate_v, 2)
                        if u == 0 and b == 1:
                            if t == 5:
                                gates_turn()
                            if t == 7:
                                pe.wait_ge(gate_out, 2)
                            pe.wait_ge(val_out, t + 1)
                        for i in range(2):
                            k = 2 * u + i
                            tok = slice(t * P, (t + 1) * P)
                            cols = slice(i * 512, (i + 1) * 512)
                            last = hi_lo(product(PS[:, t, :]), actT_hi[:, k, tok], actT_lo[:, k, tok],
                                         W_hi[:, slot, cols], W_lo[:, slot, cols], k == 0, k == KT - 1)
                        if u == 3:
                            last.then_inc(val_mm, 1)
                    if u < 3:
                        last.then_inc(w_used, 1)

            pe.wait_ge(val_mm, 2 * TT)
            pe.sem_inc(tile_mm, 2)

            pe.wait_ge(val_out, TT + 2)
            pe.sem_inc(score_mm, 1)
            with pe.Fori(0, PAIRS) as p:
                for step in fox_steps:
                    kind, *at = step
                    if kind == "unit":
                        j, = at
                        pe.wait_ge(w_lo, U_FOX + FOX_UNITS * p + j + 1)
                    elif kind == "dense":
                        j, h, a, b = at
                        if a == 0:
                            pe.wait_ge(tile_out, 2 * FOX_UNITS * p + 2 * j + h + 1)
                        last = dense(h, j % RING, h, a, b)
                        if b == 24:
                            last.then_inc(tile_mm, 1)
                    elif kind == "norm":
                        q_or_k, h = at
                        pe.wait_ge(val_out, 2 * TT)
                        pe.wait_ge(sq_set, 4 * p + 2 * q_or_k + h + 1)
                        pe.matmul(PS[:, 2 + 2 * q_or_k + h, :], head_mean[:], sq[:], start=True,
                                  stop=True).then_inc(mean_mm, 1)
                    elif kind == "scores":
                        s, = at
                        i, hd = divmod(s, 2)
                        length = (i + 1) * P
                        if s == 0:
                            pe.wait_ge(qk_set, 8 * p + 8)
                            pe.wait_ge(c_in[0], 16 * (p + 1))
                            pe.wait_ge(c_in[1], 16 * (p + 1))
                        if s >= 2:
                            pe.wait_ge(prob_set, 2 * TT * p + s - 1)
                        query = QA[:, hd, i * P:(i + 1) * P]
                        bank = 2 + 2 * (s % 2)
                        for part in range(0, length, HALF):
                            n = min(HALF, length - part)
                            diagonal = part + n == length
                            last = pe.matmul(PS[:, bank + part // HALF, 0:n], query, KA[:, hd, part:part + n],
                                             start=True, stop=not diagonal)
                            if diagonal:
                                last = pe.matmul(PS[:, bank + part // HALF, n - P:n], ident_bf[:], mask_bf[:],
                                                 start=False, stop=True)
                        last.then_inc(score_mm, 1)
                    elif kind == "turn":
                        s, part = at
                        if part == 0:
                            pe.wait_ge(prob_set, 2 * TT * p + s + 1)
                        if part:
                            pe.wait_ge(probT_set[0], 2 * TT * p + s + 1)
                        elif s > 8:
                            pe.wait_ge(probT_set[1], TT * p + s - 8)
                        elif s:
                            pe.wait_ge(probT_set[0], 2 * TT * p + s)
                        for b in range(4 * part, min(4 * part + 4, s // 2 + 1)):
                            last = pe.transpose(PS[:, 6, (b % 4) * P:(b % 4 + 1) * P],
                                                prob[:, s % 2, b * P:(b + 1) * P], ident[:])
                        last.then_inc(prob_turn, 1)
                    elif kind == "values":
                        s, = at
                        i, hd = divmod(s, 2)
                        pe.wait_ge(probT_set[0], 2 * TT * p + s + 1)
                        if i >= 4:
                            pe.wait_ge(probT_set[1], TT * p + s - 7)
                        if s:
                            pe.wait_ge(y_set, 2 * TT * p + s)
                        for b in range(i + 1):
                            head = bass.ds(p * P + hd * FOX_DIM, FOX_DIM)
                            last = pe.matmul(PS[:, 7, 0:FOX_DIM], probT[:, b, :], V[:, b, head],
                                             start=b == 0, stop=b == i)
                        last.then_inc(y_mm, 1)

            pe.wait_ge(ml_v, ML_SETUP)
            with pe.Fori(0, ML_STEPS) as q:
                for step in ml_steps:
                    kind, *at = step
                    if kind == "unit":
                        j, = at
                        pe.wait_ge(w_lo, U_ML + ML_UNITS * q + j + 1)
                    elif kind == "dense":
                        j, h, a, b = at
                        done = 2 * FOX_UNITS * PAIRS + 2 * ML_UNITS * q + 2 * j + h
                        if a == 0:
                            pe.wait_ge(tile_out, done + 1)
                        last = dense(h, j % RING, h, a, b)
                        if b == 24:
                            last.then_inc(tile_mm, 1)
                    elif kind == "kq":
                        c, = at
                        if c == 0:
                            pe.wait_ge(ml_v, ML_SETUP + ML_V_STEPS * q)
                        for which in (0, 1):
                            pe.wait_ge(chunk_in[which][c], 16 * (q + 1))
                        for h in range(ML_HEADS):
                            pe.transpose(PS[:, 6, h * P:(h + 1) * P], kc[c][:, h, :], ident[:])
                        for h in range(ML_HEADS):
                            last = pe.matmul(PS[:, 2, h * P:(h + 1) * P], kc[c][:, h, :], qc[c][:, h, :],
                                             start=True, stop=True)
                        last.then_inc(kq_mm, 1)
                    elif kind == "num":
                        c, = at
                        pe.wait_ge(chunk_in[2][c], 16 * (q + 1))
                        pe.wait_ge(ml_v, ml_at(q, "kq", c, 4))
                        for h in range(ML_HEADS):
                            dst = PS[:, 3 + h // 2, (h % 2) * 129:(h % 2 + 1) * 129]
                            pe.matmul(dst, sw[:, h, :], vc[c][:, h, :], start=True, stop=False)
                            last = pe.matmul(dst, qs[:, h, :], state[:, h, :], start=False, stop=True)
                        last.then_inc(num_mm, 1)
                    elif kind == "state":
                        c, = at
                        pe.wait_ge(ml_v, ml_at(q, "kq", c, 5))
                        for h in range(ML_HEADS):
                            dst = PS[:, (5, 7)[h // 2], (h % 2) * 129:(h % 2 + 1) * 129]
                            last = pe.matmul(dst, kw[:, h, :], vc[c][:, h, :], start=True, stop=True)
                        last.then_inc(state_mm, 1)
                    elif kind == "flip":
                        c, = at
                        pe.wait_ge(ml_v, ml_at(q, "out", c, 7))
                        for h in range(ML_HEADS):
                            last = pe.transpose(PS[:, 6, h * P:(h + 1) * P], HN[:, h * P:(h + 1) * P], ident[:])
                        last.then_inc(flip_mm, 1)

            def turn_y(pieces):
                for n in pieces:
                    h, k = divmod(n, PAIRS)
                    if n >= 6:
                        pe.wait_ge(act_lo, 2 * KT + n - 5)
                    for j in range(4):
                        last = pe.transpose(PS[:, Y_BANKS[n], j * P:(j + 1) * P],
                                            Y[:, 4 * h + j, k * P:(k + 1) * P], ident[:])
                    last.then_inc(turned, 1)

            pe.wait_ge(ml_v, ml_at(ML_STEPS - 1, "state", 1, 4))
            pe.wait_ge(ml_v, ml_at(ML_STEPS - 1, "flip", 1, 1))
            turn_y(range(6))

            def down(slot, a_slot, tile, groups):
                for g in groups:
                    t, c = divmod(g, 2)
                    pe.wait_ge(x_add, X_START + 16 * tile + g - 3)
                    tok, cols = slice(t * P, (t + 1) * P), slice(c * 512, (c + 1) * 512)
                    last = hi_lo(product(PS[:, 4 + g % 4, :]), A_hi[:, a_slot, tok], A_lo[:, a_slot, tok],
                                 W_hi[:, slot, cols], W_lo[:, slot, cols], True, True)
                    last.then_inc(down_mm, 1)

            def ready(n, tile):
                pe.wait_ge(w_lo, n + 1)
                pe.wait_ge(a_lo, 2 * (tile + 1))

            def branches(m, n, slot, down_unit, down_slot, a_slot):
                pe.wait_ge(w_lo, n + 1)
                hi, lo = w_tile(W_hi, slot), w_tile(W_lo, slot)
                for b in range(2):
                    if b:
                        ready(down_unit, m - 1)
                    for h in range(2):
                        tokens = slice(h * HALF, (h + 1) * HALF)
                        pe.wait_ge(mix_v, 6 * (m - 1) + (1, 2, 3, 5)[2 * b + h])
                        for i in range(4):
                            k = 4 * b + i
                            last = hi_lo(product(PS[:, 2 * b + h, :]), hi[:, k, :], lo[:, k, :],
                                         actT_hi[:, k, tokens], actT_lo[:, k, tokens], i == 0, i == 3)
                            if i == 3:
                                last.then_inc(br_mm, 1)
                            if b:
                                g = 8 * h + 2 * i
                                down(down_slot, a_slot, m - 1, (g, g + 1))

            pe.wait_ge(w_lo, U_MERGE + 1)
            pe.wait_ge(tile_out, 2 + 2 * (U_MERGE - U_FOX))
            hi, lo = w_tile(W_hi, 0), w_tile(W_lo, 0)
            for b in range(2):
                for h in range(2):
                    tokens = slice(h * HALF, (h + 1) * HALF)
                    for i in range(4):
                        k = 4 * b + i
                        pe.wait_ge(act_lo, 2 * KT + 8 * b + 4 * h + i + 1)
                        last = hi_lo(product(PS[:, 2 * b + h, :]), hi[:, k, :], lo[:, k, :],
                                     actT_hi[:, k, tokens], actT_lo[:, k, tokens], i == 0, i == 3)
                    last.then_inc(br_mm, 1)
                    if b == 0 and h == 0:
                        turn_y((6, 7))
            pe.wait_ge(br_mm, 4)
            pe.sem_inc(down_mm, DOWN_START)
            with pe.Fori(0, 2) as r:
                for i in range(3):
                    n = U_MERGE + 2 * i + 1
                    branches(3 * r + i + 1, n + 6 * r, n % RING, n + 6 * r + 1, (n + 1) % RING, i)
            n = U_MERGE + 13
            branches(KT - 1, n, n % RING, n + 1, (n + 1) % RING, 0)
            ready(n + 2, KT - 1)
            down((n + 2) % RING, 1, KT - 1, range(12))
            pe.wait_ge(scaled, 15)
            pe.wait_ge(mix_v, 6 * KT)
            norm_turn(1, 0, range(4), X, scale)
            down((n + 2) % RING, 1, KT - 1, range(12, 16))
            norm_turn(1, 0, range(4, KT), X, scale)
            pe.wait_ge(scaled, 20)
            norm_turn(1, 1, range(4), X, scale)

            def gate_up(m, n, slot, a_slot):
                for b in range(2):
                    pe.wait_ge(w_lo, n + b + 1)
                    if b:
                        ready(n + 2, KT + m - 1)
                    for h in range(2):
                        pe.wait_ge((glu_a, glu_b)[b], 2 * m + h - 1)
                        for i in range(KT):
                            last = dense(2 * b + h, (slot + b) % RING, h, 3 * i, 3 * i + 3)
                            if i == KT - 1:
                                last.then_inc(gu_mm, 1)
                            if b:
                                down((slot + 2) % RING, a_slot, KT + m - 1, (8 * h + i,))

            pe.wait_ge(act_lo, 5 * KT)
            pe.wait_ge(w_lo, U_FFN + 1)
            dense(0, U_FFN % RING, 0, 0, 24).then_inc(gu_mm, 1)
            norm_turn(1, 1, range(4, KT), X, scale)
            pe.wait_ge(act_lo, 6 * KT)
            dense(1, U_FFN % RING, 1, 0, 24).then_inc(gu_mm, 1)
            pe.wait_ge(w_lo, U_FFN + 2)
            for h in range(2):
                dense(2 + h, (U_FFN + 1) % RING, h, 0, 24).then_inc(gu_mm, 1)
            with pe.Fori(0, FT // 2 - 1) as r:
                for i in range(2):
                    n = U_FFN + 3 * i + 2
                    gate_up(2 * r + i + 1, n + 6 * r, n % RING, i)
            n = U_FFN + 3 * (FT - 2) + 2
            gate_up(FT - 1, n, n % RING, 0)
            ready(n + 3, KT + FT - 1)
            down((n + 3) % RING, 1, KT + FT - 1, range(16))

        @block.scalar
        def _(act):
            def split(n, rounds=0):
                slot = n % RING
                act.wait_ge(w_raw[slot], 16 * raw_count(n, rounds))
                act.activation(W_hi[:, slot, :], W_raw[:, slot, :], ACT.Copy).then_inc(w_hi, 1)

            def squares(round_, tiles, arrived, src, dst):
                for t in tiles:
                    arrived(t)
                    if t >= 4:
                        act.wait_ge(sumsq, TT * round_ + t - 3)
                    act.activation(dst[:, t % 4, :], src[:, t, :], ACT.Square,
                                   accum_out=stat[:, 0, t:t + 1]).then_inc(sumsq, 1)
                    if t % 4 == 3:
                        act.wait_ge(sumsq, TT * round_ + t + 1)
                        act.activation(stat[:, 1, t - 3:t + 1], stat[:, 0, t - 3:t + 1], ACT.Sqrt,
                                       bias=eps_col[:], scale=1.0 / D_MODEL).then_inc(rooted, 1)

            def norm_hi(round_, h, tiles):
                for k in tiles:
                    act.wait_ge(turned, 3 * KT * round_ + h * KT + k + 1)
                    act.activation(actT_hi[:, k, h * HALF:(h + 1) * HALF], PS[:, 4 * h + k % 4, :], ACT.Copy,
                                   scale=g_cols[:, round_, k:k + 1]).then_inc(act_hi, 1)

            act.wait_ge(cols_set, 1)
            act.activation(stat[:, 1, 0:1], eps_col[:], ACT.Sqrt).then_inc(table_in, 1)
            act.wait_ge(table_in, 1)
            squares(0, range(TT), lambda t: act.wait_ge(x_in[t], 16), X0, dump0)
            act.wait_ge(gate_raw, 48)
            act.activation(W_hi[:, 0, :], W_raw[:, 0, :], ACT.Copy).then_inc(w_hi, 1)
            act.wait_ge(gains_in, 32)
            norm_hi(0, 0, range(KT))
            split(1)
            norm_hi(0, 1, range(KT))
            split(2)

            rows = slice(ROW_FB, ROW_FB + ML_HEADS)
            act.wait_ge(gate_v, 2)
            act.activation(u_m[rows, 0, :], z[ROW_IB:ROW_IB + ML_HEADS, :], ACT.Copy).then_inc(gate_a, 1)
            act.activation(soft[:], z[:], ACT.Abs).then_inc(gate_a, 1)
            act.wait_ge(gate_a, 2)
            act.activation(soft[:], soft[:], ACT.Exp, scale=-1.0).then_inc(gate_a, 1)
            act.wait_ge(gate_a, 3)
            act.activation(soft[:], soft[:], ACT.Ln, bias=1.0).then_inc(gate_a, 1)
            act.wait_ge(gate_mm, 2)
            split(3)
            act.wait_ge(gate_v, 17)
            act.activation(wi_em[rows, 0, :], wi_em[rows, 0, :], ACT.Exp).then_inc(gate_a, 1)
            act.activation(wi_em[rows, 1, :], wi_em[rows, 1, :], ACT.Exp, scale=-1.0).then_inc(gate_a, 1)

            act.sem_inc(tile_out, 2)
            for n in (4, 5, 6):
                act.wait_ge(w_used, n - 3)
                split(n)
            for t in range(TT):
                act.wait_ge(val_mm, t + 1)
                act.activation(V[:, t, :], PS[:, t, :], ACT.Copy).then_inc(val_out, 1)
            split(7)
            for n in (8, 9, 10):
                act.wait_ge(w_used, n - 4)
                split(n)
            for t in range(TT):
                act.wait_ge(val_mm, TT + t + 1)
                if t >= 2:
                    act.wait_ge(stored[t % 2], 16 * (t // 2))
                act.activation(stage[:, t % 2, 0:ML_WIDTH], PS[:, t, :], ACT.Copy).then_inc(val_out, 1)

            with act.Fori(0, PAIRS) as p:
                for step in fox_steps:
                    kind, *at = step
                    if kind == "unit":
                        j, = at
                        act.wait_ge(tile_mm, 2 + 2 * FOX_UNITS * p + 2 * j)
                        split(U_FOX + j + 2, FOX_UNITS // RING * p)
                    elif kind == "half":
                        j, h = at
                        n = 2 * FOX_UNITS * p + 2 * j + h
                        tokens = slice(h * HALF, (h + 1) * HALF)
                        if j < 2:
                            if j or h:
                                act.wait_ge(mean_mm, 4 * p + 2 * j + h)
                            act.wait_ge(tile_mm, n + 3)
                            act.activation(sq[:], PS[:, h, :], ACT.Square).then_inc(sq_set, 1)
                            act.activation(qk_raw[:, j, tokens], PS[:, h, :], ACT.Copy).then_inc(tile_out, 1)
                        elif j < 4:
                            if j == 3 and h == 0:
                                act.wait_ge(conv_step, 8 * p + 4)
                            act.wait_ge(tile_mm, n + 3)
                            act.activation(conv_in[:, TAPS - 1 + h * HALF:TAPS - 1 + (h + 1) * HALF],
                                           PS[:, h, :], ACT.Copy).then_inc(tile_out, 1)
                        else:
                            if h == 0:
                                act.wait_ge(stored[j % 2], 16 * (4 + 2 * p + 1))
                            act.wait_ge(tile_mm, n + 3)
                            act.activation(stage[:, j % 2, tokens], PS[:, h, :], ACT.Tanh,
                                           scale=0.5).then_inc(tile_out, 1)
                    elif kind == "norm":
                        x_, h = at
                        if x_ or h:
                            act.wait_ge(qk_set, 8 * p + 2 * (2 * x_ + h))
                        act.wait_ge(mean_mm, 4 * p + 2 * x_ + h + 1)
                        act.activation(root[:], PS[:, 2 + 2 * x_ + h, :], ACT.Sqrt,
                                       bias=eps_col[:]).then_inc(root_set, 1)
                    elif kind == "silu":
                        j, = at
                        act.wait_ge(stored[j % 2], 16 * (4 + 2 * p))
                        act.wait_ge(conv_step, 4 * (2 * p + j - 2) + 4)
                        act.activation(stage[:, j % 2, :], conv_acc[:], ACT.Tanh, scale=0.5).then_inc(tanh_set, 1)
                    elif kind == "turn" and at[1] == 0:
                        s = at[0]
                        n = min(4, s // 2 + 1)
                        if s:
                            act.wait_ge(y_mm, 2 * TT * p + s)
                        act.wait_ge(prob_turn, FILLS * p + turn_fill(s, 0) + 1)
                        act.activation(probT[:, 0:n, :].rearrange("p b q -> p (b q)"), PS[:, 6, 0:n * P],
                                       ACT.Copy).then_inc(probT_set[0], 1)
                    elif kind == "exp":
                        s, = at
                        length = (s // 2 + 1) * P
                        if s >= 2:
                            act.wait_ge(prob_turn, FILLS * p + turn_fill(s - 2, int((s - 2) // 2 >= 4)) + 1)
                            act.wait_ge(rinv_set, 2 * TT * p + s - 1)
                        act.wait_ge(nmax_set, 2 * TT * p + s + 1)
                        act.activation(prob[:, s % 2, 0:length], score_row(s), ACT.Exp, bias=nmax[:, s % 2:s % 2 + 1],
                                       accum_out=psumrow[:, s % 2:s % 2 + 1]).then_inc(prob_set, 1)

            with act.Fori(0, ML_STEPS) as q:
                for step in ml_steps:
                    kind, *at = step
                    if kind == "unit":
                        j, = at
                        act.wait_ge(tile_mm, 2 + 2 * FOX_UNITS * PAIRS + 2 * ML_UNITS * q + 2 * j)
                        split(U_ML + j + 2, ML_UNITS // RING * q)
                    elif kind == "half":
                        j, h = at
                        n = 2 * FOX_UNITS * PAIRS + 2 * ML_UNITS * q + 2 * j + h
                        if h == 0:
                            act.wait_ge(stored[j % 2], 16 * ml_stores(q, j))
                        act.wait_ge(tile_mm, n + 3)
                        act.activation(stage[:, j % 2, h * HALF:(h + 1) * HALF], PS[:, h, :], ACT.Tanh,
                                       scale=0.5).then_inc(tile_out, 1)
                    elif kind == "kq":
                        c, = at
                        act.wait_ge(ml_v, ml_at(q, "kq", c, 2))
                        act.activation(decay[:], decay[:], ACT.Exp).then_inc(decay_set, 1)
                    elif kind == "out":
                        c, = at
                        act.wait_ge(ml_v, ml_at(q, "out", c, 5))
                        act.activation(hstat[:, 4, :], hstat[:, 3, :], ACT.Sqrt, bias=eps_col[:],
                                       scale=1.0 / ML_DIM).then_inc(ml_root, 1)

            for b in range(2):
                for h in range(2):
                    for i in range(4):
                        n = 4 * h + i
                        if b == 0:
                            act.wait_ge(turned, 2 * KT + n + 1)
                            src = PS[:, Y_BANKS[n], :]
                        else:
                            src = YB[:, i, h * HALF:(h + 1) * HALF]
                        act.activation(actT_hi[:, 4 * b + i, h * HALF:(h + 1) * HALF], src,
                                       ACT.Copy).then_inc(act_hi, 1)
                if b == 0:
                    act.wait_ge(tile_mm, 2 + 2 * (U_MERGE - U_FOX))
                    split(U_MERGE + 2)
                    act.wait_ge(ml_v, ML_SETUP + ML_STEPS * ML_V_STEPS)

            def merge_hi(m, a_slot, h):
                act.wait_ge(mix_v, 6 * m + 4 + 2 * h)
                act.activation(A_hi[:, a_slot, h * HALF:(h + 1) * HALF], sg[:, 0, h * HALF:(h + 1) * HALF],
                               ACT.Copy).then_inc(a_hi, 1)

            act.wait_ge(stored[0], 16 * ml_stores(ML_STEPS, 0))
            act.wait_ge(stored[1], 16 * ml_stores(ML_STEPS, 1))
            merge_hi(0, 0, 0)
            merge_hi(0, 0, 1)
            with act.Fori(0, 2) as r:
                for i in range(3):
                    m = 3 * r + i + 1
                    act.wait_ge(down_mm, DOWN_START + 16 * (m - 1))
                    split(U_MERGE + 2 * i + 3, 2 * r)
                    merge_hi(m, (i + 1) % 3, 0)
                    act.wait_ge(br_mm, 4 * (m + 1))
                    split(U_MERGE + 2 * i + 4, 2 * r)
                    merge_hi(m, (i + 1) % 3, 1)
            act.wait_ge(down_mm, DOWN_START + 16 * (KT - 2))
            split(U_MERGE + 15)
            merge_hi(KT - 1, 1, 0)
            act.wait_ge(br_mm, 4 * KT)
            split(U_FFN)
            merge_hi(KT - 1, 1, 1)
            act.wait_ge(down_mm, DOWN_START + 16 * (KT - 1))
            split(U_FFN + 1)

            def added(t):
                act.wait_ge(x_add, X_START + 16 * (KT - 1) + 2 * t + 2)

            squares(1, range(6), added, X, dump)
            norm_hi(1, 0, range(4))
            squares(1, range(6, TT), added, X, dump)
            norm_hi(1, 0, range(4, KT))
            norm_hi(1, 1, range(KT))

            def gate_tanh(m, h):
                act.wait_ge(gu_mm, 4 * m + h + 1)
                act.activation(sg[:, 0, h * HALF:(h + 1) * HALF], PS[:, h, :], ACT.Tanh,
                               scale=0.5).then_inc(tanh_g, 1)

            def glu_hi(m, h, a_slot):
                act.wait_ge(glu_b, 2 * m + h + 1)
                act.activation(A_hi[:, a_slot, h * HALF:(h + 1) * HALF], sg[:, 1, h * HALF:(h + 1) * HALF],
                               ACT.Copy).then_inc(a_hi, 1)

            act.wait_ge(down_mm, DOWN_START + 16 * KT)
            split(U_FFN + 2)
            for h in range(2):
                gate_tanh(0, h)
            for h in range(2):
                glu_hi(0, h, 0)

            def ffn_tile(m, n, rounds, a_slot):
                act.wait_ge(gu_mm, 4 * m)
                split(n + 1, rounds)
                act.wait_ge(down_mm, DOWN_START + 16 * (KT + m - 1))
                split(n + 2, rounds)
                for h in range(2):
                    gate_tanh(m, h)
                act.wait_ge(gu_mm, 4 * m + 2)
                split(n + 3, rounds)
                for h in range(2):
                    glu_hi(m, h, a_slot)

            with act.Fori(0, FT // 2 - 1) as r:
                for i in range(2):
                    at = 3 * i + 2
                    ffn_tile(2 * r + i + 1, U_FFN + at, 2 * r, (i + 1) % 2)
            at = U_FFN + 3 * (FT - 2) + 2
            ffn_tile(FT - 1, at, 0, 1)

        @block.vector
        def _(dve):
            def split(n, rounds=0):
                slot = n % RING
                dve.wait_ge(w_hi, n + RING * rounds + 1)
                dve.tensor_tensor(W_lo[:, slot, :], W_raw[:, slot, :], W_hi[:, slot, :].bitcast(F32),
                                  ALU.subtract).then_inc(w_lo, 1)

            def scale_diagonals(round_, h, scales):
                dve.wait_ge(rooted, 2 * round_ + h + 1)
                dve.reciprocal(stat[:, 2, 4 * h:4 * h + 4], stat[:, 1, 4 * h:4 * h + 4]).then_inc(scaled, 1)
                dve.wait_ge(scaled, 10 * round_ + 5 * h + 1)
                for t in range(4 * h, 4 * h + 4):
                    dve.tensor_scalar(scales[:, t, :], ident[:], stat[:, 2, t:t + 1], None,
                                      ALU.mult).then_inc(scaled, 1)

            def norm_lo(round_, h, tiles):
                for k in tiles:
                    tokens = slice(h * HALF, (h + 1) * HALF)
                    dve.wait_ge(act_hi, 4 * KT * round_ + h * KT + k + 1)
                    dve.scalar_tensor_tensor(actT_lo[:, k, tokens], PS[:, 4 * h + k % 4, :],
                                             g_cols[:, round_, k:k + 1], actT_hi[:, k, tokens].bitcast(F32),
                                             ALU.mult, ALU.subtract).then_inc(act_lo, 1)

            dve.memset(eps_col[:], EPS).then_inc(cols_set, 1)
            dve.memset(conv_in[:, 0:TAPS - 1], 0.0).then_inc(cols_set, 1)
            dve.memset(head_mean[:], 0.0).then_inc(cols_set, 1)
            dve.wait_ge(cols_set, 3)
            for hd in range(2):
                at = slice(hd * FOX_DIM, (hd + 1) * FOX_DIM)
                dve.memset(head_mean[at, at], 1.0 / FOX_DIM).then_inc(cols_set, 1)

            dve.wait_ge(const_set, 8)
            scale_diagonals(0, 0, scale0)
            scale_diagonals(0, 1, scale0)
            dve.wait_ge(w_hi, 1)
            dve.tensor_tensor(W_lo[:, 0, :], W_raw[:, 0, :], W_hi[:, 0, :].bitcast(F32),
                              ALU.subtract).then_inc(w_lo, 1)
            norm_lo(0, 0, range(KT))
            norm_lo(0, 1, range(KT))
            split(1)
            dve.wait_ge(const_in, 16 * N_CONST)
            dve.tensor_scalar(g_qk[:, 0:1], g_qk[:, 0:1], FOX_DIM ** -0.5, None, ALU.mult).then_inc(cols_set, 1)
            dve.tensor_scalar(g_ml[:], g_ml[:], 0.5, None, ALU.mult).then_inc(cols_set, 1)

            ml = slice(ROW_FB, ROW_FB + ML_HEADS)
            fx = slice(ROW_FA, ROW_FA + FOX_HEADS)
            for h in range(2):
                dve.wait_ge(gate_mm, h + 1)
                dve.tensor_scalar(z[:, h * HALF:(h + 1) * HALF], PS[0:GATE_ROWS, h, :], gate_bias[:], None,
                                  ALU.add).then_inc(gate_v, 1)
            dve.memset(keep[:], 1.0).then_inc(gate_v, 1)
            dve.memset(shift[ml, :], 0.0).then_inc(gate_v, 1)
            dve.memset(m_prev[ml, :], 0.0).then_inc(gate_v, 1)
            dve.wait_ge(gate_v, 3)
            starts = keep[ml, :].rearrange("p (c t) -> p c t", t=CHUNK)[:, :, 0:1]
            dve.memset(starts, 0.0).then_inc(gate_v, 1)
            split(2)
            split(3)
            dve.wait_ge(gate_a, 4)
            dve.scalar_tensor_tensor(logs[:], z[:], 0.0, soft[:], ALU.min, ALU.subtract).then_inc(gate_v, 1)
            dve.wait_ge(gate_v, 7)
            dve.tensor_tensor_scan(csum[fx, :], keep[fx, :], logs[fx, :], 0.0, ALU.mult, ALU.add).then_inc(gate_v, 1)
            dve.tensor_tensor_scan(csum[ml, :], keep[ml, :], logs[ml, :], 0.0, ALU.mult, ALU.add).then_inc(gate_v, 1)
            dve.wait_ge(gate_v, 9)
            dve.tensor_scalar(negs[fx, :], csum[fx, :], -1.0, None, ALU.mult).then_inc(gate_v, 1)
            u_row, m_row = u_m[ml, 0, :], u_m[ml, 1, :]
            dve.tensor_tensor(u_row, u_row, csum[ml, :], ALU.subtract).then_inc(gate_v, 1)

            def ends(row):
                return row.rearrange("p (c t) -> p c t", t=CHUNK)[:, 0:CHUNKS - 1, CHUNK - 1]

            dve.tensor_copy(shift[ml, :].rearrange("p (c t) -> p c t", t=CHUNK)[:, 1:CHUNKS, 0],
                            ends(csum[ml, :])).then_inc(gate_v, 1)
            dve.wait_ge(gate_v, 12)
            dve.tensor_tensor_scan(m_row, shift[ml, :], u_row, 0.0, ALU.add, ALU.max).then_inc(gate_v, 1)
            dve.wait_ge(gate_v, 13)
            dve.tensor_tensor(m_prev[ml, 1:CHUNKS], ends(m_row), ends(csum[ml, :]), ALU.add).then_inc(gate_v, 1)
            dve.tensor_scalar(negs[ml, :], m_row, -1.0, None, ALU.mult).then_inc(gate_v, 1)
            dve.wait_ge(gate_v, 14)
            dve.tensor_tensor(wi_em[ml, 0, :].rearrange("p (c t) -> p c t", t=CHUNK),
                              m_prev[ml, :].unsqueeze(2).to_broadcast([ML_HEADS, CHUNKS, CHUNK]),
                              m_row.rearrange("p (c t) -> p c t", t=CHUNK), ALU.subtract).then_inc(gate_v, 1)
            dve.tensor_tensor(wi_em[ml, 1, :], csum[ml, :], m_row, ALU.add).then_inc(gate_v, 1)

            for n in range(4, 8):
                split(n)
            dve.wait_ge(gate_turn, 1)
            cols = CHUNKS * ML_HEADS
            dve.tensor_copy(uT[:].rearrange("p c h -> p (c h)"), PS[:, 7, 0:cols]).then_inc(gate_out, 1)
            dve.tensor_copy(emT[:].rearrange("p c h -> p (c h)"), PS[:, 7, cols:2 * cols]).then_inc(gate_out, 1)
            for n in range(8, 11):
                split(n)
            dve.wait_ge(rows_out, 64)
            dve.memset(QA[FOX_DIM:FOX_DIM + 2, :, :], 1.0).then_inc(ones_set, 1)
            dve.memset(KA[FOX_DIM:FOX_DIM + 2, :, :], 1.0).then_inc(ones_set, 1)

            with dve.Fori(0, PAIRS) as p:
                for step in fox_steps:
                    kind, *at = step
                    if kind == "unit":
                        j, = at
                        split(U_FOX + j + 2, FOX_UNITS // RING * p)
                    elif kind == "half":
                        j, h = at
                        n = 2 * FOX_UNITS * p + 2 * j + h
                        if h == 0 or j < 4:
                            continue
                        dve.wait_ge(tile_out, n + 3)
                        if j == 4:
                            dve.tensor_scalar(stage[:, j % 2, :], stage[:, j % 2, :], 1.0, g_ml[:, bass.ds(p, 1)],
                                              ALU.add, ALU.mult).then_inc(tile_set, 1)
                        else:
                            dve.tensor_scalar(stage[:, j % 2, :], stage[:, j % 2, :], 0.5, 0.5, ALU.mult,
                                              ALU.add).then_inc(tile_set, 1)
                    elif kind == "conv":
                        j, n = at
                        tile = bass.ds(p + (j - 2) * ML_HEADS, 1)
                        tap = TAPS - 1 - n
                        if n == 0:
                            dve.wait_ge(tile_out, 2 * FOX_UNITS * p + 2 * j + 4)
                            dve.tensor_scalar(conv_acc[:], conv_in[:, tap:tap + SEQ], taps[:, tile, tap].opt(),
                                              taps[:, tile, TAPS].opt(), ALU.mult, ALU.add).then_inc(conv_step, 1)
                        else:
                            dve.wait_ge(conv_step, 4 * (2 * p + j - 2) + n)
                            dve.scalar_tensor_tensor(conv_acc[:], conv_in[:, tap:tap + SEQ],
                                                     taps[:, tile, tap].opt(), conv_acc[:], ALU.mult,
                                                     ALU.add).then_inc(conv_step, 1)
                    elif kind == "norm":
                        x_, h = at
                        tokens = slice(h * HALF, (h + 1) * HALF)
                        dst = (QA, KA)[x_]
                        dve.wait_ge(root_set, 4 * p + 2 * x_ + h + 1)
                        dve.reciprocal(root[:], root[:]).then_inc(inv_set, 1)
                        dve.wait_ge(inv_set, 4 * p + 2 * x_ + h + 1)
                        for hd in range(2):
                            rows = slice(hd * FOX_DIM, (hd + 1) * FOX_DIM)
                            dve.scalar_tensor_tensor(dst[0:FOX_DIM, hd, tokens], qk_raw[rows, x_, tokens],
                                                     g_qk[rows, x_:x_ + 1], root[rows, :], ALU.mult,
                                                     ALU.mult).then_inc(qk_set, 1)
                    elif kind == "silu":
                        j, = at
                        n = 2 * p + j - 2
                        dve.wait_ge(tanh_set, n + 1)
                        dve.scalar_tensor_tensor(stage[:, j % 2, :], stage[:, j % 2, :], 1.0, conv_acc[:], ALU.add,
                                                 ALU.mult).then_inc(conv_mul, 1)
                        dve.wait_ge(conv_mul, n + 1)
                        dve.tensor_scalar(stage[:, j % 2, :], stage[:, j % 2, :],
                                          0.5 if j == 2 else 0.5 * ML_DIM ** -0.5, None,
                                          ALU.mult).then_inc(tile_set, 1)
                    elif kind == "scores":
                        s, = at
                        dve.wait_ge(score_mm, 2 * TT * p + s + 2)
                        dve.tensor_reduce(nmax[:, s % 2:s % 2 + 1], score_row(s), AX_X, ALU.max,
                                          negate=True).then_inc(nmax_set, 1)
                    elif kind == "turn":
                        s, part = at
                        n = s // 2 + 1 - 4
                        if part == 0:
                            dve.wait_ge(prob_set, 2 * TT * p + s + 1)
                            dve.reciprocal(rinv[:, s % 2:s % 2 + 1],
                                           psumrow[:, s % 2:s % 2 + 1]).then_inc(rinv_set, 1)
                        else:
                            dve.wait_ge(y_mm, 2 * TT * p + s)
                            dve.wait_ge(prob_turn, FILLS * p + turn_fill(s, 1) + 1)
                            dve.tensor_copy(probT[:, 4:4 + n, :].rearrange("p b q -> p (b q)"),
                                            PS[:, 6, 0:n * P]).then_inc(probT_set[1], 1)
                    elif kind == "values":
                        s, = at
                        i, hd = divmod(s, 2)
                        n = 2 * TT * p + s
                        dve.wait_ge(rinv_set, n + 1)
                        dve.wait_ge(y_mm, n + 1)
                        dve.tensor_scalar(Y[:, i, bass.ds(p * P + hd * FOX_DIM, FOX_DIM)], PS[:, 7, 0:FOX_DIM],
                                          rinv[:, hd:hd + 1], None, ALU.mult).then_inc(y_set, 1)

            for c in range(2):
                dve.memset(vc[c][:, :, ML_DIM:ML_DIM + 1], 1.0).then_inc(ml_v, 1)
            dve.memset(state[:].rearrange("p h n -> p (h n)"), 0.0).then_inc(ml_v, 1)
            with dve.Fori(0, ML_STEPS) as q:
                for step in ml_steps:
                    kind, *at = step
                    if kind == "unit":
                        j, = at
                        split(U_ML + j + 2, ML_UNITS // RING * q)
                        continue
                    if kind == "half":
                        j, h = at
                        if h:
                            dve.wait_ge(tile_out, 2 * FOX_UNITS * PAIRS + 2 * ML_UNITS * q + 2 * j + h + 3)
                            dve.tensor_scalar(stage[:, j % 2, :], stage[:, j % 2, :], 0.5, 0.5, ALU.mult,
                                              ALU.add).then_inc(tile_set, 1)
                        continue
                    if kind == "dense":
                        continue
                    c, = at
                    chunk = bass.ds(2 * q + c, 1)

                    def step_done(n, kind=kind, c=c):
                        dve.wait_ge(ml_v, ml_at(q, kind, c, n))

                    def by_head(cols):
                        return cols.unsqueeze(2).to_broadcast([P, ML_HEADS, CHUNK])

                    if kind == "kq":
                        dve.wait_ge(chunk_in[3][c], 16 * (q + 1))
                        dve.tensor_tensor(decay[:], m_rows[c][:, 0, :, :],
                                          mask_ml[:].unsqueeze(1).to_broadcast([P, ML_HEADS, CHUNK]),
                                          ALU.add).then_inc(ml_v, 1)
                        step_done(1)
                        u_cols = uT[:, chunk, :].rearrange("p a h -> p (a h)")
                        dve.tensor_tensor(decay[:], decay[:], by_head(u_cols), ALU.add).then_inc(ml_v, 1)
                        dve.wait_ge(chunk_in[4][c], 16 * (q + 1))
                        dve.wait_ge(chunk_in[0][c], 16 * (q + 1))
                        dve.tensor_tensor(qs[:], qc[c][:], m_rows[c][:, 1, :, :], ALU.mult).then_inc(ml_v, 1)
                        dve.wait_ge(decay_set, 2 * q + c + 1)
                        dve.wait_ge(kq_mm, 2 * q + c + 1)
                        dve.tensor_tensor(sw[:], PS[:, 2, :].rearrange("p (h t) -> p h t", h=ML_HEADS), decay[:],
                                          ALU.mult).then_inc(ml_v, 1)
                        dve.tensor_tensor(kw[:], PS[:, 6, :].rearrange("p (h t) -> p h t", h=ML_HEADS),
                                          by_head(decay[:, :, CHUNK - 1]), ALU.mult).then_inc(ml_v, 1)
                    elif kind == "num":
                        dve.wait_ge(num_mm, 2 * q + c + 1)
                        for b in range(2):
                            two = PS[:, 3 + b, 0:258].rearrange("p (h n) -> p h n", h=2)
                            dve.scalar_tensor_tensor(
                                hstat[:, 0, 2 * b:2 * b + 2], two[:, :, ML_DIM], -1.0,
                                emT[:, chunk, 2 * b:2 * b + 2].rearrange("p a h -> p (a h)"), ALU.mult,
                                ALU.max).then_inc(ml_v, 1)
                        step_done(2)
                        for b in range(2):
                            two = PS[:, 3 + b, 0:258].rearrange("p (h n) -> p h n", h=2)
                            den = hstat[:, 0, 2 * b:2 * b + 2]
                            dve.tensor_tensor(den, two[:, :, ML_DIM], den, ALU.max).then_inc(ml_v, 1)
                        step_done(4)
                        dve.reciprocal(hstat[:, 1, :], hstat[:, 0, :]).then_inc(ml_v, 1)
                        step_done(5)
                        for b in range(2):
                            two = PS[:, 3 + b, 0:258].rearrange("p (h n) -> p h n", h=2)
                            dve.tensor_tensor(hb[:, 2 * b:2 * b + 2, :], two[:, :, 0:ML_DIM],
                                              hstat[:, 1, 2 * b:2 * b + 2].unsqueeze(2).to_broadcast([P, 2, ML_DIM]),
                                              ALU.mult).then_inc(ml_v, 1)
                    elif kind == "state":
                        dve.wait_ge(state_mm, 2 * q + c + 1)
                        for h in range(ML_HEADS):
                            dve.scalar_tensor_tensor(
                                state[:, h, :], state[:, h, :], m_rows[c][:, 1, h, CHUNK - 1:CHUNK],
                                PS[:, (5, 7)[h // 2], (h % 2) * 129:(h % 2 + 1) * 129], ALU.mult,
                                ALU.add).then_inc(ml_v, 1)
                    elif kind == "out":
                        step_done(7, "num")
                        dve.tensor_reduce(hstat[:, 2, :], hb[:], AX_X, ALU.add).then_inc(ml_v, 1)
                        step_done(1)
                        dve.tensor_scalar(hstat[:, 2, :], hstat[:, 2, :], -1.0 / ML_DIM, None,
                                          ALU.mult).then_inc(ml_v, 1)
                        step_done(2)
                        dve.tensor_tensor(hb[:], hb[:], by_head(hstat[:, 2, :]), ALU.add).then_inc(ml_v, 1)
                        step_done(3)
                        dve.tensor_tensor(hsq[:], hb[:], hb[:], ALU.mult).then_inc(ml_v, 1)
                        step_done(4)
                        dve.tensor_reduce(hstat[:, 3, :], hsq[:], AX_X, ALU.add).then_inc(ml_v, 1)
                        dve.wait_ge(ml_root, 2 * q + c + 1)
                        dve.reciprocal(hstat[:, 5, :], hstat[:, 4, :]).then_inc(ml_v, 1)
                        step_done(6)
                        dve.tensor_tensor(HN[:].rearrange("p (h n) -> p h n", h=ML_HEADS), hb[:],
                                          by_head(hstat[:, 5, :]), ALU.mult).then_inc(ml_v, 1)
                    elif kind == "flip":
                        dve.wait_ge(flip_mm, 2 * q + c + 1)
                        dve.wait_ge(chunk_in[5][c], 16 * (q + 1))
                        dve.tensor_tensor(YB[:, :, bass.ds(CHUNK * (2 * q + c), CHUNK)],
                                          PS[:, 6, :].rearrange("p (h t) -> p h t", h=ML_HEADS), oc[c][:],
                                          ALU.mult).then_inc(ml_v, 1)

            def piece_lo(b, h, i):
                n = 4 * h + i
                tokens = slice(h * HALF, (h + 1) * HALF)
                src = YB[:, i, tokens] if b else PS[:, Y_BANKS[n], :]
                dve.wait_ge(act_hi, 2 * KT + 8 * b + n + 1)
                dve.tensor_tensor(actT_lo[:, 4 * b + i, tokens], src, actT_hi[:, 4 * b + i, tokens].bitcast(F32),
                                  ALU.subtract).then_inc(act_lo, 1)

            def add_down(tile, groups=range(16)):
                for g in groups:
                    t, c = divmod(g, 2)
                    cols = slice(c * 512, (c + 1) * 512)
                    dve.wait_ge(x_add, X_START + 16 * (tile - 1) + g + 1)
                    dve.wait_ge(down_mm, DOWN_START + 16 * tile + g + 1)
                    dve.tensor_tensor(X[:, t, cols], X[:, t, cols], PS[:, 4 + g % 4, :],
                                      ALU.add).then_inc(x_add, 1)

            def a_lo_part(tile, h, a_slot, src):
                tokens = slice(h * HALF, (h + 1) * HALF)
                dve.wait_ge(a_hi, 2 * tile + h + 1)
                dve.tensor_tensor(A_lo[:, a_slot, tokens], sg[:, src, tokens],
                                  A_hi[:, a_slot, tokens].bitcast(F32), ALU.subtract).then_inc(a_lo, 1)

            def mix_fox(m):
                dve.wait_ge(g_in[0], 16 * (m + 1))
                for h in range(2):
                    tokens = slice(h * HALF, (h + 1) * HALF)
                    dve.wait_ge(br_mm, 4 * m + h + 1)
                    dve.tensor_tensor(sg[:, 0, tokens], PS[:, h, :], sg[:, 0, tokens], ALU.mult).then_inc(mix_v, 1)

            def mix_ml(m, h):
                tokens = slice(h * HALF, (h + 1) * HALF)
                dve.wait_ge(g_in[1], 16 * (m + 1))
                dve.wait_ge(br_mm, 4 * m + h + 3)
                dve.tensor_tensor(sg[:, 1, tokens], PS[:, 2 + h, :], sg[:, 1, tokens], ALU.mult).then_inc(mix_v, 1)
                dve.wait_ge(mix_v, 6 * m + 3 + 2 * h)
                dve.tensor_tensor(sg[:, 0, tokens], sg[:, 0, tokens], sg[:, 1, tokens], ALU.add).then_inc(mix_v, 1)

            def merge_tile(m, n, rounds, a_slot):
                split(n + 2, rounds)
                mix_fox(m)
                add_down(m - 1, range(0, 8))
                mix_ml(m, 0)
                add_down(m - 1, range(8, 10))
                a_lo_part(m, 0, a_slot, 0)
                add_down(m - 1, range(10, 16))
                mix_ml(m, 1)
                split(n + 3, rounds)
                a_lo_part(m, 1, a_slot, 0)

            dve.sem_inc(x_add, X_START)
            for b, h in ((0, 0), (0, 1), (1, 0)):
                for i in range(4):
                    piece_lo(b, h, i)
            mix_fox(0)
            for i in range(4):
                piece_lo(1, 1, i)
            split(U_MERGE + 2)
            for h in range(2):
                mix_ml(0, h)
                a_lo_part(0, h, 0, 0)
            for t in range(TT):
                dve.wait_ge(x_in[t], 32)
            with dve.Fori(0, 2) as r:
                for i in range(3):
                    merge_tile(3 * r + i + 1, U_MERGE + 2 * i + 1, 2 * r, (i + 1) % 3)
            merge_tile(KT - 1, U_MERGE + 13, 0, 1)
            split(U_FFN + 1)
            add_down(KT - 1, range(12))

            scale_diagonals(1, 0, scale)
            add_down(KT - 1, range(12, 16))
            norm_lo(1, 0, range(4))
            scale_diagonals(1, 1, scale)
            norm_lo(1, 0, range(4, KT))
            norm_lo(1, 1, range(KT))

            def glu_gate(m, h):
                tokens = slice(h * HALF, (h + 1) * HALF)
                dve.wait_ge(tanh_g, 2 * m + h + 1)
                dve.scalar_tensor_tensor(sg[:, 0, tokens], sg[:, 0, tokens], 1.0, PS[:, h, :], ALU.add,
                                         ALU.mult).then_inc(glu_a, 1)

            def glu_up(m, h):
                tokens = slice(h * HALF, (h + 1) * HALF)
                dve.wait_ge(glu_a, 2 * m + h + 1)
                dve.wait_ge(gu_mm, 4 * m + h + 3)
                dve.scalar_tensor_tensor(sg[:, 1, tokens], sg[:, 0, tokens], 0.5, PS[:, 2 + h, :], ALU.mult,
                                         ALU.mult).then_inc(glu_b, 1)

            split(U_FFN + 2)
            for h in range(2):
                glu_gate(0, h)
            for h in range(2):
                glu_up(0, h)
                a_lo_part(KT, h, 0, 1)

            def ffn_tile(m, n, rounds, a_slot):
                split(n + 1, rounds)
                split(n + 2, rounds)
                for h in range(2):
                    glu_gate(m, h)
                split(n + 3, rounds)
                add_down(KT + m - 1, range(0, 8))
                glu_up(m, 0)
                add_down(KT + m - 1, range(8, 10))
                a_lo_part(KT + m, 0, a_slot, 1)
                add_down(KT + m - 1, range(10, 16))
                glu_up(m, 1)
                a_lo_part(KT + m, 1, a_slot, 1)

            with dve.Fori(0, FT // 2 - 1) as r:
                for i in range(2):
                    at = 3 * i + 2
                    ffn_tile(2 * r + i + 1, U_FFN + at, 2 * r, (i + 1) % 2)
            at = U_FFN + 3 * (FT - 2) + 2
            ffn_tile(FT - 1, at, 0, 1)
            add_down(KT + FT - 1)

        @block.sync
        def _(sp):
            for t in range(4):
                sp.dma_start(X0[:, t, :], x_tiles[t]).then_inc(x_in[t], 16)
            sp.wait_ge(gate_zero, 1)
            w_gates = w_tile(W_raw, 0)
            for row, name, n in ((ROW_FA, "fa", FOX_HEADS), (ROW_IB, "ib", ML_HEADS), (ROW_FB, "fb", ML_HEADS)):
                sp.dma_start(w_gates[:, :, row:row + n], w_cols(w_in, COL[name], n)).then_inc(gate_raw, 16)
            for t in range(4, TT):
                sp.dma_start(X0[:, t, :], x_tiles[t]).then_inc(x_in[t], 16)

            def load(n, slot, src, free=True):
                if free:
                    sp.wait_ge(w_lo, n - 2)
                sp.dma_start(w_tile(W_raw, slot), src).then_inc(w_raw[slot], 16)

            for b, name in enumerate(("va", "vb")):
                for u in range(4):
                    n = U_VALUES + 4 * b + u
                    if n >= RING:
                        sp.wait_ge(w_lo, n - 2)
                    src = w_in[2 * u * P:2 * (u + 1) * P, COL[name]:COL[name] + 512]
                    sp.dma_start(W_raw[:, n % RING, :].rearrange("p (k n) -> p k n", k=2),
                                 src.rearrange("(k p) n -> p k n", p=P)).then_inc(w_raw[n % RING], 16)

            with sp.Fori(0, PAIRS) as p:
                for j, name in enumerate(("qa", "ka", "qb", "kb", "ob", "ga")):
                    load(U_FOX + FOX_UNITS * p + j, j % RING, w_cols(w_in, P * p + COL[name]))

            with sp.Fori(0, ML_STEPS) as q:
                for j in range(ML_UNITS):
                    col = COL["ga"] + P * G_IN_FOX + P * ML_UNITS * q + P * j
                    load(U_ML + ML_UNITS * q + j, j % RING, w_cols(w_in, col))

            def load_branches(n, slot, m):
                sp.wait_ge(w_lo, n - 2)
                raw = w_tile(W_raw, slot)
                sp.dma_start(raw[:, 0:4, :], w_cols(w_fox_out, P * m)).then_inc(w_first, 16)
                sp.wait_ge(w_first, 16 * (m + 1))
                sp.dma_start(raw[:, 4:8, :], w_cols(w_mlstm_out, P * m)).then_inc(w_raw[slot], 16)

            def load_rows(n, slot, w, tile):
                sp.wait_ge(w_lo, n - 2)
                sp.dma_start(W_raw[:, slot, :],
                             w.rearrange("(k p) n -> k p n", p=P)[bass.ds(tile, 1)].rearrange("a p n -> (a p) n"))\
                    .then_inc(w_raw[slot], 16)

            load_branches(U_MERGE, 0, 0)
            load_branches(U_MERGE + 1, 1, 1)
            load_rows(U_MERGE + 2, 2, w_o, 0)
            sp.wait_ge(ml_v, ML_SETUP + ML_STEPS * ML_V_STEPS)
            for t in range(TT):
                sp.dma_start(X[:, t, :], x_tiles[t]).then_inc(x_in[t], 16)
            with sp.Fori(0, 2) as r:
                for i in range(3):
                    n = U_MERGE + 6 * r + 2 * i + 3
                    load_branches(n, (2 * i + 3) % RING, 3 * r + i + 2)
                    load_rows(n + 1, (2 * i + 4) % RING, w_o, 3 * r + i + 1)
            load_rows(U_MERGE + 15, 15 % RING, w_o, KT - 1)

            load(U_FFN, U_FFN % RING, w_cols(w_gate, 0))
            load(U_FFN + 1, (U_FFN + 1) % RING, w_cols(w_up, 0))
            with sp.Fori(0, FT // 2 - 1) as r:
                for i in range(2):
                    n = U_FFN + 6 * r + 3 * i + 2
                    slot = U_FFN + 3 * i + 2
                    m = 2 * r + i + 1
                    load(n, slot % RING, w_cols(w_gate, P * m))
                    load(n + 1, (slot + 1) % RING, w_cols(w_up, P * m))
                    load_rows(n + 2, (slot + 2) % RING, w_down, m - 1)
            n = U_FFN + 3 * (FT - 2) + 2
            load(n, n % RING, w_cols(w_gate, P * (FT - 1)))
            load(n + 1, (n + 1) % RING, w_cols(w_up, P * (FT - 1)))
            load_rows(n + 2, (n + 2) % RING, w_down, FT - 2)
            load_rows(n + 3, (n + 3) % RING, w_down, FT - 1)

            for t in range(TT):
                sp.wait_ge(x_add, X_START + 16 * (KT + FT - 1) + 2 * t + 2)
                sp.dma_start(out_tiles[t], X[:, t, :]).then_inc(out_in, 16)
            sp.wait_ge(out_in, 16 * TT)

        @block.gpsimd
        def _(pool):
            def wait(signal, count):
                pool.wait_ge(signal, count)
                pool.sem_inc(transfer_due, 1)

            pool.memset(W_raw[:, 0, :], 0.0).then_inc(gate_zero, 1)
            pool.memset(gate_bias[:], 0.0).then_inc(gate_zero, 1)
            pool.memset(ident[:], 0.0).then_inc(const_set, 1)
            pool.memset(ident_bf[:], 0.0).then_inc(const_set, 1)
            pool.memset(mask_bf[:], 0.0).then_inc(const_set, 1)
            pool.memset(mask_ml[:], 0.0).then_inc(const_set, 1)
            pool.wait_ge(const_set, 4)
            for m in (ident, ident_bf):
                pool.affine_select(out=m[:], in_=m[:], compare_op=ALU.not_equal, fill=1.0, base=0,
                                   pattern=[[-1, P]], channel_multiplier=1).then_inc(const_set, 1)
            pool.affine_select(out=mask_bf[:], in_=mask_bf[:], compare_op=ALU.is_ge, fill=MASKED, base=0,
                               pattern=[[-1, P]], channel_multiplier=1).then_inc(const_set, 1)
            pool.affine_select(out=mask_ml[:], in_=mask_ml[:], compare_op=ALU.is_ge, fill=MASKED, base=0,
                               pattern=[[1, P]], channel_multiplier=-1).then_inc(const_set, 1)

            for i, g in enumerate((g_mix, g_ffn)):
                pool.dma_start(g_cols[:, i, :], g[0].rearrange("(k p) -> p k", p=P),
                               allow_slow_non_contiguous=True).then_inc(gains_in, 16)
            pool.wait_ge(gate_zero, 2)
            consts = (
                [(gate_bias[row:row + n, :], b[0].rearrange("(p a) -> p a", a=1))
                 for row, b, n in ((ROW_FA, b_fox_f, FOX_HEADS), (ROW_IB, b_mlstm_i, ML_HEADS),
                                   (ROW_FB, b_mlstm_f, ML_HEADS))]
                + [(g_qk[hd * FOX_DIM:(hd + 1) * FOX_DIM, i:i + 1], g[0].rearrange("(p a) -> p a", a=1))
                   for i, g in enumerate((g_q_fox, g_k_fox)) for hd in range(2)]
                + [(g_ml[:], g_mlstm_h[0].rearrange("(k p) -> p k", p=P))]
                + [(taps[:, :, tap], conv_w[tap].rearrange("(k p) -> p k", p=P)) for tap in range(TAPS)]
                + [(taps[:, :, TAPS], conv_b[0].rearrange("(k p) -> p k", p=P))])
            assert len(consts) == N_CONST
            for dst, src in consts:
                pool.dma_start(dst, src, allow_slow_non_contiguous=True).then_inc(const_in, 16)

            rows = slice(ROW_FB, ROW_FB + ML_HEADS)
            pool.wait_ge(gate_a, 6)
            for dst, src in ((d_c[0], csum[0:FOX_HEADS, :]), (d_c[1], negs[0:FOX_HEADS, :]),
                             (d_m[0], negs[rows, :]), (d_m[1], wi_em[rows, 0, :])):
                pool.dma_start(dst, src).then_inc(rows_out, 16)

            for t in range(TT):
                pool.wait_ge(val_out, TT + t + 1)
                pool.dma_start(d_v[t], stage[:, t % 2, 0:ML_WIDTH]).then_inc(stored[t % 2], 16)

            def store(dst, slot):
                pool.dma_start(dst, stage[:, slot, :]).then_inc(stored[slot], 16)

            def one(d, at):
                return d[bass.ds(at, 1)].rearrange("a p n -> (a p) n")

            pool.wait_ge(rows_out, 64)
            pool.wait_ge(ones_set, 2)
            def load_c(p):
                wait(score_mm, 2 * TT * p + 1)
                pair = bass.ds(2 * p, 2)
                pool.dma_start(QA[FOX_DIM:FOX_DIM + 1, :, :], d_c[0:1, pair, :]).then_inc(c_in[0], 16)
                pool.dma_start(KA[FOX_DIM + 1:FOX_DIM + 2, :, :], d_c[1:2, pair, :]).then_inc(c_in[1], 16)

            def store_tile(p, n):
                wait(tile_set, 4 * p + n + 1)
                store(one((d_qk, d_qk, d_ob, d_g)[n], p + ML_HEADS if n == 1 else p), n % 2)

            def load_chunk(n, c):
                tok = bass.ds(CHUNK * n, CHUNK)
                for i in range(2):
                    pool.dma_start(m_rows[c][:, i, :, :], d_m[i, :, tok].partition_broadcast(P))\
                        .then_inc(chunk_in[3 + i][c], 16)
                pool.dma_start(qc[c][:], d_qk[0:ML_HEADS, :, tok].rearrange("h p t -> p h t"))\
                    .then_inc(chunk_in[0][c], 16)
                pool.dma_start(kc[c][:], d_qk[ML_HEADS:2 * ML_HEADS, :, tok].rearrange("h p t -> p h t"))\
                    .then_inc(chunk_in[1][c], 16)
                pool.dma_start(vc[c][:, :, 0:ML_DIM],
                               one(d_v, n).rearrange("p (h n) -> p h n", h=ML_HEADS)).then_inc(chunk_in[2][c], 16)

            def load_o(n, c):
                pool.dma_start(oc[c][:], d_ob[:, :, bass.ds(CHUNK * n, CHUNK)].rearrange("h p t -> p h t"))\
                    .then_inc(chunk_in[5][c], 16)

            with pool.Fori(0, PAIRS - 1) as p:
                load_c(p)
                for n in range(4):
                    store_tile(p, n)
            load_c(PAIRS - 1)
            store_tile(PAIRS - 1, 0)
            store_tile(PAIRS - 1, 1)
            pool.wait_ge(stored[0], 16 * (4 + 2 * PAIRS - 1))
            pool.wait_ge(stored[1], 16 * (4 + 2 * PAIRS - 1))
            load_chunk(0, 0)
            store_tile(PAIRS - 1, 2)
            store_tile(PAIRS - 1, 3)

            pool.wait_ge(stored[0], 16 * (4 + 2 * PAIRS))
            load_o(0, 0)
            pool.wait_ge(ml_v, ML_SETUP)
            load_chunk(1, 1)
            load_o(1, 1)

            def ml_stage(q, more):
                for step in ml_steps:
                    kind, *at = step
                    if kind == "half" and at[1] == 1:
                        j = at[0]
                        wait(tile_set, 4 * PAIRS + ML_UNITS * q + j + 1)
                        store(one(d_g, G_IN_FOX + ML_UNITS * q + j), j % 2)
                    elif kind == "out" and more:
                        c, = at
                        wait(ml_v, ml_at(q, "state", c, 4))
                        load_chunk(2 * q + 2 + c, c)
                    elif kind == "flip":
                        c, = at
                        wait(ml_v, ml_at(q, "flip", c, 1))
                        if more:
                            load_o(2 * q + 2 + c, c)
                        elif c == 0:
                            pool.wait_ge(stored[0], 16 * ml_stores(ML_STEPS - 1, 0))
                            pool.wait_ge(stored[1], 16 * ml_stores(ML_STEPS - 1, 1))
                            load_g(0)

            def load_g(m):
                for i in range(2):
                    pool.dma_start(sg[:, i, :], one(d_g, m + KT * i)).then_inc(g_in[i], 16)

            with pool.Fori(0, ML_STEPS - 1) as q:
                ml_stage(q, True)
            ml_stage(ML_STEPS - 1, False)

            pool.wait_ge(stored[0], 16 * ml_stores(ML_STEPS, 0))
            pool.wait_ge(stored[1], 16 * ml_stores(ML_STEPS, 1))
            with pool.Fori(1, KT) as m:
                wait(a_lo, 2 * m)
                load_g(m)


_INS = ["x", "g_mix", "w_in", "b_fox_f", "g_q_fox", "g_k_fox", "conv_w", "conv_b", "b_mlstm_i", "b_mlstm_f",
        "g_mlstm_h", "w_fox_out", "w_mlstm_out", "w_o", "g_ffn", "w_gate", "w_up", "w_down"]


def kernel(**inputs):
    import concourse.bacc as bacc
    from concourse.bass_utils import run_bass_kernel_spmd

    nc = bacc.Bacc("TRN2", target_bir_lowering=False, num_devices=1)
    arrays, args = {}, []
    for name in _INS:
        a = np.ascontiguousarray(inputs[name])
        arrays[f"in_{name}"] = a
        args.append(nc.dram_tensor(f"in_{name}", a.shape, F32, kind="ExternalInput").ap())
    out = nc.dram_tensor("out", (1, SEQ, D_MODEL), F32, kind="ExternalOutput").ap()
    hybrid_block(nc, *args, out)
    r = run_bass_kernel_spmd(nc, [arrays], core_ids=[0])
    return r.results[0]["out"]
```

```python
from contextlib import ExitStack

import numpy as np

import concourse.bass as bass
from concourse import mybir

F32 = mybir.dt.float32
F32R = mybir.dt.float32r
BF16 = mybir.dt.bfloat16
ACT = mybir.ActivationFunctionType
ALU = mybir.AluOpType
AX_X = mybir.AxisListType.X

P = 128
SEQ = 1024
D_MODEL = 1024
KT = D_MODEL // P
TT = SEQ // P
HALF = SEQ // 2
FOX_HEADS, FOX_DIM = 8, 64
FOX_WIDTH = FOX_HEADS * FOX_DIM
PAIRS = FOX_HEADS // 2
ML_HEADS, ML_DIM = 4, 128
ML_WIDTH = ML_HEADS * ML_DIM
CHUNK = 128
CHUNKS = SEQ // CHUNK
TAPS = 4
D_FF = 2816
FT = D_FF // P
EPS = 1e-6
MASKED = -1e30

COL = {}
_at = 0
for _name, _width in (("qa", FOX_WIDTH), ("ka", FOX_WIDTH), ("va", FOX_WIDTH), ("fa", FOX_HEADS),
                      ("qb", ML_WIDTH), ("kb", ML_WIDTH), ("vb", ML_WIDTH), ("ib", ML_HEADS), ("fb", ML_HEADS),
                      ("ob", ML_WIDTH), ("ga", D_MODEL), ("gb", D_MODEL)):
    COL[_name] = _at
    _at += _width

ROW_FA, ROW_IB, ROW_FB = 0, 32, 64
GATE_ROWS = ROW_FB + ML_HEADS

RING = 3
U_VALUES = 1
U_FOX = U_VALUES + 8
FOX_UNITS = 6
U_ML = U_FOX + PAIRS * FOX_UNITS
ML_UNITS = 3
ML_STEPS = CHUNKS // 2
U_MERGE = U_ML + ML_STEPS * ML_UNITS
U_FFN = U_MERGE + 2 * KT
assert U_FOX % RING == 0 and FOX_UNITS % RING == 0 and ML_UNITS % RING == 0 and U_MERGE % RING == 0
G_IN_FOX = PAIRS
N_TAPS_COLS = TAPS + 1
N_CONST = 13


def raw_count(n, rounds):
    return n // RING + (1 if n % RING else 0) + rounds


def ml_stores(q, j):
    before = 4 + 2 * PAIRS
    return before + 2 * q + (j == 2) if j % 2 == 0 else before + q


EARLY_GAP = 6
TURN_GAP, VALUES_GAP = 4, 5
ATTEND_AFTER = 12


def fox_schedule():
    def half(j, h):
        return ([("unit", j)] if h == 0 else []) + [("dense", j, h, a, a + 1) for a in range(24)] + [("half", j, h)]
    def then(j, h, x, xh):
        steps = half(j, h)
        return steps[:7] + [("norm", x, xh)] + steps[7:] + [("parts", x, xh)]
    head = half(0, 0) + then(0, 1, 0, 0) + then(1, 0, 0, 1) + then(1, 1, 1, 0) + then(2, 0, 1, 1)
    rest = half(2, 1) + [e for j in (3, 4, 5) for h in (0, 1) for e in half(j, h)]
    steps = 2 * TT
    start = [("scores", 0), ("exp", 0), ("scores", 1), ("exp", 1)]
    attend, gap = [], []
    for s in range(steps + 1):
        if s < steps:
            attend.append([("turn", s, 0)] + ([("scores", s + 2)] if s + 2 < steps else []))
            gap.append(TURN_GAP if s // 2 >= 4 else EARLY_GAP)
        group = ([("turn", s, 1)] if 4 <= s // 2 < TT else []) + ([("exp", s + 2)] if s + 2 < steps else []) \
            + ([("values", s - 1)] if s else [])
        attend.append(group)
        gap.append(VALUES_GAP if s // 2 >= 4 else EARLY_GAP)
    n_mm = sum(e[0] == "dense" for e in rest)
    out, seen, used, later = [], 0, 0, []
    for e in rest:
        if e[0] == "dense":
            while (used < len(attend)
                   and sum(gap[:used + 1]) * (n_mm - ATTEND_AFTER) <= (seen - ATTEND_AFTER) * sum(gap)):
                out += attend[used]
                used += 1
            while later and seen >= later[0][0]:
                out.append(later.pop(0)[1])
            seen += 1
        out.append(e)
        if e[0] == "half" and e[1] in (2, 3) and e[2] == 1:
            later += [(seen + 5 * n, ("conv", e[1], n)) for n in range(TAPS)] + [(seen + 21, ("silu", e[1]))]
    assert not later
    return head[:-1] + start + head[-1:] + out + [x for a in attend[used:] for x in a]


def ml_schedule():
    steps = [("kq", 0), ("num", 0), ("state", 0), ("kq", 1), ("out", 0), ("num", 1), ("flip", 0), ("state", 1),
             ("out", 1), ("flip", 1)]
    at = [9, 30, 42, 58, 62, 74, 84, 90, 104, 138]
    out, seen = [], 0
    for j in range(ML_UNITS):
        for h in (0, 1):
            if h == 0:
                out.append(("unit", j))
            for a in range(24):
                while at and at[0] <= seen:
                    out.append(steps.pop(0))
                    at.pop(0)
                out.append(("dense", j, h, a, a + 1))
                seen += 1
            out.append(("half", j, h))
    return out + steps


def turn_fill(s, part):
    i = s // 2
    return (s if i < 4 else 8 + 2 * (s - 8)) + part


FILLS = turn_fill(2 * TT - 1, 1) + 1


ML_STEP_COUNT = {"kq": 5, "num": 7, "state": 4, "out": 7, "flip": 1}
ML_SETUP = 3
ML_OFFSET = {}
ML_V_STEPS = 0
for _step in ml_schedule():
    if _step[0] in ML_STEP_COUNT:
        ML_OFFSET[_step] = ML_V_STEPS
        ML_V_STEPS += ML_STEP_COUNT[_step[0]]

Y_BANKS = (4, 5, 7, 6, 2, 3, 4, 5)
X_START = 16
DOWN_START = 16


def ml_at(q, kind, c, steps):
    return ML_SETUP + ML_V_STEPS * q + ML_OFFSET[kind, c] + steps


def hybrid_block(nc, x, g_mix, w_in, b_fox_f, g_q_fox, g_k_fox, conv_w, conv_b, b_mlstm_i, b_mlstm_f,
                 g_mlstm_h, w_fox_out, w_mlstm_out, w_o, g_ffn, w_gate, w_up, w_down, out):
    fox_steps, ml_steps = fox_schedule(), ml_schedule()
    w_in, conv_w, w_fox_out, w_mlstm_out, w_o = w_in[0], conv_w[0], w_fox_out[0], w_mlstm_out[0], w_o[0]
    w_gate, w_up, w_down = w_gate[0], w_up[0], w_down[0]

    d_qk = nc.dram_tensor("d_qk", (2 * ML_HEADS, P, SEQ), F32, kind="Internal").ap()
    d_v = nc.dram_tensor("d_v", (TT, P, ML_WIDTH), F32, kind="Internal").ap()
    d_ob = nc.dram_tensor("d_ob", (ML_HEADS, P, SEQ), F32, kind="Internal").ap()
    d_g = nc.dram_tensor("d_g", (2 * KT, P, SEQ), F32, kind="Internal").ap()
    d_c = nc.dram_tensor("d_c", (4, FOX_HEADS, SEQ), F32R, kind="Internal").ap()
    d_m = nc.dram_tensor("d_m", (2, ML_HEADS, SEQ), F32, kind="Internal").ap()

    x_tiles = x[0].rearrange("(t p) d -> t p d", p=P)
    out_tiles = out[0].rearrange("(t p) d -> t p d", p=P)

    def w_cols(w, col, n=P):
        return w.rearrange("(k p) n -> p k n", p=P)[:, :, bass.ds(col, n)]

    with ExitStack() as ctx:
        def sb(name, shape, dt=F32, where=ctx):
            return where.enter_context(nc.sbuf_tensor(name, shape, dt))

        def sem(name):
            return ctx.enter_context(nc.semaphore(name))

        actT_hi = sb("actT_hi", [P, KT, SEQ], F32R)
        actT_lo = sb("actT_lo", [P, KT, SEQ], F32R)
        W_hi = sb("W_hi", [P, RING, 1024], F32R)
        W_lo = sb("W_lo", [P, RING, 1024], F32R)
        W_raw = sb("W_raw", [P, RING, 1024])
        ident = sb("ident", [P, P])
        ident_bf = sb("ident_bf", [P, P], BF16)
        mask_bf = sb("mask_bf", [P, P], BF16)
        mask_ml = sb("mask_ml", [P, P])
        head_mean = sb("head_mean", [P, P])
        g_cols = sb("g_cols", [P, 2, KT])
        g_qk = sb("g_qk", [P, 2])
        g_ml = sb("g_ml", [P, ML_HEADS])
        gate_bias = sb("gate_bias", [GATE_ROWS, 1])
        taps = sb("taps", [P, 2 * ML_HEADS, N_TAPS_COLS])
        eps_col = sb("eps_col", [P, 1])
        stat = sb("stat", [P, 3, TT])
        uT = sb("uT", [P, CHUNKS, ML_HEADS])
        emT = sb("emT", [P, CHUNKS, ML_HEADS])
        nmax = sb("nmax", [P, 2])
        psumrow = sb("psumrow", [P, 2])
        rinv = sb("rinv", [P, 2])
        hstat = sb("hstat", [P, 6, ML_HEADS])

        def chunk_buffers(n, where):
            return (sb(f"qc{n}", [P, ML_HEADS, CHUNK], where=where), sb(f"kc{n}", [P, ML_HEADS, CHUNK], where=where),
                    sb(f"vc{n}", [P, ML_HEADS, ML_DIM + 1], where=where),
                    sb(f"m_rows{n}", [P, 2, ML_HEADS, CHUNK], where=where),
                    sb(f"oc{n}", [P, ML_HEADS, CHUNK], where=where))

        with ExitStack() as early:
            X0 = sb("X0", [P, TT, D_MODEL], where=early)
            scale0 = sb("scale0", [P, TT, P], where=early)
            dump0 = sb("dump0", [P, 4, D_MODEL], where=early)
        with ExitStack() as gates:
            V = sb("V", [P, TT, FOX_WIDTH], where=gates)
            z = sb("z", [GATE_ROWS, SEQ], where=gates)
            soft = sb("soft", [GATE_ROWS, SEQ], where=gates)
            logs = sb("logs", [GATE_ROWS, SEQ], where=gates)
            keep = sb("keep", [GATE_ROWS, SEQ], where=gates)
            csum = sb("csum", [GATE_ROWS, SEQ], where=gates)
            negs = sb("negs", [GATE_ROWS, SEQ], where=gates)
            u_m = sb("u_m", [GATE_ROWS, 2, SEQ], where=gates)
            shift = sb("shift", [GATE_ROWS, SEQ], where=gates)
            wi_em = sb("wi_em", [GATE_ROWS, 2, SEQ], where=gates)
            m_prev = sb("m_prev", [GATE_ROWS, CHUNKS], where=gates)
        with ExitStack() as mid:
            sb("fox_V", [P, TT, FOX_WIDTH], where=mid)
            QHL = sb("QHL", [P, 2, SEQ], F32R, where=mid)
            KHH = sb("KHH", [P, 2, SEQ], F32R, where=mid)
            Y = sb("Y", [P, TT, FOX_WIDTH], where=mid)
            QHC = sb("QHC", [P, 2, SEQ], F32R, where=mid)
            KLC = sb("KLC", [P, 2, SEQ], F32R, where=mid)
        with ExitStack() as mlo:
            sb("ml_before_", [P, 6, 2 * SEQ], where=mlo)
            YB = sb("YB", [P, ML_HEADS, SEQ], where=mlo)
        with ExitStack() as mlp:
            chunk1 = chunk_buffers(1, mlp)
            state = sb("state", [P, ML_HEADS, ML_DIM + 1], where=mlp)
            HN = sb("HN", [P, ML_WIDTH], where=mlp)
        with ExitStack() as late:
            X = sb("X", [P, TT, D_MODEL], where=late)
            scale = sb("scale", [P, TT, P], where=late)
            dump = sb("dump", [P, 4, D_MODEL], where=late)

        big = ctx.enter_context(nc.sbuf_tensor("big_region", [P, 2 * TT * D_MODEL], F32))
        with ExitStack() as fox:
            stage = sb("stage", [P, 2, SEQ], where=fox)
            sq = sb("sq", [P, HALF], where=fox)
            root = sb("root", [P, HALF], where=fox)
            prob = sb("prob", [P, 2, SEQ], where=fox)
            probT = sb("probT", [P, TT, P], where=fox)
            qk_raw = sb("qk_raw", [P, 2, SEQ], where=fox)
            conv_in = sb("conv_in", [P, TAPS - 1 + SEQ], where=fox)
            conv_acc = sb("conv_acc", [P, SEQ], where=fox)
        with ExitStack() as fox2:
            sb("fox_before_", [P, 2, SEQ], where=fox2)
            probT_odd = sb("probT_odd", [P, TT, P], where=fox2)
        probT = (probT, probT_odd)
        with ExitStack() as gates2:
            sb("gates_before_", [P, 3, SEQ], where=gates2)
            c_parts = sb("c_parts", [FOX_HEADS, 4, SEQ], F32R, where=gates2)
        with ExitStack() as mlt:
            sb("ml_stage_", [P, 2, SEQ], where=mlt)
            decay = sb("decay", [P, ML_HEADS, CHUNK], where=mlt)
            qs = sb("qs", [P, ML_HEADS, CHUNK], where=mlt)
            sw = sb("sw", [P, ML_HEADS, CHUNK], where=mlt)
            kw = sb("kw", [P, ML_HEADS, ML_DIM], where=mlt)
            hb = sb("hb", [P, ML_HEADS, ML_DIM], where=mlt)
            hsq = sb("hsq", [P, ML_HEADS, ML_DIM], where=mlt)
            sb("ml_probT_", [P, TT, P], where=mlt)
            chunk0 = chunk_buffers(0, mlt)
        with ExitStack() as fin:
            A_hi = sb("A_hi", [P, 3, SEQ], F32R, where=fin)
            A_lo = sb("A_lo", [P, 3, SEQ], F32R, where=fin)
            sg = sb("sg", [P, 2, SEQ], where=fin)
        qc, kc, vc, m_rows, oc = zip(chunk0, chunk1)

        PS = ctx.enter_context(nc.psum_tensor("PS", [P, 8, HALF], F32))

        def score_row(s):
            bank = 2 + 2 * (s % 2)
            return PS[:, bank:bank + 2, :].rearrange("p b n -> p (b n)")[:, 0:(s // 2 + 1) * P]

        x_in = [sem(f"x_in{t}") for t in range(TT)]
        gains_in = sem("gains_in")
        const_in = sem("const_in")
        table_in = sem("table_in")
        const_set = sem("const_set")
        cols_set = sem("cols_set")
        gate_zero = sem("gate_zero")
        gate_raw = sem("gate_raw")
        w_raw = [sem(f"w_raw{s}") for s in range(RING)]
        w_first = sem("w_first")
        w_hi = sem("w_hi")
        w_lo = sem("w_lo")
        w_used = sem("w_used")
        sumsq = sem("sumsq")
        rooted = sem("rooted")
        scaled = sem("scaled")
        turned = sem("turned")
        act_hi = sem("act_hi")
        act_lo = sem("act_lo")
        gate_mm = sem("gate_mm")
        gate_v = sem("gate_v")
        gate_a = sem("gate_a")
        gate_turn = sem("gate_turn")
        gate_out = sem("gate_out")
        rows_out = sem("rows_out")
        val_mm = sem("val_mm")
        val_out = sem("val_out")
        tile_mm = sem("tile_mm")
        tile_out = sem("tile_out")
        sq_set = sem("sq_set")
        mean_mm = sem("mean_mm")
        root_set = sem("root_set")
        inv_set = sem("inv_set")
        qk_norm = sem("qk_norm")
        qk_hi = sem("qk_hi")
        qk_set = sem("qk_set")
        ones_set = sem("ones_set")
        c_in = [sem("cq_in"), sem("ck_in")]
        score_mm = sem("score_mm")
        nmax_set = sem("nmax_set")
        prob_set = sem("prob_set")
        prob_turn = sem("prob_turn")
        probT_set = [sem("probT_set0"), sem("probT_set1")]
        y_mm = sem("y_mm")
        rinv_set = sem("rinv_set")
        y_set = sem("y_set")
        conv_step = sem("conv_step")
        tanh_set = sem("tanh_set")
        conv_mul = sem("conv_mul")
        tile_set = sem("tile_set")
        stored = [sem("stored0"), sem("stored1")]
        chunk_in = [[sem(f"{n}_in{b}") for b in range(2)] for n in ("qc", "kc", "vc", "mc", "wc", "oc")]
        kq_mm = sem("kq_mm")
        num_mm = sem("num_mm")
        state_mm = sem("state_mm")
        ml_v = sem("ml_v")
        decay_set = sem("decay_set")
        ml_root = sem("ml_root")
        flip_mm = sem("flip_mm")
        g_in = [sem("ga_in"), sem("gb_in")]
        br_mm = sem("br_mm")
        mix_v = sem("mix_v")
        a_hi = sem("a_hi")
        a_lo = sem("a_lo")
        down_mm = sem("down_mm")
        x_add = sem("x_add")
        gu_mm = sem("gu_mm")
        tanh_g = sem("tanh_g")
        glu_a = sem("glu_a")
        glu_b = sem("glu_b")
        out_in = sem("out_in")
        transfer_due = sem("transfer_due")

        def w_tile(parts, slot):
            return parts[:, slot, :].rearrange("p (k n) -> p k n", k=KT)

        def norm_bank(round_, h, k):
            return k if round_ == h == 0 else 4 * h + k % 4

        def hi_lo(product, hi_a, lo_a, hi_b, lo_b, first, last):
            product(hi_a, hi_b, first, False)
            product(hi_a, lo_b, False, False)
            return product(lo_a, hi_b, False, last)

        block = ctx.enter_context(nc.Block())

        @block.tensor
        def _(pe):
            def product(dst):
                return lambda a, b, start, stop: pe.matmul(dst, a, b, start=start, stop=stop)

            def dense(bank, slot, half, a, b):
                tokens = slice(half * HALF, (half + 1) * HALF)
                hi, lo = w_tile(W_hi, slot), w_tile(W_lo, slot)
                for n in range(a, b):
                    k, part = divmod(n, 3)
                    w = (hi, hi, lo)[part][:, k, :]
                    act = (actT_hi, actT_lo, actT_hi)[part][:, k, tokens]
                    last = pe.matmul(PS[:, bank, :], w, act, start=n == 0, stop=n == 23)
                return last

            def norm_turn(round_, h, tiles, src, scales):
                for k in tiles:
                    if round_ == 0 and h == 1:
                        pe.wait_ge(act_lo, 4 * h + k + 1)
                    elif round_ and k >= 4:
                        pe.wait_ge(act_lo, 4 * KT * round_ + h * KT + k - 3)
                    for j in range(4):
                        t = 4 * h + j
                        last = pe.matmul(PS[:, norm_bank(round_, h, k), j * P:(j + 1) * P], src[:, t, k * P:(k + 1) * P],
                                         scales[:, t, :], start=True, stop=True)
                    last.then_inc(turned, 1)

            pe.wait_ge(scaled, 5)
            norm_turn(0, 0, range(KT), X0, scale0)
            pe.wait_ge(scaled, 10)
            norm_turn(0, 1, range(4), X0, scale0)
            pe.wait_ge(act_lo, KT)
            pe.wait_ge(w_lo, 1)
            for i in range(4):
                norm_turn(0, 1, (4 + i,), X0, scale0)
                last = dense(0, 0, 0, 6 * i, 6 * i + 6)
            last.then_inc(gate_mm, 1)
            pe.wait_ge(act_lo, 2 * KT)
            dense(1, 0, 1, 0, 24).then_inc(gate_mm, 1)

            def gates_turn():
                pe.wait_ge(gate_a, 6)
                pe.wait_ge(val_out, TT)
                rows = slice(ROW_FB, ROW_FB + ML_HEADS)
                for kind, src in enumerate((u_m[rows, 0, :], wi_em[rows, 1, :])):
                    for c in range(CHUNKS):
                        at = (kind * CHUNKS + c) * ML_HEADS
                        last = pe.transpose(PS[:, 7, at:at + ML_HEADS], src[:, c * CHUNK:(c + 1) * CHUNK],
                                            ident[rows, rows])
                last.then_inc(gate_turn, 1)

            for b in range(2):
                for u in range(4):
                    n = U_VALUES + 4 * b + u
                    slot = n % RING
                    pe.wait_ge(w_lo, n + 1)
                    for t in (range(TT), (2, 3, 4, 5, 6, 7, 0, 1))[n == U_VALUES]:
                        if u == 0 and b == 0 and t < 2:
                            pe.wait_ge(gate_v, 2)
                        if u == 0 and b == 1:
                            if t == 5:
                                gates_turn()
                            if t == 7:
                                pe.wait_ge(gate_out, 2)
                            pe.wait_ge(val_out, t + 1)
                        for i in range(2):
                            k = 2 * u + i
                            tok = slice(t * P, (t + 1) * P)
                            cols = slice(i * 512, (i + 1) * 512)
                            last = hi_lo(product(PS[:, t, :]), actT_hi[:, k, tok], actT_lo[:, k, tok],
                                         W_hi[:, slot, cols], W_lo[:, slot, cols], k == 0, k == KT - 1)
                        if u == 3:
                            last.then_inc(val_mm, 1)
                    if u < 3:
                        last.then_inc(w_used, 1)

            pe.wait_ge(val_mm, 2 * TT)
            pe.sem_inc(tile_mm, 2)

            pe.wait_ge(val_out, TT + 2)
            pe.sem_inc(score_mm, 1)
            with pe.Fori(0, PAIRS) as p:
                for step in fox_steps:
                    kind, *at = step
                    if kind == "unit":
                        j, = at
                        pe.wait_ge(w_lo, U_FOX + FOX_UNITS * p + j + 1)
                    elif kind == "dense":
                        j, h, a, b = at
                        if a == 0:
                            pe.wait_ge(tile_out, 2 * FOX_UNITS * p + 2 * j + h + 1)
                        last = dense(h, j % RING, h, a, b)
                        if b == 24:
                            last.then_inc(tile_mm, 1)
                    elif kind == "norm":
                        q_or_k, h = at
                        pe.wait_ge(val_out, 2 * TT)
                        pe.wait_ge(sq_set, 4 * p + 2 * q_or_k + h + 1)
                        pe.matmul(PS[:, 2 + 2 * q_or_k + h, :], head_mean[:], sq[:], start=True,
                                  stop=True).then_inc(mean_mm, 1)
                    elif kind == "scores":
                        s, = at
                        i, hd = divmod(s, 2)
                        length = (i + 1) * P
                        if s in (0, TT):
                            h = s // TT
                            pe.wait_ge(qk_hi, 16 * p + 12 + 4 * h)
                            pe.wait_ge(qk_set, 8 * p + 6 + 2 * h)
                        if s == 0:
                            pe.wait_ge(c_in[0], 32 * (p + 1))
                            pe.wait_ge(c_in[1], 32 * (p + 1))
                        if s >= 2:
                            pe.wait_ge(prob_set, 2 * TT * p + s - 1)
                        rows = slice(0, (FOX_DIM + 4, P)[hd])
                        passes = ((QHL[:, hd, i * P:(i + 1) * P], KHH[:, hd, :]),
                                  (QHC[rows, hd, i * P:(i + 1) * P], KLC[rows, hd, :]))
                        bank = 2 + 2 * (s % 2)
                        for part in range(0, length, HALF):
                            n = min(HALF, length - part)
                            diagonal = part + n == length
                            dst = PS[:, bank + part // HALF, 0:n]
                            for first, (query, key) in zip((True, False), passes):
                                last = pe.matmul(dst, query, key[:, part:part + n], start=first,
                                                 stop=not (first or diagonal))
                            if diagonal:
                                last = pe.matmul(PS[:, bank + part // HALF, n - P:n], ident_bf[:], mask_bf[:],
                                                 start=False, stop=True)
                        last.then_inc(score_mm, 1)
                    elif kind == "turn":
                        s, part = at
                        if part == 0:
                            pe.wait_ge(prob_set, 2 * TT * p + s + 1)
                        if part:
                            pe.wait_ge(probT_set[0], 2 * TT * p + s + 1)
                        elif s > 8:
                            pe.wait_ge(probT_set[1], TT * p + s - 8)
                        elif s:
                            pe.wait_ge(probT_set[0], 2 * TT * p + s)
                        for b in range(4 * part, min(4 * part + 4, s // 2 + 1)):
                            last = pe.transpose(PS[:, 6, (b % 4) * P:(b % 4 + 1) * P],
                                                prob[:, s % 2, b * P:(b + 1) * P], ident[:])
                        last.then_inc(prob_turn, 1)
                    elif kind == "values":
                        s, = at
                        i, hd = divmod(s, 2)
                        pe.wait_ge(probT_set[0], 2 * TT * p + s + 1)
                        if i >= 4:
                            pe.wait_ge(probT_set[1], TT * p + s - 7)
                        if s:
                            pe.wait_ge(y_set, 2 * TT * p + s)
                        for b in range(i + 1):
                            head = bass.ds(p * P + hd * FOX_DIM, FOX_DIM)
                            last = pe.matmul(PS[:, 7, 0:FOX_DIM], probT[s % 2][:, b, :], V[:, b, head],
                                             start=b == 0, stop=b == i)
                        last.then_inc(y_mm, 1)

            with pe.Fori(0, ML_STEPS) as q:
                for step in ml_steps:
                    kind, *at = step
                    if kind == "unit":
                        j, = at
                        pe.wait_ge(w_lo, U_ML + ML_UNITS * q + j + 1)
                    elif kind == "dense":
                        j, h, a, b = at
                        done = 2 * FOX_UNITS * PAIRS + 2 * ML_UNITS * q + 2 * j + h
                        if a == 0:
                            pe.wait_ge(tile_out, done + 1)
                        last = dense(h, j % RING, h, a, b)
                        if b == 24:
                            last.then_inc(tile_mm, 1)
                    elif kind == "kq":
                        c, = at
                        if c == 0:
                            pe.wait_ge(ml_v, ML_SETUP + ML_V_STEPS * q)
                        for which in (0, 1):
                            pe.wait_ge(chunk_in[which][c], 16 * (q + 1))
                        for h in range(ML_HEADS):
                            pe.transpose(PS[:, 6, h * P:(h + 1) * P], kc[c][:, h, :], ident[:])
                        for h in range(ML_HEADS):
                            last = pe.matmul(PS[:, 2, h * P:(h + 1) * P], kc[c][:, h, :], qc[c][:, h, :],
                                             start=True, stop=True)
                        last.then_inc(kq_mm, 1)
                    elif kind == "num":
                        c, = at
                        pe.wait_ge(chunk_in[2][c], 16 * (q + 1))
                        pe.wait_ge(ml_v, ml_at(q, "kq", c, 4))
                        for h in range(ML_HEADS):
                            dst = PS[:, 3 + h // 2, (h % 2) * 129:(h % 2 + 1) * 129]
                            pe.matmul(dst, sw[:, h, :], vc[c][:, h, :], start=True, stop=False)
                            last = pe.matmul(dst, qs[:, h, :], state[:, h, :], start=False, stop=True)
                        last.then_inc(num_mm, 1)
                    elif kind == "state":
                        c, = at
                        pe.wait_ge(ml_v, ml_at(q, "kq", c, 5))
                        for h in range(ML_HEADS):
                            dst = PS[:, (5, 7)[h // 2], (h % 2) * 129:(h % 2 + 1) * 129]
                            last = pe.matmul(dst, kw[:, h, :], vc[c][:, h, :], start=True, stop=True)
                        last.then_inc(state_mm, 1)
                    elif kind == "flip":
                        c, = at
                        pe.wait_ge(ml_v, ml_at(q, "out", c, 7))
                        for h in range(ML_HEADS):
                            last = pe.transpose(PS[:, 6, h * P:(h + 1) * P], HN[:, h * P:(h + 1) * P], ident[:])
                        last.then_inc(flip_mm, 1)

            def turn_y(pieces):
                for n in pieces:
                    h, k = divmod(n, PAIRS)
                    if n >= 6:
                        pe.wait_ge(act_lo, 2 * KT + n - 5)
                    for j in range(4):
                        last = pe.transpose(PS[:, Y_BANKS[n], j * P:(j + 1) * P],
                                            Y[:, 4 * h + j, k * P:(k + 1) * P], ident[:])
                    last.then_inc(turned, 1)

            pe.wait_ge(ml_v, ml_at(ML_STEPS - 1, "state", 1, 4))
            pe.wait_ge(ml_v, ml_at(ML_STEPS - 1, "flip", 1, 1))
            turn_y(range(6))

            def down(slot, a_slot, tile, groups):
                for g in groups:
                    t, c = divmod(g, 2)
                    pe.wait_ge(x_add, X_START + 16 * tile + g - 3)
                    tok, cols = slice(t * P, (t + 1) * P), slice(c * 512, (c + 1) * 512)
                    last = hi_lo(product(PS[:, 4 + g % 4, :]), A_hi[:, a_slot, tok], A_lo[:, a_slot, tok],
                                 W_hi[:, slot, cols], W_lo[:, slot, cols], True, True)
                    last.then_inc(down_mm, 1)

            def ready(n, tile, halves=2):
                pe.wait_ge(w_lo, n + 1)
                pe.wait_ge(a_lo, 2 * tile + halves)

            def branches(m, n, slot, down_unit, down_slot, a_slot):
                pe.wait_ge(w_lo, n + 1)
                hi, lo = w_tile(W_hi, slot), w_tile(W_lo, slot)
                for b in range(2):
                    if b:
                        ready(down_unit, m - 1)
                    for h in range(2):
                        tokens = slice(h * HALF, (h + 1) * HALF)
                        pe.wait_ge(mix_v, 6 * (m - 1) + (1, 2, 3, 5)[2 * b + h])
                        for i in range(4):
                            k = 4 * b + i
                            last = hi_lo(product(PS[:, 2 * b + h, :]), hi[:, k, :], lo[:, k, :],
                                         actT_hi[:, k, tokens], actT_lo[:, k, tokens], i == 0, i == 3)
                            if i == 3:
                                last.then_inc(br_mm, 1)
                            if b:
                                g = 8 * h + 2 * i
                                down(down_slot, a_slot, m - 1, (g, g + 1))

            pe.wait_ge(w_lo, U_MERGE + 1)
            pe.wait_ge(tile_out, 2 + 2 * (U_MERGE - U_FOX))
            hi, lo = w_tile(W_hi, 0), w_tile(W_lo, 0)
            for b in range(2):
                for h in range(2):
                    tokens = slice(h * HALF, (h + 1) * HALF)
                    for i in range(4):
                        k = 4 * b + i
                        pe.wait_ge(act_lo, 2 * KT + 8 * b + 4 * h + i + 1)
                        last = hi_lo(product(PS[:, 2 * b + h, :]), hi[:, k, :], lo[:, k, :],
                                     actT_hi[:, k, tokens], actT_lo[:, k, tokens], i == 0, i == 3)
                    last.then_inc(br_mm, 1)
                    if b == 0 and h == 0:
                        turn_y((6, 7))
            pe.wait_ge(br_mm, 4)
            pe.sem_inc(down_mm, DOWN_START)
            with pe.Fori(0, 2) as r:
                for i in range(3):
                    n = U_MERGE + 2 * i + 1
                    branches(3 * r + i + 1, n + 6 * r, n % RING, n + 6 * r + 1, (n + 1) % RING, i)
            n = U_MERGE + 13
            branches(KT - 1, n, n % RING, n + 1, (n + 1) % RING, 0)
            ready(n + 2, KT - 1, 1)
            down((n + 2) % RING, 1, KT - 1, range(8))
            ready(n + 2, KT - 1)
            down((n + 2) % RING, 1, KT - 1, range(8, 12))
            pe.wait_ge(scaled, 15)
            pe.wait_ge(mix_v, 6 * KT)
            norm_turn(1, 0, range(4), X, scale)
            down((n + 2) % RING, 1, KT - 1, range(12, 16))
            norm_turn(1, 0, range(4, KT), X, scale)
            pe.wait_ge(scaled, 20)
            norm_turn(1, 1, range(4), X, scale)

            def gate_up(m, n, slot, a_slot):
                for b in range(2):
                    pe.wait_ge(w_lo, n + b + 1)
                    if b:
                        ready(n + 2, KT + m - 1)
                    for h in range(2):
                        pe.wait_ge((glu_a, glu_b)[b], 2 * m + h - 1)
                        for i in range(KT):
                            last = dense(2 * b + h, (slot + b) % RING, h, 3 * i, 3 * i + 3)
                            if i == KT - 1:
                                last.then_inc(gu_mm, 1)
                            if b:
                                down((slot + 2) % RING, a_slot, KT + m - 1, (8 * h + i,))

            pe.wait_ge(act_lo, 5 * KT)
            pe.wait_ge(w_lo, U_FFN + 1)
            for i in range(4):
                norm_turn(1, 1, (4 + i,), X, scale)
                last = dense(0, U_FFN % RING, 0, 6 * i, 6 * i + 6)
            last.then_inc(gu_mm, 1)
            pe.wait_ge(act_lo, 6 * KT)
            dense(1, U_FFN % RING, 1, 0, 24).then_inc(gu_mm, 1)
            pe.wait_ge(w_lo, U_FFN + 2)
            for h in range(2):
                dense(2 + h, (U_FFN + 1) % RING, h, 0, 24).then_inc(gu_mm, 1)
            with pe.Fori(0, FT // 2 - 1) as r:
                for i in range(2):
                    n = U_FFN + 3 * i + 2
                    gate_up(2 * r + i + 1, n + 6 * r, n % RING, i)
            n = U_FFN + 3 * (FT - 2) + 2
            gate_up(FT - 1, n, n % RING, 0)
            ready(n + 3, KT + FT - 1, 1)
            down((n + 3) % RING, 1, KT + FT - 1, range(8))
            ready(n + 3, KT + FT - 1)
            down((n + 3) % RING, 1, KT + FT - 1, range(8, 16))

        @block.scalar
        def _(act):
            def split(n, rounds=0):
                slot = n % RING
                act.wait_ge(w_raw[slot], 16 * raw_count(n, rounds))
                act.activation(W_hi[:, slot, :], W_raw[:, slot, :], ACT.Copy).then_inc(w_hi, 1)

            def squares(round_, tiles, arrived, src, dst):
                for t in tiles:
                    arrived(t)
                    if t >= 4:
                        act.wait_ge(sumsq, TT * round_ + t - 3)
                    act.activation(dst[:, t % 4, :], src[:, t, :], ACT.Square,
                                   accum_out=stat[:, 0, t:t + 1]).then_inc(sumsq, 1)
                    if t % 4 == 3:
                        act.wait_ge(sumsq, TT * round_ + t + 1)
                        act.activation(stat[:, 1, t - 3:t + 1], stat[:, 0, t - 3:t + 1], ACT.Sqrt,
                                       bias=eps_col[:], scale=1.0 / D_MODEL).then_inc(rooted, 1)

            def norm_hi(round_, h, tiles):
                for k in tiles:
                    act.wait_ge(turned, 3 * KT * round_ + h * KT + k + 1)
                    act.activation(actT_hi[:, k, h * HALF:(h + 1) * HALF], PS[:, norm_bank(round_, h, k), :], ACT.Copy,
                                   scale=g_cols[:, round_, k:k + 1]).then_inc(act_hi, 1)

            act.wait_ge(cols_set, 1)
            act.activation(stat[:, 1, 0:1], eps_col[:], ACT.Sqrt).then_inc(table_in, 1)
            act.wait_ge(table_in, 1)
            def came(t):
                act.wait_ge(x_in[t], 16)

            squares(0, range(6), came, X0, dump0)
            act.wait_ge(gains_in, 32)
            norm_hi(0, 0, range(2))
            squares(0, range(6, TT), came, X0, dump0)
            norm_hi(0, 0, range(2, 6))
            act.wait_ge(gate_raw, 48)
            act.activation(W_hi[:, 0, :], W_raw[:, 0, :], ACT.Copy).then_inc(w_hi, 1)
            norm_hi(0, 0, range(6, KT))
            split(1)
            norm_hi(0, 1, range(KT))
            split(2)

            rows = slice(ROW_FB, ROW_FB + ML_HEADS)
            act.wait_ge(gate_v, 2)
            act.activation(u_m[rows, 0, :], z[ROW_IB:ROW_IB + ML_HEADS, :], ACT.Copy).then_inc(gate_a, 1)
            act.activation(soft[:], z[:], ACT.Abs).then_inc(gate_a, 1)
            act.wait_ge(gate_a, 2)
            act.activation(soft[:], soft[:], ACT.Exp, scale=-1.0).then_inc(gate_a, 1)
            act.wait_ge(gate_a, 3)
            act.activation(soft[:], soft[:], ACT.Ln, bias=1.0).then_inc(gate_a, 1)
            act.wait_ge(gate_mm, 2)
            split(3)
            act.wait_ge(gate_v, 16)
            act.activation(wi_em[rows, 0, :], wi_em[rows, 0, :], ACT.Exp).then_inc(gate_a, 1)
            act.activation(wi_em[rows, 1, :], wi_em[rows, 1, :], ACT.Exp, scale=-1.0).then_inc(gate_a, 1)
            for sign in range(2):
                act.activation(c_parts[:, 2 * sign, :], csum[0:FOX_HEADS, :], ACT.Copy,
                               scale=(1.0, -1.0)[sign]).then_inc(gate_a, 1)

            act.sem_inc(tile_out, 2)
            for n in (4, 5, 6):
                act.wait_ge(w_used, n - 3)
                split(n)
            for t in range(TT):
                act.wait_ge(val_mm, t + 1)
                act.activation(V[:, t, :], PS[:, t, :], ACT.Copy).then_inc(val_out, 1)
            split(7)
            for n in (8, 9, 10):
                act.wait_ge(w_used, n - 4)
                split(n)
            for t in range(TT):
                act.wait_ge(val_mm, TT + t + 1)
                if t >= 2:
                    act.wait_ge(stored[t % 2], 16 * (t // 2))
                act.activation(stage[:, t % 2, 0:ML_WIDTH], PS[:, t, :], ACT.Copy).then_inc(val_out, 1)

            act.wait_ge(rows_out, 48)
            with act.Fori(0, PAIRS) as p:
                for step in fox_steps:
                    kind, *at = step
                    if kind == "unit":
                        j, = at
                        act.wait_ge(tile_mm, 2 + 2 * FOX_UNITS * p + 2 * j)
                        split(U_FOX + j + 2, FOX_UNITS // RING * p)
                    elif kind == "half":
                        j, h = at
                        n = 2 * FOX_UNITS * p + 2 * j + h
                        tokens = slice(h * HALF, (h + 1) * HALF)
                        if j < 2:
                            if j or h:
                                act.wait_ge(mean_mm, 4 * p + 2 * j + h)
                            act.wait_ge(tile_mm, n + 3)
                            act.activation(sq[:], PS[:, h, :], ACT.Square).then_inc(sq_set, 1)
                            act.activation(qk_raw[:, j, tokens], PS[:, h, :], ACT.Copy).then_inc(tile_out, 1)
                        elif j < 4:
                            if j == 3 and h == 0:
                                act.wait_ge(conv_step, 8 * p + 4)
                            act.wait_ge(tile_mm, n + 3)
                            act.activation(conv_in[:, TAPS - 1 + h * HALF:TAPS - 1 + (h + 1) * HALF],
                                           PS[:, h, :], ACT.Copy).then_inc(tile_out, 1)
                        else:
                            if h == 0:
                                act.wait_ge(stored[j % 2], 16 * (4 + 2 * p + 1))
                            act.wait_ge(tile_mm, n + 3)
                            act.activation(stage[:, j % 2, tokens], PS[:, h, :], ACT.Tanh,
                                           scale=0.5).then_inc(tile_out, 1)
                    elif kind == "norm":
                        x_, h = at
                        if x_ or h:
                            act.wait_ge(qk_norm, 4 * p + 2 * x_ + h)
                        act.wait_ge(mean_mm, 4 * p + 2 * x_ + h + 1)
                        act.activation(root[:], PS[:, 2 + 2 * x_ + h, :], ACT.Sqrt,
                                       bias=eps_col[:]).then_inc(root_set, 1)
                    elif kind == "parts":
                        x_, h = at
                        tokens = slice(h * HALF, (h + 1) * HALF)
                        act.wait_ge(qk_norm, 4 * p + 2 * x_ + h + 1)
                        upper, lower = slice(0, FOX_DIM), slice(FOX_DIM, P)
                        for dst, to, frm in ((QHL, upper, upper), (QHL, lower, lower), (QHC, upper, upper),
                                             (QHC, lower, lower)) if x_ == 0 else \
                                            ((KHH, upper, upper), (KHH, lower, lower), (KHH, lower, upper),
                                             (KHH, upper, lower)):
                            act.activation(dst[to, int(frm is lower), tokens], qk_raw[frm, x_, tokens],
                                           ACT.Copy).then_inc(qk_hi, 1)
                    elif kind == "silu":
                        j, = at
                        act.wait_ge(stored[j % 2], 16 * (4 + 2 * p))
                        act.wait_ge(conv_step, 4 * (2 * p + j - 2) + 4)
                        act.activation(stage[:, j % 2, :], conv_acc[:], ACT.Tanh, scale=0.5).then_inc(tanh_set, 1)
                    elif kind == "turn" and at[1] == 0:
                        s = at[0]
                        n = min(4, s // 2 + 1)
                        if s >= 2:
                            act.wait_ge(y_mm, 2 * TT * p + s - 1)
                        act.wait_ge(prob_turn, FILLS * p + turn_fill(s, 0) + 1)
                        act.activation(probT[s % 2][:, 0:n, :].rearrange("p b q -> p (b q)"), PS[:, 6, 0:n * P],
                                       ACT.Copy).then_inc(probT_set[0], 1)
                    elif kind == "exp":
                        s, = at
                        length = (s // 2 + 1) * P
                        if s >= 2:
                            act.wait_ge(prob_turn, FILLS * p + turn_fill(s - 2, int((s - 2) // 2 >= 4)) + 1)
                            act.wait_ge(rinv_set, 2 * TT * p + s - 1)
                        act.wait_ge(nmax_set, 2 * TT * p + s + 1)
                        act.activation(prob[:, s % 2, 0:length], score_row(s), ACT.Exp, bias=nmax[:, s % 2:s % 2 + 1],
                                       accum_out=psumrow[:, s % 2:s % 2 + 1]).then_inc(prob_set, 1)

            with act.Fori(0, ML_STEPS) as q:
                for step in ml_steps:
                    kind, *at = step
                    if kind == "unit":
                        j, = at
                        act.wait_ge(tile_mm, 2 + 2 * FOX_UNITS * PAIRS + 2 * ML_UNITS * q + 2 * j)
                        split(U_ML + j + 2, ML_UNITS // RING * q)
                    elif kind == "half":
                        j, h = at
                        n = 2 * FOX_UNITS * PAIRS + 2 * ML_UNITS * q + 2 * j + h
                        if h == 0:
                            act.wait_ge(stored[j % 2], 16 * ml_stores(q, j))
                        act.wait_ge(tile_mm, n + 3)
                        act.activation(stage[:, j % 2, h * HALF:(h + 1) * HALF], PS[:, h, :], ACT.Tanh,
                                       scale=0.5).then_inc(tile_out, 1)
                    elif kind == "kq":
                        c, = at
                        act.wait_ge(ml_v, ml_at(q, "kq", c, 2))
                        act.activation(decay[:], decay[:], ACT.Exp).then_inc(decay_set, 1)
                    elif kind == "out":
                        c, = at
                        act.wait_ge(ml_v, ml_at(q, "out", c, 5))
                        act.activation(hstat[:, 4, :], hstat[:, 3, :], ACT.Sqrt, bias=eps_col[:],
                                       scale=1.0 / ML_DIM).then_inc(ml_root, 1)

            for b in range(2):
                for h in range(2):
                    for i in range(4):
                        n = 4 * h + i
                        if b == 0:
                            act.wait_ge(turned, 2 * KT + n + 1)
                            src = PS[:, Y_BANKS[n], :]
                        else:
                            src = YB[:, i, h * HALF:(h + 1) * HALF]
                        act.activation(actT_hi[:, 4 * b + i, h * HALF:(h + 1) * HALF], src,
                                       ACT.Copy).then_inc(act_hi, 1)
                if b == 0:
                    act.wait_ge(tile_mm, 2 + 2 * (U_MERGE - U_FOX))
                    split(U_MERGE + 2)
                    act.wait_ge(ml_v, ML_SETUP + ML_STEPS * ML_V_STEPS)

            def merge_hi(m, a_slot, h):
                act.wait_ge(mix_v, 6 * m + 4 + 2 * h)
                act.activation(A_hi[:, a_slot, h * HALF:(h + 1) * HALF], sg[:, 0, h * HALF:(h + 1) * HALF],
                               ACT.Copy).then_inc(a_hi, 1)

            act.wait_ge(stored[0], 16 * ml_stores(ML_STEPS, 0))
            act.wait_ge(stored[1], 16 * ml_stores(ML_STEPS, 1))
            merge_hi(0, 0, 0)
            merge_hi(0, 0, 1)
            with act.Fori(0, 2) as r:
                for i in range(3):
                    m = 3 * r + i + 1
                    act.wait_ge(down_mm, DOWN_START + 16 * (m - 1))
                    split(U_MERGE + 2 * i + 3, 2 * r)
                    merge_hi(m, (i + 1) % 3, 0)
                    act.wait_ge(br_mm, 4 * (m + 1))
                    split(U_MERGE + 2 * i + 4, 2 * r)
                    merge_hi(m, (i + 1) % 3, 1)
            act.wait_ge(down_mm, DOWN_START + 16 * (KT - 2))
            split(U_MERGE + 15)
            merge_hi(KT - 1, 1, 0)
            act.wait_ge(br_mm, 4 * KT)
            split(U_FFN)
            merge_hi(KT - 1, 1, 1)
            act.wait_ge(down_mm, DOWN_START + 16 * (KT - 1))
            split(U_FFN + 1)

            def added(t):
                act.wait_ge(x_add, X_START + 16 * (KT - 1) + 2 * t + 2)

            act.activation(stat[:, 1, 0:1], eps_col[:], ACT.Sqrt).then_inc(table_in, 1)
            act.wait_ge(table_in, 2)
            squares(1, range(6), added, X, dump)
            norm_hi(1, 0, range(4))
            squares(1, range(6, TT), added, X, dump)
            norm_hi(1, 0, range(4, KT))
            norm_hi(1, 1, range(KT))

            def gate_tanh(m, h):
                act.wait_ge(gu_mm, 4 * m + h + 1)
                act.activation(sg[:, 0, h * HALF:(h + 1) * HALF], PS[:, h, :], ACT.Tanh,
                               scale=0.5).then_inc(tanh_g, 1)

            def glu_hi(m, h, a_slot):
                act.wait_ge(glu_b, 2 * m + h + 1)
                act.activation(A_hi[:, a_slot, h * HALF:(h + 1) * HALF], sg[:, 1, h * HALF:(h + 1) * HALF],
                               ACT.Copy).then_inc(a_hi, 1)

            act.wait_ge(down_mm, DOWN_START + 16 * KT)
            split(U_FFN + 2)
            for h in range(2):
                gate_tanh(0, h)
            for h in range(2):
                glu_hi(0, h, 0)

            def ffn_tile(m, n, rounds, a_slot):
                act.wait_ge(gu_mm, 4 * m)
                split(n + 1, rounds)
                act.wait_ge(down_mm, DOWN_START + 16 * (KT + m - 1))
                split(n + 2, rounds)
                for h in range(2):
                    gate_tanh(m, h)
                act.wait_ge(gu_mm, 4 * m + 2)
                split(n + 3, rounds)
                for h in range(2):
                    glu_hi(m, h, a_slot)

            with act.Fori(0, FT // 2 - 1) as r:
                for i in range(2):
                    at = 3 * i + 2
                    ffn_tile(2 * r + i + 1, U_FFN + at, 2 * r, (i + 1) % 2)
            at = U_FFN + 3 * (FT - 2) + 2
            ffn_tile(FT - 1, at, 0, 1)

        @block.vector
        def _(dve):
            def split(n, rounds=0):
                slot = n % RING
                dve.wait_ge(w_hi, n + RING * rounds + 1)
                dve.tensor_tensor(W_lo[:, slot, :], W_raw[:, slot, :], W_hi[:, slot, :].bitcast(F32),
                                  ALU.subtract).then_inc(w_lo, 1)

            def scale_diagonals(round_, h, scales):
                dve.wait_ge(rooted, 2 * round_ + h + 1)
                dve.reciprocal(stat[:, 2, 4 * h:4 * h + 4], stat[:, 1, 4 * h:4 * h + 4]).then_inc(scaled, 1)
                dve.wait_ge(scaled, 10 * round_ + 5 * h + 1)
                for t in range(4 * h, 4 * h + 4):
                    dve.tensor_scalar(scales[:, t, :], ident[:], stat[:, 2, t:t + 1], None,
                                      ALU.mult).then_inc(scaled, 1)

            def norm_lo(round_, h, tiles):
                for k in tiles:
                    tokens = slice(h * HALF, (h + 1) * HALF)
                    dve.wait_ge(act_hi, 4 * KT * round_ + h * KT + k + 1)
                    dve.scalar_tensor_tensor(actT_lo[:, k, tokens], PS[:, norm_bank(round_, h, k), :],
                                             g_cols[:, round_, k:k + 1], actT_hi[:, k, tokens].bitcast(F32),
                                             ALU.mult, ALU.subtract).then_inc(act_lo, 1)

            dve.memset(eps_col[:], EPS).then_inc(cols_set, 1)
            dve.memset(conv_in[:, 0:TAPS - 1], 0.0).then_inc(cols_set, 1)
            dve.memset(head_mean[:], 0.0).then_inc(cols_set, 1)
            dve.wait_ge(cols_set, 3)
            for hd in range(2):
                at = slice(hd * FOX_DIM, (hd + 1) * FOX_DIM)
                dve.memset(head_mean[at, at], 1.0 / FOX_DIM).then_inc(cols_set, 1)

            dve.wait_ge(const_set, 8)
            scale_diagonals(0, 0, scale0)
            norm_lo(0, 0, range(2))
            scale_diagonals(0, 1, scale0)
            norm_lo(0, 0, range(2, KT))
            norm_lo(0, 1, range(KT))
            dve.wait_ge(const_in, 16 * N_CONST)
            dve.tensor_scalar(g_qk[:, 0:1], g_qk[:, 0:1], FOX_DIM ** -0.5, None, ALU.mult).then_inc(cols_set, 1)
            dve.tensor_scalar(g_ml[:], g_ml[:], 0.5, None, ALU.mult).then_inc(cols_set, 1)

            ml = slice(ROW_FB, ROW_FB + ML_HEADS)
            fx = slice(ROW_FA, ROW_FA + FOX_HEADS)
            for h in range(2):
                dve.wait_ge(gate_mm, h + 1)
                dve.tensor_scalar(z[:, h * HALF:(h + 1) * HALF], PS[0:GATE_ROWS, h, :], gate_bias[:], None,
                                  ALU.add).then_inc(gate_v, 1)
            dve.memset(keep[:], 1.0).then_inc(gate_v, 1)
            dve.memset(shift[ml, :], 0.0).then_inc(gate_v, 1)
            dve.memset(m_prev[ml, :], 0.0).then_inc(gate_v, 1)
            dve.wait_ge(gate_v, 3)
            starts = keep[ml, :].rearrange("p (c t) -> p c t", t=CHUNK)[:, :, 0:1]
            dve.memset(starts, 0.0).then_inc(gate_v, 1)
            dve.wait_ge(w_lo, RING)
            split(3)
            dve.wait_ge(gate_a, 4)
            dve.scalar_tensor_tensor(logs[:], z[:], 0.0, soft[:], ALU.min, ALU.subtract).then_inc(gate_v, 1)
            dve.wait_ge(gate_v, 7)
            dve.tensor_tensor_scan(csum[fx, :], keep[fx, :], logs[fx, :], 0.0, ALU.mult, ALU.add).then_inc(gate_v, 1)
            dve.tensor_tensor_scan(csum[ml, :], keep[ml, :], logs[ml, :], 0.0, ALU.mult, ALU.add).then_inc(gate_v, 1)
            dve.wait_ge(gate_v, 9)
            u_row, m_row = u_m[ml, 0, :], u_m[ml, 1, :]
            dve.tensor_tensor(u_row, u_row, csum[ml, :], ALU.subtract).then_inc(gate_v, 1)

            def ends(row):
                return row.rearrange("p (c t) -> p c t", t=CHUNK)[:, 0:CHUNKS - 1, CHUNK - 1]

            dve.tensor_copy(shift[ml, :].rearrange("p (c t) -> p c t", t=CHUNK)[:, 1:CHUNKS, 0],
                            ends(csum[ml, :])).then_inc(gate_v, 1)
            dve.wait_ge(gate_v, 11)
            dve.tensor_tensor_scan(m_row, shift[ml, :], u_row, 0.0, ALU.add, ALU.max).then_inc(gate_v, 1)
            dve.wait_ge(gate_v, 12)
            dve.tensor_tensor(m_prev[ml, 1:CHUNKS], ends(m_row), ends(csum[ml, :]), ALU.add).then_inc(gate_v, 1)
            dve.tensor_scalar(negs[ml, :], m_row, -1.0, None, ALU.mult).then_inc(gate_v, 1)
            dve.wait_ge(gate_v, 13)
            dve.tensor_tensor(wi_em[ml, 0, :].rearrange("p (c t) -> p c t", t=CHUNK),
                              m_prev[ml, :].unsqueeze(2).to_broadcast([ML_HEADS, CHUNKS, CHUNK]),
                              m_row.rearrange("p (c t) -> p c t", t=CHUNK), ALU.subtract).then_inc(gate_v, 1)
            dve.tensor_tensor(wi_em[ml, 1, :], csum[ml, :], m_row, ALU.add).then_inc(gate_v, 1)

            dve.wait_ge(gate_a, 8)
            c_hi = c_parts[:, 0, :].bitcast(F32)
            dve.tensor_tensor(c_parts[:, 1, :], csum[fx, :], c_hi, ALU.subtract).then_inc(gate_v, 1)
            dve.tensor_tensor(c_parts[:, 3, :], c_hi, csum[fx, :], ALU.subtract).then_inc(gate_v, 1)

            for n in range(4, 8):
                split(n)
            dve.wait_ge(gate_turn, 1)
            cols = CHUNKS * ML_HEADS
            dve.tensor_copy(uT[:].rearrange("p c h -> p (c h)"), PS[:, 7, 0:cols]).then_inc(gate_out, 1)
            dve.tensor_copy(emT[:].rearrange("p c h -> p (c h)"), PS[:, 7, cols:2 * cols]).then_inc(gate_out, 1)
            for n in range(8, 11):
                split(n)
            dve.wait_ge(rows_out, 48)
            for i, rows_of in enumerate((QHC, KLC)):
                whole = rows_of[:].bitcast(F32)
                dve.memset(whole[FOX_DIM:FOX_DIM + 4, 0, :], 1.0).then_inc(ones_set, 1)
                dve.memset(whole[0:FOX_DIM, 1, :], 0.0).then_inc(ones_set, 1)
                dve.wait_ge(ones_set, 3 * i + 2)
                dve.memset(whole[0:4, 1, :], 1.0).then_inc(ones_set, 1)

            with dve.Fori(0, PAIRS) as p:
                for step in fox_steps:
                    kind, *at = step
                    if kind == "half":
                        j, h = at
                        n = 2 * FOX_UNITS * p + 2 * j + h
                        if h == 0 or j < 4:
                            continue
                        dve.wait_ge(tile_out, n + 3)
                        if j == 4:
                            dve.tensor_scalar(stage[:, j % 2, :], stage[:, j % 2, :], 1.0, g_ml[:, bass.ds(p, 1)],
                                              ALU.add, ALU.mult).then_inc(tile_set, 1)
                        else:
                            dve.tensor_scalar(stage[:, j % 2, :], stage[:, j % 2, :], 0.5, 0.5, ALU.mult,
                                              ALU.add).then_inc(tile_set, 1)
                    elif kind == "conv":
                        j, n = at
                        tile = bass.ds(p + (j - 2) * ML_HEADS, 1)
                        tap = TAPS - 1 - n
                        if n == 0:
                            dve.wait_ge(tile_out, 2 * FOX_UNITS * p + 2 * j + 4)
                            dve.tensor_scalar(conv_acc[:], conv_in[:, tap:tap + SEQ], taps[:, tile, tap].opt(),
                                              taps[:, tile, TAPS].opt(), ALU.mult, ALU.add).then_inc(conv_step, 1)
                        else:
                            dve.wait_ge(conv_step, 4 * (2 * p + j - 2) + n)
                            dve.scalar_tensor_tensor(conv_acc[:], conv_in[:, tap:tap + SEQ],
                                                     taps[:, tile, tap].opt(), conv_acc[:], ALU.mult,
                                                     ALU.add).then_inc(conv_step, 1)
                    elif kind == "norm":
                        x_, h = at
                        tokens = slice(h * HALF, (h + 1) * HALF)
                        dve.wait_ge(root_set, 4 * p + 2 * x_ + h + 1)
                        dve.reciprocal(root[:], root[:]).then_inc(inv_set, 1)
                        dve.wait_ge(inv_set, 4 * p + 2 * x_ + h + 1)
                        dve.scalar_tensor_tensor(qk_raw[:, x_, tokens], qk_raw[:, x_, tokens], g_qk[:, x_:x_ + 1],
                                                 root[:], ALU.mult, ALU.mult).then_inc(qk_norm, 1)
                    elif kind == "parts":
                        x_, h = at
                        tokens = slice(h * HALF, (h + 1) * HALF)
                        for hd in range(2):
                            rows = slice(hd * FOX_DIM, (hd + 1) * FOX_DIM)
                            other = slice((1 - hd) * FOX_DIM, (2 - hd) * FOX_DIM)
                            hi = (QHL, KHH)[x_][rows, hd, tokens].bitcast(F32)
                            dst = KLC[rows, hd, tokens] if x_ else QHL[other, hd, tokens]
                            dve.wait_ge(qk_hi, 16 * p + 8 * x_ + 4 * h + hd + 1)
                            dve.tensor_tensor(dst, qk_raw[rows, x_, tokens], hi,
                                              ALU.subtract).then_inc(qk_set, 1)
                    elif kind == "silu":
                        j, = at
                        n = 2 * p + j - 2
                        dve.wait_ge(tanh_set, n + 1)
                        dve.scalar_tensor_tensor(stage[:, j % 2, :], stage[:, j % 2, :], 1.0, conv_acc[:], ALU.add,
                                                 ALU.mult).then_inc(conv_mul, 1)
                        dve.wait_ge(conv_mul, n + 1)
                        dve.tensor_scalar(stage[:, j % 2, :], stage[:, j % 2, :],
                                          0.5 if j == 2 else 0.5 * ML_DIM ** -0.5, None,
                                          ALU.mult).then_inc(tile_set, 1)
                    elif kind == "scores":
                        s, = at
                        dve.wait_ge(score_mm, 2 * TT * p + s + 2)
                        dve.tensor_reduce(nmax[:, s % 2:s % 2 + 1], score_row(s), AX_X, ALU.max,
                                          negate=True).then_inc(nmax_set, 1)
                    elif kind == "turn":
                        s, part = at
                        n = s // 2 + 1 - 4
                        if part == 0:
                            if s >= 2:
                                dve.wait_ge(y_set, 2 * TT * p + s - 1)
                            dve.wait_ge(prob_set, 2 * TT * p + s + 1)
                            dve.reciprocal(rinv[:, s % 2:s % 2 + 1],
                                           psumrow[:, s % 2:s % 2 + 1]).then_inc(rinv_set, 1)
                        else:
                            dve.wait_ge(y_mm, 2 * TT * p + s - 1)
                            dve.wait_ge(prob_turn, FILLS * p + turn_fill(s, 1) + 1)
                            dve.tensor_copy(probT[s % 2][:, 4:4 + n, :].rearrange("p b q -> p (b q)"),
                                            PS[:, 6, 0:n * P]).then_inc(probT_set[1], 1)
                    elif kind == "values":
                        s, = at
                        i, hd = divmod(s, 2)
                        n = 2 * TT * p + s
                        dve.wait_ge(rinv_set, n + 1)
                        dve.wait_ge(y_mm, n + 1)
                        dve.tensor_scalar(Y[:, i, bass.ds(p * P + hd * FOX_DIM, FOX_DIM)], PS[:, 7, 0:FOX_DIM],
                                          rinv[:, hd:hd + 1], None, ALU.mult).then_inc(y_set, 1)

            dve.wait_ge(w_lo, U_ML + 2)
            for c in range(2):
                dve.memset(vc[c][:, :, ML_DIM:ML_DIM + 1], 1.0).then_inc(ml_v, 1)
            dve.memset(state[:].rearrange("p h n -> p (h n)"), 0.0).then_inc(ml_v, 1)
            with dve.Fori(0, ML_STEPS) as q:
                for step in ml_steps:
                    kind, *at = step
                    if kind == "unit":
                        j, = at
                        split(U_ML + j + 2, ML_UNITS // RING * q)
                        continue
                    if kind == "half":
                        j, h = at
                        if h:
                            dve.wait_ge(tile_out, 2 * FOX_UNITS * PAIRS + 2 * ML_UNITS * q + 2 * j + h + 3)
                            dve.tensor_scalar(stage[:, j % 2, :], stage[:, j % 2, :], 0.5, 0.5, ALU.mult,
                                              ALU.add).then_inc(tile_set, 1)
                        continue
                    if kind == "dense":
                        continue
                    c, = at
                    chunk = bass.ds(2 * q + c, 1)

                    def step_done(n, kind=kind, c=c):
                        dve.wait_ge(ml_v, ml_at(q, kind, c, n))

                    def by_head(cols):
                        return cols.unsqueeze(2).to_broadcast([P, ML_HEADS, CHUNK])

                    if kind == "kq":
                        dve.wait_ge(chunk_in[3][c], 16 * (q + 1))
                        dve.tensor_tensor(decay[:], m_rows[c][:, 0, :, :],
                                          mask_ml[:].unsqueeze(1).to_broadcast([P, ML_HEADS, CHUNK]),
                                          ALU.add).then_inc(ml_v, 1)
                        step_done(1)
                        u_cols = uT[:, chunk, :].rearrange("p a h -> p (a h)")
                        dve.tensor_tensor(decay[:], decay[:], by_head(u_cols), ALU.add).then_inc(ml_v, 1)
                        dve.wait_ge(chunk_in[4][c], 16 * (q + 1))
                        dve.wait_ge(chunk_in[0][c], 16 * (q + 1))
                        dve.tensor_tensor(qs[:], qc[c][:], m_rows[c][:, 1, :, :], ALU.mult).then_inc(ml_v, 1)
                        dve.wait_ge(decay_set, 2 * q + c + 1)
                        dve.wait_ge(kq_mm, 2 * q + c + 1)
                        dve.tensor_tensor(sw[:], PS[:, 2, :].rearrange("p (h t) -> p h t", h=ML_HEADS), decay[:],
                                          ALU.mult).then_inc(ml_v, 1)
                        dve.tensor_tensor(kw[:], PS[:, 6, :].rearrange("p (h t) -> p h t", h=ML_HEADS),
                                          by_head(decay[:, :, CHUNK - 1]), ALU.mult).then_inc(ml_v, 1)
                    elif kind == "num":
                        dve.wait_ge(num_mm, 2 * q + c + 1)
                        for b in range(2):
                            two = PS[:, 3 + b, 0:258].rearrange("p (h n) -> p h n", h=2)
                            dve.scalar_tensor_tensor(
                                hstat[:, 0, 2 * b:2 * b + 2], two[:, :, ML_DIM], -1.0,
                                emT[:, chunk, 2 * b:2 * b + 2].rearrange("p a h -> p (a h)"), ALU.mult,
                                ALU.max).then_inc(ml_v, 1)
                        step_done(2)
                        for b in range(2):
                            two = PS[:, 3 + b, 0:258].rearrange("p (h n) -> p h n", h=2)
                            den = hstat[:, 0, 2 * b:2 * b + 2]
                            dve.tensor_tensor(den, two[:, :, ML_DIM], den, ALU.max).then_inc(ml_v, 1)
                        step_done(4)
                        dve.reciprocal(hstat[:, 1, :], hstat[:, 0, :]).then_inc(ml_v, 1)
                        step_done(5)
                        for b in range(2):
                            two = PS[:, 3 + b, 0:258].rearrange("p (h n) -> p h n", h=2)
                            dve.tensor_tensor(hb[:, 2 * b:2 * b + 2, :], two[:, :, 0:ML_DIM],
                                              hstat[:, 1, 2 * b:2 * b + 2].unsqueeze(2).to_broadcast([P, 2, ML_DIM]),
                                              ALU.mult).then_inc(ml_v, 1)
                    elif kind == "state":
                        dve.wait_ge(state_mm, 2 * q + c + 1)
                        for h in range(ML_HEADS):
                            dve.scalar_tensor_tensor(
                                state[:, h, :], state[:, h, :], m_rows[c][:, 1, h, CHUNK - 1:CHUNK],
                                PS[:, (5, 7)[h // 2], (h % 2) * 129:(h % 2 + 1) * 129], ALU.mult,
                                ALU.add).then_inc(ml_v, 1)
                    elif kind == "out":
                        step_done(7, "num")
                        dve.tensor_reduce(hstat[:, 2, :], hb[:], AX_X, ALU.add).then_inc(ml_v, 1)
                        step_done(1)
                        dve.tensor_scalar(hstat[:, 2, :], hstat[:, 2, :], -1.0 / ML_DIM, None,
                                          ALU.mult).then_inc(ml_v, 1)
                        step_done(2)
                        dve.tensor_tensor(hb[:], hb[:], by_head(hstat[:, 2, :]), ALU.add).then_inc(ml_v, 1)
                        step_done(3)
                        dve.tensor_tensor(hsq[:], hb[:], hb[:], ALU.mult).then_inc(ml_v, 1)
                        step_done(4)
                        dve.tensor_reduce(hstat[:, 3, :], hsq[:], AX_X, ALU.add).then_inc(ml_v, 1)
                        dve.wait_ge(ml_root, 2 * q + c + 1)
                        dve.reciprocal(hstat[:, 5, :], hstat[:, 4, :]).then_inc(ml_v, 1)
                        step_done(6)
                        dve.tensor_tensor(HN[:].rearrange("p (h n) -> p h n", h=ML_HEADS), hb[:],
                                          by_head(hstat[:, 5, :]), ALU.mult).then_inc(ml_v, 1)
                    elif kind == "flip":
                        dve.wait_ge(flip_mm, 2 * q + c + 1)
                        dve.wait_ge(chunk_in[5][c], 16 * (q + 1))
                        dve.tensor_tensor(YB[:, :, bass.ds(CHUNK * (2 * q + c), CHUNK)],
                                          PS[:, 6, :].rearrange("p (h t) -> p h t", h=ML_HEADS), oc[c][:],
                                          ALU.mult).then_inc(ml_v, 1)

            def piece_lo(b, h, i):
                n = 4 * h + i
                tokens = slice(h * HALF, (h + 1) * HALF)
                src = YB[:, i, tokens] if b else PS[:, Y_BANKS[n], :]
                dve.wait_ge(act_hi, 2 * KT + 8 * b + n + 1)
                dve.tensor_tensor(actT_lo[:, 4 * b + i, tokens], src, actT_hi[:, 4 * b + i, tokens].bitcast(F32),
                                  ALU.subtract).then_inc(act_lo, 1)

            def add_down(tile, groups=range(16)):
                for g in groups:
                    t, c = divmod(g, 2)
                    cols = slice(c * 512, (c + 1) * 512)
                    dve.wait_ge(x_add, X_START + 16 * (tile - 1) + g + 1)
                    dve.wait_ge(down_mm, DOWN_START + 16 * tile + g + 1)
                    dve.tensor_tensor(X[:, t, cols], X[:, t, cols], PS[:, 4 + g % 4, :],
                                      ALU.add).then_inc(x_add, 1)

            def a_lo_part(tile, h, a_slot, src):
                tokens = slice(h * HALF, (h + 1) * HALF)
                dve.wait_ge(a_hi, 2 * tile + h + 1)
                dve.tensor_tensor(A_lo[:, a_slot, tokens], sg[:, src, tokens],
                                  A_hi[:, a_slot, tokens].bitcast(F32), ALU.subtract).then_inc(a_lo, 1)

            def mix_fox(m):
                dve.wait_ge(g_in[0], 16 * (m + 1))
                for h in range(2):
                    tokens = slice(h * HALF, (h + 1) * HALF)
                    dve.wait_ge(br_mm, 4 * m + h + 1)
                    dve.tensor_tensor(sg[:, 0, tokens], PS[:, h, :], sg[:, 0, tokens], ALU.mult).then_inc(mix_v, 1)

            def mix_ml(m, h):
                tokens = slice(h * HALF, (h + 1) * HALF)
                dve.wait_ge(g_in[1], 16 * (m + 1))
                dve.wait_ge(br_mm, 4 * m + h + 3)
                dve.tensor_tensor(sg[:, 1, tokens], PS[:, 2 + h, :], sg[:, 1, tokens], ALU.mult).then_inc(mix_v, 1)
                dve.wait_ge(mix_v, 6 * m + 3 + 2 * h)
                dve.tensor_tensor(sg[:, 0, tokens], sg[:, 0, tokens], sg[:, 1, tokens], ALU.add).then_inc(mix_v, 1)

            def merge_tile(m, a_slot, ahead=0):
                mix_fox(m)
                add_down(m - 1, range(0, 8))
                mix_ml(m, 0)
                add_down(m - 1, range(8, 10))
                a_lo_part(m, 0, a_slot, 0)
                add_down(m - 1, range(10, 16))
                mix_ml(m, 1)
                add_down(m, range(ahead))
                a_lo_part(m, 1, a_slot, 0)

            dve.sem_inc(x_add, X_START)
            for b, h in ((0, 0), (0, 1), (1, 0)):
                for i in range(4):
                    piece_lo(b, h, i)
            mix_fox(0)
            for i in range(4):
                piece_lo(1, 1, i)
            for h in range(2):
                mix_ml(0, h)
                a_lo_part(0, h, 0, 0)
            for t in range(TT):
                dve.wait_ge(x_in[t], 32)
            with dve.Fori(0, 2) as r:
                for i in range(3):
                    merge_tile(3 * r + i + 1, (i + 1) % 3)
            merge_tile(KT - 1, 1, ahead=1)
            add_down(KT - 1, range(1, 12))

            scale_diagonals(1, 0, scale)
            add_down(KT - 1, range(12, 16))
            norm_lo(1, 0, range(4))
            scale_diagonals(1, 1, scale)
            norm_lo(1, 0, range(4, KT))
            norm_lo(1, 1, range(KT))

            def glu_gate(m, h):
                tokens = slice(h * HALF, (h + 1) * HALF)
                dve.wait_ge(tanh_g, 2 * m + h + 1)
                dve.scalar_tensor_tensor(sg[:, 0, tokens], sg[:, 0, tokens], 1.0, PS[:, h, :], ALU.add,
                                         ALU.mult).then_inc(glu_a, 1)

            def glu_up(m, h):
                tokens = slice(h * HALF, (h + 1) * HALF)
                dve.wait_ge(glu_a, 2 * m + h + 1)
                dve.wait_ge(gu_mm, 4 * m + h + 3)
                dve.scalar_tensor_tensor(sg[:, 1, tokens], sg[:, 0, tokens], 0.5, PS[:, 2 + h, :], ALU.mult,
                                         ALU.mult).then_inc(glu_b, 1)

            dve.wait_ge(w_lo, U_FFN + 2)
            split(U_FFN + 2)
            for h in range(2):
                glu_gate(0, h)
            for h in range(2):
                glu_up(0, h)
                a_lo_part(KT, h, 0, 1)

            def ffn_tile(m, n, rounds, a_slot, ahead=0):
                split(n + 1, rounds)
                split(n + 2, rounds)
                for h in range(2):
                    glu_gate(m, h)
                split(n + 3, rounds)
                add_down(KT + m - 1, range(0, 8))
                glu_up(m, 0)
                add_down(KT + m - 1, range(8, 10))
                a_lo_part(KT + m, 0, a_slot, 1)
                add_down(KT + m - 1, range(10, 16))
                glu_up(m, 1)
                add_down(KT + m, range(ahead))
                a_lo_part(KT + m, 1, a_slot, 1)

            with dve.Fori(0, FT // 2 - 1) as r:
                for i in range(2):
                    at = 3 * i + 2
                    ffn_tile(2 * r + i + 1, U_FFN + at, 2 * r, (i + 1) % 2)
            at = U_FFN + 3 * (FT - 2) + 2
            ffn_tile(FT - 1, at, 0, 1, ahead=1)
            add_down(KT + FT - 1, range(1, 16))

        @block.sync
        def _(sp):
            for t in range(4):
                sp.dma_start(X0[:, t, :], x_tiles[t]).then_inc(x_in[t], 16)
            sp.wait_ge(gate_zero, 1)
            w_gates = w_tile(W_raw, 0)
            for row, name, n in ((ROW_FA, "fa", FOX_HEADS), (ROW_IB, "ib", ML_HEADS), (ROW_FB, "fb", ML_HEADS)):
                sp.dma_start(w_gates[:, :, row:row + n], w_cols(w_in, COL[name], n)).then_inc(gate_raw, 16)
            for t in range(4, TT):
                sp.dma_start(X0[:, t, :], x_tiles[t]).then_inc(x_in[t], 16)

            def load(n, slot, src):
                sp.wait_ge(w_lo, n - 2)
                sp.dma_start(w_tile(W_raw, slot), src).then_inc(w_raw[slot], 16)

            for b, name in enumerate(("va", "vb")):
                for u in range(4):
                    n = U_VALUES + 4 * b + u
                    if n >= RING:
                        sp.wait_ge(w_lo, n - 2)
                    src = w_in[2 * u * P:2 * (u + 1) * P, COL[name]:COL[name] + 512]
                    sp.dma_start(W_raw[:, n % RING, :].rearrange("p (k n) -> p k n", k=2),
                                 src.rearrange("(k p) n -> p k n", p=P)).then_inc(w_raw[n % RING], 16)

            with sp.Fori(0, PAIRS) as p:
                for j, name in enumerate(("qa", "ka", "qb", "kb", "ob", "ga")):
                    load(U_FOX + FOX_UNITS * p + j, j % RING, w_cols(w_in, P * p + COL[name]))

            with sp.Fori(0, ML_STEPS) as q:
                for j in range(ML_UNITS):
                    col = COL["ga"] + P * G_IN_FOX + P * ML_UNITS * q + P * j
                    load(U_ML + ML_UNITS * q + j, j % RING, w_cols(w_in, col))

            def load_branches(n, slot, m):
                sp.wait_ge(w_lo, n - 2)
                raw = w_tile(W_raw, slot)
                sp.dma_start(raw[:, 0:4, :], w_cols(w_fox_out, P * m)).then_inc(w_first, 16)
                sp.wait_ge(w_first, 16 * (m + 1))
                sp.dma_start(raw[:, 4:8, :], w_cols(w_mlstm_out, P * m)).then_inc(w_raw[slot], 16)

            def load_rows(n, slot, w, tile):
                sp.wait_ge(w_lo, n - 2)
                sp.dma_start(W_raw[:, slot, :],
                             w.rearrange("(k p) n -> k p n", p=P)[bass.ds(tile, 1)].rearrange("a p n -> (a p) n"))\
                    .then_inc(w_raw[slot], 16)

            load_branches(U_MERGE, 0, 0)
            load_branches(U_MERGE + 1, 1, 1)
            load_rows(U_MERGE + 2, 2, w_o, 0)
            sp.wait_ge(ml_v, ML_SETUP + ML_STEPS * ML_V_STEPS)
            for t in range(TT):
                sp.dma_start(X[:, t, :], x_tiles[t]).then_inc(x_in[t], 16)
            with sp.Fori(0, 2) as r:
                for i in range(3):
                    n = U_MERGE + 6 * r + 2 * i + 3
                    load_branches(n, (2 * i + 3) % RING, 3 * r + i + 2)
                    load_rows(n + 1, (2 * i + 4) % RING, w_o, 3 * r + i + 1)
            load_rows(U_MERGE + 15, 15 % RING, w_o, KT - 1)

            load(U_FFN, U_FFN % RING, w_cols(w_gate, 0))
            load(U_FFN + 1, (U_FFN + 1) % RING, w_cols(w_up, 0))
            with sp.Fori(0, FT // 2 - 1) as r:
                for i in range(2):
                    n = U_FFN + 6 * r + 3 * i + 2
                    slot = U_FFN + 3 * i + 2
                    m = 2 * r + i + 1
                    load(n, slot % RING, w_cols(w_gate, P * m))
                    load(n + 1, (slot + 1) % RING, w_cols(w_up, P * m))
                    load_rows(n + 2, (slot + 2) % RING, w_down, m - 1)
            n = U_FFN + 3 * (FT - 2) + 2
            load(n, n % RING, w_cols(w_gate, P * (FT - 1)))
            load(n + 1, (n + 1) % RING, w_cols(w_up, P * (FT - 1)))
            load_rows(n + 2, (n + 2) % RING, w_down, FT - 2)
            load_rows(n + 3, (n + 3) % RING, w_down, FT - 1)

            for t in range(TT - 1):
                sp.wait_ge(x_add, X_START + 16 * (KT + FT - 1) + 2 * t + 2)
                sp.dma_start(out_tiles[t], X[:, t, :]).then_inc(out_in, 16)
            for c in range(2):
                cols = slice(c * 512, (c + 1) * 512)
                sp.wait_ge(x_add, X_START + 16 * (KT + FT) - 1 + c)
                sp.dma_start(out_tiles[TT - 1][:, cols], X[:, TT - 1, cols]).then_inc(out_in, 16)
            sp.wait_ge(out_in, 16 * (TT + 1))

        @block.gpsimd
        def _(pool):
            def wait(signal, count):
                pool.wait_ge(signal, count)
                pool.sem_inc(transfer_due, 1)

            pool.memset(W_raw[:, 0, :], 0.0).then_inc(gate_zero, 1)
            pool.memset(gate_bias[:], 0.0).then_inc(gate_zero, 1)
            pool.memset(ident[:], 0.0).then_inc(const_set, 1)
            pool.memset(ident_bf[:], 0.0).then_inc(const_set, 1)
            pool.memset(mask_bf[:], 0.0).then_inc(const_set, 1)
            pool.memset(mask_ml[:], 0.0).then_inc(const_set, 1)
            pool.wait_ge(const_set, 4)
            for m in (ident, ident_bf):
                pool.affine_select(out=m[:], in_=m[:], compare_op=ALU.not_equal, fill=1.0, base=0,
                                   pattern=[[-1, P]], channel_multiplier=1).then_inc(const_set, 1)
            pool.affine_select(out=mask_bf[:], in_=mask_bf[:], compare_op=ALU.is_ge, fill=MASKED, base=0,
                               pattern=[[-1, P]], channel_multiplier=1).then_inc(const_set, 1)
            pool.affine_select(out=mask_ml[:], in_=mask_ml[:], compare_op=ALU.is_ge, fill=MASKED, base=0,
                               pattern=[[1, P]], channel_multiplier=-1).then_inc(const_set, 1)

            for i, g in enumerate((g_mix, g_ffn)):
                pool.dma_start(g_cols[:, i, :], g[0].rearrange("(k p) -> p k", p=P),
                               allow_slow_non_contiguous=True).then_inc(gains_in, 16)
            pool.wait_ge(gate_zero, 2)
            consts = (
                [(gate_bias[row:row + n, :], b[0].rearrange("(p a) -> p a", a=1))
                 for row, b, n in ((ROW_FA, b_fox_f, FOX_HEADS), (ROW_IB, b_mlstm_i, ML_HEADS),
                                   (ROW_FB, b_mlstm_f, ML_HEADS))]
                + [(g_qk[hd * FOX_DIM:(hd + 1) * FOX_DIM, i:i + 1], g[0].rearrange("(p a) -> p a", a=1))
                   for i, g in enumerate((g_q_fox, g_k_fox)) for hd in range(2)]
                + [(g_ml[:], g_mlstm_h[0].rearrange("(k p) -> p k", p=P))]
                + [(taps[:, :, tap], conv_w[tap].rearrange("(k p) -> p k", p=P)) for tap in range(TAPS)]
                + [(taps[:, :, TAPS], conv_b[0].rearrange("(k p) -> p k", p=P))])
            assert len(consts) == N_CONST
            for dst, src in consts:
                pool.dma_start(dst, src, allow_slow_non_contiguous=True).then_inc(const_in, 16)

            def split(n, rounds=0):
                slot = n % RING
                pool.wait_ge(w_hi, n + RING * rounds + 1)
                pool.tensor_tensor(W_lo[:, slot, :], W_raw[:, slot, :], W_hi[:, slot, :].bitcast(F32),
                                   ALU.subtract).then_inc(w_lo, 1)

            for n in range(RING):
                split(n)

            rows = slice(ROW_FB, ROW_FB + ML_HEADS)
            pool.wait_ge(gate_a, 8)
            pool.wait_ge(gate_v, 18)
            for dst, src in ((d_c.rearrange("k h n -> h k n"), c_parts[:]),
                             (d_m[0], negs[rows, :]), (d_m[1], wi_em[rows, 0, :])):
                pool.dma_start(dst, src).then_inc(rows_out, 16)

            for t in range(TT):
                pool.wait_ge(val_out, TT + t + 1)
                pool.dma_start(d_v[t], stage[:, t % 2, 0:ML_WIDTH]).then_inc(stored[t % 2], 16)

            def store(dst, slot):
                pool.dma_start(dst, stage[:, slot, :]).then_inc(stored[slot], 16)

            def one(d, at):
                return d[bass.ds(at, 1)].rearrange("a p n -> (a p) n")

            pool.wait_ge(rows_out, 48)
            pool.wait_ge(ones_set, 6)
            def load_c(p):
                wait(score_mm, 2 * TT * p + 1)
                for hd, q_row in enumerate((FOX_DIM, 0)):
                    for i, rows_of in enumerate((QHC, KLC)):
                        rows = slice(q_row + 2 * i, q_row + 2 * i + 2)
                        pool.dma_start(rows_of[rows, hd:hd + 1, :],
                                       d_c[2 * i:2 * i + 2, bass.ds(2 * p + hd, 1), :]).then_inc(c_in[i], 16)

            def store_tile(p, n):
                wait(tile_set, 4 * p + n + 1)
                store(one((d_qk, d_qk, d_ob, d_g)[n], p + ML_HEADS if n == 1 else p), n % 2)

            def load_chunk_mv(n, c):
                tok = bass.ds(CHUNK * n, CHUNK)
                for i in range(2):
                    pool.dma_start(m_rows[c][:, i, :, :], d_m[i, :, tok].partition_broadcast(P))\
                        .then_inc(chunk_in[3 + i][c], 16)
                pool.dma_start(vc[c][:, :, 0:ML_DIM],
                               one(d_v, n).rearrange("p (h n) -> p h n", h=ML_HEADS)).then_inc(chunk_in[2][c], 16)

            def load_chunk_qk(n, c):
                tok = bass.ds(CHUNK * n, CHUNK)
                pool.dma_start(qc[c][:], d_qk[0:ML_HEADS, :, tok].rearrange("h p t -> p h t"))\
                    .then_inc(chunk_in[0][c], 16)
                pool.dma_start(kc[c][:], d_qk[ML_HEADS:2 * ML_HEADS, :, tok].rearrange("h p t -> p h t"))\
                    .then_inc(chunk_in[1][c], 16)

            def load_o(n, c):
                pool.dma_start(oc[c][:], d_ob[:, :, bass.ds(CHUNK * n, CHUNK)].rearrange("h p t -> p h t"))\
                    .then_inc(chunk_in[5][c], 16)

            def fox_pair(p, last):
                load_c(p)
                for step in fox_steps:
                    kind, *at = step
                    if kind == "unit":
                        j, = at
                        split(U_FOX + j + 2, FOX_UNITS // RING * p)
                    elif kind == "silu":
                        j, = at
                        store_tile(p, j - 2)
                        if last and j == 3:
                            load_chunk_mv(0, 0)
                    elif kind == "half" and at[0] >= 4 and at[1] == 1:
                        j = at[0]
                        if last and j == 4:
                            pool.wait_ge(stored[0], 16 * (4 + 2 * PAIRS - 1))
                            pool.wait_ge(stored[1], 16 * (4 + 2 * PAIRS - 1))
                            load_chunk_qk(0, 0)
                        store_tile(p, j - 2)

            pool.wait_ge(w_lo, U_FOX + 2)
            with pool.Fori(0, PAIRS - 1) as p:
                fox_pair(p, False)
            fox_pair(PAIRS - 1, True)

            pool.wait_ge(stored[0], 16 * (4 + 2 * PAIRS))
            load_o(0, 0)
            pool.wait_ge(ml_v, ML_SETUP)
            load_chunk_mv(1, 1)
            load_chunk_qk(1, 1)
            load_o(1, 1)

            def ml_stage(q, more):
                for step in ml_steps:
                    kind, *at = step
                    if kind == "half" and at[1] == 1:
                        j = at[0]
                        wait(tile_set, 4 * PAIRS + ML_UNITS * q + j + 1)
                        store(one(d_g, G_IN_FOX + ML_UNITS * q + j), j % 2)
                    elif kind == "out" and more:
                        c, = at
                        wait(ml_v, ml_at(q, "state", c, 4))
                        load_chunk_mv(2 * q + 2 + c, c)
                        load_chunk_qk(2 * q + 2 + c, c)
                    elif kind == "flip":
                        c, = at
                        wait(ml_v, ml_at(q, "flip", c, 1))
                        if more:
                            load_o(2 * q + 2 + c, c)
                        elif c == 0:
                            pool.wait_ge(stored[0], 16 * ml_stores(ML_STEPS - 1, 0))
                            pool.wait_ge(stored[1], 16 * ml_stores(ML_STEPS - 1, 1))
                            load_g(0)

            def load_g(m):
                for i in range(2):
                    pool.dma_start(sg[:, i, :], one(d_g, m + KT * i)).then_inc(g_in[i], 16)

            with pool.Fori(0, ML_STEPS - 1) as q:
                ml_stage(q, True)
            ml_stage(ML_STEPS - 1, False)

            pool.wait_ge(w_lo, U_MERGE + 2)
            split(U_MERGE + 2)
            pool.wait_ge(stored[0], 16 * ml_stores(ML_STEPS, 0))
            pool.wait_ge(stored[1], 16 * ml_stores(ML_STEPS, 1))

            def merge_tile(m, n, rounds=0):
                wait(a_lo, 2 * m)
                load_g(m)
                split(n + 2, rounds)
                split(n + 3, rounds)

            with pool.Fori(0, 2) as r:
                for i in range(3):
                    merge_tile(3 * r + i + 1, U_MERGE + 2 * i + 1, 2 * r)
            merge_tile(KT - 1, U_MERGE + 13)

            split(U_FFN + 1)


_INS = ["x", "g_mix", "w_in", "b_fox_f", "g_q_fox", "g_k_fox", "conv_w", "conv_b", "b_mlstm_i", "b_mlstm_f",
        "g_mlstm_h", "w_fox_out", "w_mlstm_out", "w_o", "g_ffn", "w_gate", "w_up", "w_down"]


def kernel(**inputs):
    import concourse.bacc as bacc
    from concourse.bass_utils import run_bass_kernel_spmd

    nc = bacc.Bacc("TRN2", target_bir_lowering=False, num_devices=1)
    arrays, args = {}, []
    for name in _INS:
        a = np.ascontiguousarray(inputs[name])
        arrays[f"in_{name}"] = a
        args.append(nc.dram_tensor(f"in_{name}", a.shape, F32, kind="ExternalInput").ap())
    out = nc.dram_tensor("out", (1, SEQ, D_MODEL), F32, kind="ExternalOutput").ap()
    hybrid_block(nc, *args, out)
    r = run_bass_kernel_spmd(nc, [arrays], core_ids=[0])
    return r.results[0]["out"]
```
